# Optimizing a Trainium2 kernel written in Bass

```python
import math
import jax, jax.numpy as jnp
from jax import lax
import numpy as np
import jax
import jax.numpy as jnp

D_MODEL = 1024
BATCH = 1
SEQ = 256
DEPTH = 1

HEAD_DIM = 64
FOX_HEADS = 8
NSA_HEADS = 8
NSA_KV_HEADS = 2
CMP_BLOCK = 32
CMP_STRIDE = 16
CMP_HIDDEN = 256
SLC_BLOCK = 64
SLC_TOPK = 16
WINDOW = 512
Q_BLOCK = 128
N_GROUPS = 4
EXPERTS_PER_GROUP = 4
N_EXPERTS = N_GROUPS * EXPERTS_PER_GROUP
TOP_K_IN_GROUP = 2
D_EXPERT = 512
RMS_EPS = 1e-6
NEG_INF = -1e30
FORCE_SCORE = 1e4

FOX_W = FOX_HEADS * HEAD_DIM
NSA_W = NSA_HEADS * HEAD_DIM
NSA_KV_W = NSA_KV_HEADS * HEAD_DIM
IN_COLS = (FOX_W, FOX_W, FOX_W, FOX_HEADS,
           NSA_W, NSA_KV_W, NSA_KV_W, NSA_KV_W, NSA_KV_W, NSA_KV_W, NSA_KV_W, 3 * NSA_HEADS,
           D_MODEL, D_MODEL)
D_IN = sum(IN_COLS)


def rms_norm(x, g):
    xf = x.astype(jnp.float32)
    y = xf * lax.rsqrt(jnp.mean(xf * xf, axis=-1, keepdims=True) + RMS_EPS)
    return (y * g.astype(jnp.float32)).astype(x.dtype)

def split_cols(z):
    outs, off = [], 0
    for c in IN_COLS:
        outs.append(z[..., off:off + c])
        off += c
    return outs

def to_heads(t, n):
    B, S, _ = t.shape
    return t.reshape(B, S, n, HEAD_DIM).transpose(0, 2, 1, 3)

def from_heads(t):
    B, n, S, dh = t.shape
    return t.transpose(0, 2, 1, 3).reshape(B, S, n * dh)

def alibi_slopes(n):
    return jnp.asarray([2.0 ** (-8.0 * (h + 1) / n) for h in range(n)], jnp.float32)

def fox_attention(q, k, v, log_f):
    B, H, S, dh = q.shape
    cum = jnp.cumsum(log_f, axis=-1)
    scale = dh ** -0.5
    kpos = jnp.arange(S)

    def block(i):
        q0 = i * Q_BLOCK
        qpos = q0 + jnp.arange(Q_BLOCK)
        qb = lax.dynamic_slice_in_dim(q, q0, Q_BLOCK, axis=2)
        cb = lax.dynamic_slice_in_dim(cum, q0, Q_BLOCK, axis=2)
        s = jnp.einsum('bhqd,bhkd->bhqk', qb, k, preferred_element_type=jnp.float32) * scale
        s = s + cb[..., :, None] - cum[..., None, :]
        s = jnp.where(kpos[None, :] <= qpos[:, None], s, NEG_INF)
        p = jax.nn.softmax(s, axis=-1)
        return jnp.einsum('bhqk,bhkd->bhqd', p.astype(v.dtype), v)

    o = lax.map(block, jnp.arange(S // Q_BLOCK))
    return jnp.moveaxis(o, 0, 2).reshape(B, H, S, dh)

def compress_blocks(t, w1, w2, pos):
    B, S, G, dh = t.shape
    n_cmp = (S - CMP_BLOCK) // CMP_STRIDE + 1
    idx = jnp.arange(n_cmp)[:, None] * CMP_STRIDE + jnp.arange(CMP_BLOCK)[None, :]
    blk = t[:, idx] + pos[None, None, :, None, :]
    blk = jnp.moveaxis(blk, 3, 1).reshape(B, G, n_cmp, CMP_BLOCK * dh)
    return jax.nn.gelu(blk @ w1) @ w2

def nsa_attention(q, k_cmp, v_cmp, k_slc, v_slc, k_win, v_win, gates):
    B, H, S, dh = q.shape
    G = k_slc.shape[1]
    R = H // G
    n_cmp = k_cmp.shape[2]
    n_slc = S // SLC_BLOCK
    top_n = min(SLC_TOPK, n_slc)
    scale = dh ** -0.5
    slopes = alibi_slopes(H).reshape(G, R)[None, :, :, None, None]

    cmp_start = jnp.arange(n_cmp) * CMP_STRIDE
    cmp_end = cmp_start + CMP_BLOCK - 1
    slc_start = jnp.arange(n_slc) * SLC_BLOCK
    ov = jnp.minimum(cmp_start[:, None] + CMP_BLOCK, slc_start[None, :] + SLC_BLOCK) - \
        jnp.maximum(cmp_start[:, None], slc_start[None, :])
    overlap = jnp.clip(ov, 0, None).astype(jnp.float32) / CMP_BLOCK
    slc_ids = jnp.arange(n_slc)

    k_sb = k_slc.reshape(B, G, n_slc, SLC_BLOCK, dh)
    v_sb = v_slc.reshape(B, G, n_slc, SLC_BLOCK, dh)
    pad = ((0, 0), (0, 0), (WINDOW, 0), (0, 0))
    k_wp = jnp.pad(k_win, pad)
    v_wp = jnp.pad(v_win, pad)
    gather = jax.vmap(jax.vmap(lambda blocks, idx: blocks[idx]))

    def block(i):
        q0 = i * Q_BLOCK
        qpos = q0 + jnp.arange(Q_BLOCK)
        qb = lax.dynamic_slice_in_dim(q, q0, Q_BLOCK, axis=2).reshape(B, G, R, Q_BLOCK, dh)

        s = jnp.einsum('bgrqd,bgnd->bgrqn', qb, k_cmp, preferred_element_type=jnp.float32) * scale
        dist = (qpos[:, None] - cmp_end[None, :]).astype(jnp.float32)
        valid = dist >= 0
        s = jnp.where(valid, s - slopes * dist, NEG_INF)
        p_cmp = jax.nn.softmax(s, axis=-1) * jnp.any(valid, axis=-1)[:, None].astype(jnp.float32)
        o_cmp = jnp.einsum('bgrqn,bgnd->bgrqd', p_cmp.astype(v_cmp.dtype), v_cmp)

        imp = jnp.einsum('bgrqn,nj->bgqj', p_cmp, overlap)
        qblk = qpos // SLC_BLOCK
        forced = (slc_ids[None, :] == 0) | (slc_ids[None, :] == qblk[:, None]) | \
            (slc_ids[None, :] == qblk[:, None] - 1)
        future = slc_ids[None, :] * SLC_BLOCK > qpos[:, None]
        score = jnp.where(future, -1.0, jnp.where(forced, FORCE_SCORE, imp))
        _, idx = lax.top_k(score, top_n)
        n_tok = top_n * SLC_BLOCK
        ks_g = gather(k_sb, idx).reshape(B, G, Q_BLOCK, n_tok, dh)
        vs_g = gather(v_sb, idx).reshape(B, G, Q_BLOCK, n_tok, dh)
        spos = (idx[..., None] * SLC_BLOCK + jnp.arange(SLC_BLOCK)).reshape(B, G, Q_BLOCK, n_tok)
        dist = (qpos[:, None] - spos).astype(jnp.float32)[:, :, None]
        s = jnp.einsum('bgrqd,bgqkd->bgrqk', qb, ks_g, preferred_element_type=jnp.float32) * scale
        s = jnp.where(dist >= 0, s - slopes * dist, NEG_INF)
        o_slc = jnp.einsum('bgrqk,bgqkd->bgrqd', jax.nn.softmax(s, axis=-1).astype(vs_g.dtype), vs_g)

        kw_b = lax.dynamic_slice_in_dim(k_wp, q0, WINDOW + Q_BLOCK, axis=2)
        vw_b = lax.dynamic_slice_in_dim(v_wp, q0, WINDOW + Q_BLOCK, axis=2)
        wpos = q0 - WINDOW + jnp.arange(WINDOW + Q_BLOCK)
        dist = (qpos[:, None] - wpos[None, :]).astype(jnp.float32)
        valid = (dist >= 0) & (dist < WINDOW) & (wpos[None, :] >= 0)
        s = jnp.einsum('bgrqd,bgkd->bgrqk', qb, kw_b, preferred_element_type=jnp.float32) * scale
        s = jnp.where(valid, s - slopes * dist, NEG_INF)
        o_win = jnp.einsum('bgrqk,bgkd->bgrqd', jax.nn.softmax(s, axis=-1).astype(vw_b.dtype), vw_b)

        gb = lax.dynamic_slice_in_dim(gates, q0, Q_BLOCK, axis=2).reshape(B, G, R, Q_BLOCK, 3)
        o = gb[..., 0:1] * o_cmp + gb[..., 1:2] * o_slc + gb[..., 2:3] * o_win
        return o.reshape(B, H, Q_BLOCK, dh)

    o = lax.map(block, jnp.arange(S // Q_BLOCK))
    return jnp.moveaxis(o, 0, 2).reshape(B, H, S, dh)

def hierarchical_moe(x, w_group, b_group, w_router, b_router, w_gate, w_up, w_down):
    B, S, D = x.shape
    t = x.reshape(B * S, D)
    g_logits = (t @ w_group).astype(jnp.float32) + b_group.astype(jnp.float32)
    p_g, g_top = lax.top_k(jax.nn.softmax(g_logits, axis=-1), 1)
    e_logits = ((t @ w_router).astype(jnp.float32) + b_router.astype(jnp.float32)).reshape(-1, N_GROUPS, EXPERTS_PER_GROUP)
    e_in = jnp.take_along_axis(e_logits, g_top[:, :, None], axis=1)[:, 0]
    top_p, top_i = lax.top_k(jax.nn.softmax(e_in, axis=-1), TOP_K_IN_GROUP)
    w = top_p / jnp.sum(top_p, axis=-1, keepdims=True) * p_g
    expert_id = g_top * EXPERTS_PER_GROUP + top_i
    combine = jnp.sum(jax.nn.one_hot(expert_id, N_EXPERTS, dtype=jnp.float32) * w[..., None], axis=1)
    hid = jax.nn.silu(jnp.einsum('td,edf->etf', t, w_gate)) * jnp.einsum('td,edf->etf', t, w_up)
    hid = hid * combine.T.astype(hid.dtype)[:, :, None]
    y = jnp.einsum('etf,efd->td', hid, w_down)
    return y.reshape(B, S, D)

def first_inputs(seed: int = 0) -> dict:
    key = jax.random.key(seed)
    ks = jax.random.split(key, 26)
    L = DEPTH

    def nrm(k, shape, scale):
        return jax.random.normal(k, shape, jnp.float32) * scale

    def gain(k, shape):
        return 1.0 + 0.02 * jax.random.normal(k, shape, jnp.float32)

    cmp_in = CMP_BLOCK * HEAD_DIM
    return {
        "x": nrm(ks[0], (BATCH, SEQ, D_MODEL), 1.0),
        "norm_mix_g": gain(ks[1], (L, D_MODEL)),
        "w_in": nrm(ks[2], (L, D_MODEL, D_IN), D_MODEL ** -0.5),
        "b_forget": jnp.linspace(1.0, 6.0, FOX_HEADS, dtype=jnp.float32)[None, :] + nrm(ks[3], (L, FOX_HEADS), 0.1),
        "fox_q_g": gain(ks[4], (L, HEAD_DIM)),
        "fox_k_g": gain(ks[5], (L, HEAD_DIM)),
        "nsa_q_g": gain(ks[6], (L, HEAD_DIM)),
        "nsa_k_g": gain(ks[7], (L, HEAD_DIM)),
        "cmp_k_w1": nrm(ks[8], (L, cmp_in, CMP_HIDDEN), cmp_in ** -0.5),
        "cmp_k_w2": nrm(ks[9], (L, CMP_HIDDEN, HEAD_DIM), CMP_HIDDEN ** -0.5),
        "cmp_k_pos": nrm(ks[10], (L, CMP_BLOCK, HEAD_DIM), 0.1),
        "cmp_v_w1": nrm(ks[11], (L, cmp_in, CMP_HIDDEN), cmp_in ** -0.5),
        "cmp_v_w2": nrm(ks[12], (L, CMP_HIDDEN, HEAD_DIM), CMP_HIDDEN ** -0.5),
        "cmp_v_pos": nrm(ks[13], (L, CMP_BLOCK, HEAD_DIM), 0.1),
        "w_fox_up": nrm(ks[14], (L, FOX_W, D_MODEL), FOX_W ** -0.5),
        "w_nsa_up": nrm(ks[15], (L, NSA_W, D_MODEL), NSA_W ** -0.5),
        "w_out": nrm(ks[16], (L, D_MODEL, D_MODEL), D_MODEL ** -0.5),
        "norm_ffn_g": gain(ks[17], (L, D_MODEL)),
        "w_group": nrm(ks[18], (L, D_MODEL, N_GROUPS), D_MODEL ** -0.5),
        "b_group": nrm(ks[19], (L, N_GROUPS), 0.01),
        "w_router": nrm(ks[20], (L, D_MODEL, N_EXPERTS), D_MODEL ** -0.5),
        "b_router": nrm(ks[21], (L, N_EXPERTS), 0.01),
        "w_gate": nrm(ks[22], (L, N_EXPERTS, D_MODEL, D_EXPERT), D_MODEL ** -0.5),
        "w_up": nrm(ks[23], (L, N_EXPERTS, D_MODEL, D_EXPERT), D_MODEL ** -0.5),
        "w_down": nrm(ks[24], (L, N_EXPERTS, D_EXPERT, D_MODEL), D_EXPERT ** -0.5),
    }

def first_block(x, norm_mix_g, w_in, b_forget, fox_q_g, fox_k_g, nsa_q_g, nsa_k_g,
              cmp_k_w1, cmp_k_w2, cmp_k_pos, cmp_v_w1, cmp_v_w2, cmp_v_pos,
              w_fox_up, w_nsa_up, w_out, norm_ffn_g, w_group, b_group, w_router, b_router,
              w_gate, w_up, w_down):
    B, S, D = x.shape
    for l in range(DEPTH):
        h = rms_norm(x, norm_mix_g[l])
        (f_q, f_k, f_v, f_f, n_q, k_c, v_c, k_s, v_s, k_w, v_w, n_g, g_a, g_b) = split_cols(h @ w_in[l])

        qa = rms_norm(to_heads(f_q, FOX_HEADS), fox_q_g[l])
        ka = rms_norm(to_heads(f_k, FOX_HEADS), fox_k_g[l])
        va = to_heads(f_v, FOX_HEADS)
        log_f = jax.nn.log_sigmoid(f_f.astype(jnp.float32) + b_forget[l].astype(jnp.float32)).transpose(0, 2, 1)
        out_a = from_heads(fox_attention(qa, ka, va, log_f)) @ w_fox_up[l]

        qb = rms_norm(to_heads(n_q, NSA_HEADS), nsa_q_g[l])
        kc = compress_blocks(k_c.reshape(B, S, NSA_KV_HEADS, HEAD_DIM), cmp_k_w1[l], cmp_k_w2[l], cmp_k_pos[l])
        kc = rms_norm(kc, nsa_k_g[l])
        vc = compress_blocks(v_c.reshape(B, S, NSA_KV_HEADS, HEAD_DIM), cmp_v_w1[l], cmp_v_w2[l], cmp_v_pos[l])
        ks_ = rms_norm(to_heads(k_s, NSA_KV_HEADS), nsa_k_g[l])
        vs_ = to_heads(v_s, NSA_KV_HEADS)
        kw_ = rms_norm(to_heads(k_w, NSA_KV_HEADS), nsa_k_g[l])
        vw_ = to_heads(v_w, NSA_KV_HEADS)
        gates = jax.nn.sigmoid(n_g.reshape(B, S, NSA_HEADS, 3)).transpose(0, 2, 1, 3)
        out_b = from_heads(nsa_attention(qb, kc, vc, ks_, vs_, kw_, vw_, gates)) @ w_nsa_up[l]

        mix = jax.nn.sigmoid(g_a) * out_a + jax.nn.sigmoid(g_b) * out_b
        x = x + mix @ w_out[l]

        x = x + hierarchical_moe(rms_norm(x, norm_ffn_g[l]), w_group[l], b_group[l], w_router[l], b_router[l],
                                 w_gate[l], w_up[l], w_down[l])
    return x


DEPTH_2 = 2

EXPAND = 2
MIX_WIDTH = EXPAND * D_MODEL
HG_WIDTH = MIX_WIDTH // 2
HG_HEAD_DIM = 128
HG_HEADS = HG_WIDTH // HG_HEAD_DIM
HG_CHUNK = 64
ATT_WIDTH = MIX_WIDTH - HG_WIDTH
ATT_HEAD_DIM = 64
ATT_HEADS = ATT_WIDTH // ATT_HEAD_DIM
ATT_KV_HEADS = max(1, ATT_HEADS // 8)
ATT_GROUP = ATT_HEADS // ATT_KV_HEADS
KV_WIDTH = ATT_KV_HEADS * ATT_HEAD_DIM
WINDOW_2 = 128
ATT_BLOCK = 128
ATT_SCALE = 1.0 / math.sqrt(ATT_HEAD_DIM)
ROPE_THETA = 10000.0
NORM_EPS = 1e-6
NEG_INF_2 = -1e30
LB_FLOOR = 1e-20

SPLIT_SIZES = (HG_WIDTH, HG_WIDTH, HG_WIDTH, HG_WIDTH, ATT_WIDTH, KV_WIDTH, KV_WIDTH, ATT_WIDTH)
IN_WIDTH = int(sum(SPLIT_SIZES))
SPLIT_POINTS = tuple(int(v) for v in np.cumsum(SPLIT_SIZES)[:-1])


def rms_norm_2(x, g):
    xf = x.astype(jnp.float32)
    y = xf * lax.rsqrt(jnp.mean(xf * xf, axis=-1, keepdims=True) + NORM_EPS)
    return (y * g.astype(jnp.float32)).astype(x.dtype)

def rotary(x, pos):
    half = x.shape[-1] // 2
    inv_freq = ROPE_THETA ** (-jnp.arange(half, dtype=jnp.float32) / half)
    ang = pos.astype(jnp.float32)[:, None] * inv_freq[None, :]
    cos = jnp.cos(ang)[None, :, None, :]
    sin = jnp.sin(ang)[None, :, None, :]
    xf = x.astype(jnp.float32)
    x1, x2 = xf[..., :half], xf[..., half:]
    return jnp.concatenate([x1 * cos - x2 * sin, x2 * cos + x1 * sin], axis=-1).astype(x.dtype)

def hgrn2(q, f_logit, i, lb):
    B, S, _ = q.shape
    C, H, D = HG_CHUNK, HG_HEADS, HG_HEAD_DIM
    nC = S // C
    lb = lb.astype(jnp.float32)
    qf = jax.nn.silu(q.astype(jnp.float32))
    logf = jnp.logaddexp(jnp.log(jnp.maximum(lb, LB_FLOOR)),
                         jnp.log1p(-lb) + jax.nn.log_sigmoid(f_logit.astype(jnp.float32)))
    k = -jnp.expm1(logf)

    def chunks(t):
        return t.reshape(B, nC, C, H, D).transpose(1, 0, 3, 2, 4)

    qc, kc, vc, gc = chunks(qf), chunks(k), chunks(i.astype(jnp.float32)), chunks(logf)
    bc = jnp.cumsum(gc, axis=3)
    causal = jnp.tril(jnp.ones((C, C), dtype=bool))[None, None, :, :, None]

    def step(state, xs):
        qch, kch, vch, b = xs
        b_last = b[:, :, C - 1:C, :]
        diff = b[:, :, :, None, :] - b[:, :, None, :, :]
        decay = jnp.where(causal, jnp.exp(jnp.where(causal, diff, 0.0)), 0.0)
        scores = jnp.einsum('bhtd,bhsd,bhtsd->bhts', qch, kch, decay)
        o = jnp.einsum('bhts,bhsv->bhtv', scores, vch)
        o = o + jnp.einsum('bhtd,bhdv->bhtv', qch * jnp.exp(b), state)
        state = jnp.exp(b_last[:, :, 0, :])[..., None] * state + \
            jnp.einsum('bhsd,bhsv->bhdv', kch * jnp.exp(b_last - b), vch)
        return state, o

    s0 = jnp.zeros((B, H, D, D), dtype=jnp.float32)
    _, o = lax.scan(step, s0, (qc, kc, vc, bc))
    return o.transpose(1, 0, 3, 2, 4).reshape(B, S, H, D)

def sliding_window_attention(q, k, v, sinks):
    B, S = q.shape[0], q.shape[1]
    L, KV, G, D = ATT_BLOCK, ATT_KV_HEADS, ATT_GROUP, ATT_HEAD_DIM
    nB = S // L
    qb = q.reshape(B, nB, L, KV, G, D)
    kb = k.reshape(B, nB, L, KV, D)
    vb = v.reshape(B, nB, L, KV, D)
    k_prev = jnp.concatenate([jnp.zeros_like(kb[:, :1]), kb[:, :-1]], axis=1)
    v_prev = jnp.concatenate([jnp.zeros_like(vb[:, :1]), vb[:, :-1]], axis=1)
    kw = jnp.concatenate([k_prev, kb], axis=2)
    vw = jnp.concatenate([v_prev, vb], axis=2)
    s = jnp.einsum('bnqkgd,bnskd->bnkgqs', qb, kw).astype(jnp.float32) * ATT_SCALE
    qpos = jnp.arange(L)[:, None] + L
    kpos = jnp.arange(2 * L)[None, :]
    diff = qpos - kpos
    band = (diff >= 0) & (diff < WINDOW_2)
    key_exists = (jnp.arange(nB)[:, None] * L - L + jnp.arange(2 * L)[None, :]) >= 0
    mask = band[None, :, :] & key_exists[:, None, :]
    s = jnp.where(mask[None, :, None, None, :, :], s, NEG_INF_2)
    sink = jnp.broadcast_to(sinks.astype(jnp.float32).reshape(KV, G)[None, None, :, :, None, None],
                            s.shape[:-1] + (1,))
    p = jax.nn.softmax(jnp.concatenate([s, sink], axis=-1), axis=-1)[..., :-1]
    o = jnp.einsum('bnkgqs,bnskd->bnqkgd', p.astype(v.dtype), vw)
    return o.reshape(B, S, KV * G * D)

def hybrid_layer(x, w_in, w_out, g_pre, g_post, lb, g_head, sinks):
    B, S, _ = x.shape
    h = rms_norm_2(x, g_pre)
    proj = jnp.einsum('bsd,de->bse', h, w_in)
    q_h, f_h, i_h, z_h, q_a, k_a, v_a, z_a = jnp.split(proj, SPLIT_POINTS, axis=-1)

    o_h = hgrn2(q_h, f_h, i_h, lb)
    o_h = rms_norm_2(o_h, g_head).reshape(B, S, HG_WIDTH).astype(z_h.dtype) * jax.nn.silu(z_h)

    pos = jnp.arange(S)
    q_a = rotary(q_a.reshape(B, S, ATT_HEADS, ATT_HEAD_DIM), pos)
    k_a = rotary(k_a.reshape(B, S, ATT_KV_HEADS, ATT_HEAD_DIM), pos)
    v_a = v_a.reshape(B, S, ATT_KV_HEADS, ATT_HEAD_DIM)
    o_a = sliding_window_attention(q_a, k_a, v_a, sinks).astype(z_a.dtype) * jax.nn.silu(z_a)

    y = jnp.einsum('bse,ed->bsd', jnp.concatenate([o_h, o_a], axis=-1), w_out)
    return x + rms_norm_2(y, g_post)

def second_inputs(seed: int = 0) -> dict:
    key = jax.random.key(seed)
    ks = jax.random.split(key, 9)
    x = jax.random.normal(ks[0], (BATCH, SEQ, D_MODEL), dtype=jnp.float32)
    w_in = jax.random.normal(ks[1], (DEPTH_2, D_MODEL, IN_WIDTH), dtype=jnp.float32) * D_MODEL ** -0.5
    w_out = jax.random.normal(ks[2], (DEPTH_2, MIX_WIDTH, D_MODEL), dtype=jnp.float32) * MIX_WIDTH ** -0.5
    g_pre = 1.0 + 0.05 * jax.random.normal(ks[3], (DEPTH_2, D_MODEL), dtype=jnp.float32)
    g_post = 1.0 + 0.05 * jax.random.normal(ks[4], (DEPTH_2, D_MODEL), dtype=jnp.float32)
    lb_param = 0.1 * jax.random.normal(ks[5], (DEPTH_2, HG_WIDTH), dtype=jnp.float32)
    g_head = 1.0 + 0.05 * jax.random.normal(ks[6], (DEPTH_2, HG_HEAD_DIM), dtype=jnp.float32)
    sinks = jax.random.normal(ks[7], (DEPTH_2, ATT_HEADS), dtype=jnp.float32)
    return {"x": x, "w_in": w_in, "w_out": w_out, "g_pre": g_pre, "g_post": g_post,
            "lb_param": lb_param, "g_head": g_head, "sinks": sinks}

def second_block(x, w_in, w_out, g_pre, g_post, lb_param, g_head, sinks):
    p = jax.nn.softmax(lb_param.astype(jnp.float32), axis=0)
    lower_bounds = jnp.cumsum(p, axis=0) - p[0:1]
    for l in range(DEPTH_2):
        x = hybrid_layer(x, w_in[l], w_out[l], g_pre[l], g_post[l], lower_bounds[l], g_head[l], sinks[l])
    return x


def setup_inputs(seed=0):
    out = dict(first_inputs(seed))
    for name, value in second_inputs(seed + 1).items():
        if name != "x":
            out[name + "_2"] = value
    return out


def reference(
    x, norm_mix_g, w_in, b_forget, fox_q_g, fox_k_g, nsa_q_g, nsa_k_g, cmp_k_w1, cmp_k_w2,
    cmp_k_pos, cmp_v_w1, cmp_v_w2, cmp_v_pos, w_fox_up, w_nsa_up, w_out, norm_ffn_g, w_group,
    b_group, w_router, b_router, w_gate, w_up, w_down, w_in_2, w_out_2, g_pre_2, g_post_2,
    lb_param_2, g_head_2, sinks_2,
):
    x = first_block(
        x, norm_mix_g, w_in, b_forget, fox_q_g, fox_k_g, nsa_q_g, nsa_k_g, cmp_k_w1, cmp_k_w2,
        cmp_k_pos, cmp_v_w1, cmp_v_w2, cmp_v_pos, w_fox_up, w_nsa_up, w_out, norm_ffn_g,
        w_group, b_group, w_router, b_router, w_gate, w_up, w_down,
    )
    return second_block(
        x, w_in_2, w_out_2, g_pre_2, g_post_2, lb_param_2, g_head_2, sinks_2,
    )


_drawn_inputs = setup_inputs


def setup_inputs(seed=0):
    import zlib

    import numpy as np

    out = dict(_drawn_inputs(seed))
    spreads = {}
    factors = {'norm_mix_g': 3.344,
     'fox_q_g': 8.0,
     'fox_k_g': 8.0,
     'nsa_q_g': 8.0,
     'nsa_k_g': 8.0,
     'cmp_k_pos': 3.819,
     'b_group': 22.898,
     'b_router': 30.946,
     'lb_param_2': 50.584,
     'sinks_2': 21.055,
     'cmp_v_pos': 5.132,
     'norm_ffn_g': 3.996,
     'g_pre_2': 4.814,
     'g_post_2': 7.105,
     'g_head_2': 7.11}
    for name, (base, spread) in spreads.items():
        noise = np.random.default_rng([zlib.crc32(name.encode()), seed]).standard_normal(out[name].shape)
        drawn = base * np.exp(spread * noise) if base else spread * noise
        out[name] = jnp.asarray(drawn.astype(out[name].dtype))
    for name, factor in factors.items():
        out[name] = (out[name] * factor).astype(out[name].dtype)
    return out
```

```python
from contextlib import ExitStack

import numpy as np
import concourse.bass as bass
from concourse import mybir
from concourse.alu_op_type import AluOpType as ALU

ACT = mybir.ActivationFunctionType
F32 = mybir.dt.float32
U32 = mybir.dt.uint32
AX = mybir.AxisListType.X

P = 128
S = 256
TT = S // P
D = 1024
KT = D // P
HD = 64
PAIRS = 4
EPS = 1e-6
NEG = -1e30
N_CMP, CMP_PAD = 15, 32
N_EXP = 16
GRP, EPG = 4, 4
LAYERS = 2
HG = 8
SWA_PAIRS = 8
LB_FLOOR = 1e-20
LEVELS = 8
RING = 3
PANEL = 4096

PN_Z, PN_Z5, PN_GATE, PN_CMP, PN_FOX_UP, PN_NSA_UP, PN_OUT, PN_MOE = 0, 5, 6, 10, 12, 13, 14, 16
PN_L2 = PN_MOE + 3 * N_EXP
L2_PANELS = 17
N_PANELS = PN_L2 + LAYERS * L2_PANELS
Z5 = 288

PRM = {}
_n = 0
for _name, _w in (("g_mix", 8), ("g_ffn", 8), ("fq_g", 1), ("fk_g", 1), ("nq_g", 1), ("nk_g", 1),
                  ("pos_k", 16), ("pos_v", 16), ("b_forget", 8), ("b_route", 20), ("w_route", 160),
                  ("w2_k", 128), ("w2_v", 128), ("lb", 16)):
    PRM[_name] = (_n, _n + _w)
    _n += _w
PRM_W = _n
PL = {"g_pre": (0, 8), "g_head": (8, 136), "sinks": (136, 152)}
PL_IN = 152
PL_W = PL_IN + 3 * 8
ZB = 4352
C1 = {"ntri": (0, 256), "causal": (256, 1024), "alibi": (1024, 4096), "cmp": (4096, 4608), "any": (4608, 4610),
      "first": (4610, 4614), "slot": (4614, 4742)}
C1_W = 4742
C2 = {"band": (0, 768), "cos": (768, 832), "sin": (832, 896), "level": (896, 896 + LEVELS * P)}
C2_W = 896 + LEVELS * P


class Token:

    def __init__(self, sem, scope, off, back=0):
        self.sem, self.scope, self.off, self.back = sem, scope, off, back

    def prev(self):
        return Token(self.sem, self.scope, self.off, 1)


class Later:

    def __init__(self):
        self.token = None


class Scope:
    def __init__(self, parent, n):
        self.parent, self.n, self.flag = parent, n, None
        self.count, self.start, self.items = {}, {}, {}
        self.depth = 0 if parent is None else parent.depth + 1


class Program:

    def __init__(self, nc, ctx):
        self.nc, self.ctx = nc, ctx
        self.engines = {"pe": nc.tensor, "dve": nc.vector, "act": nc.scalar, "pool": nc.gpsimd, "sp": nc.sync}
        self.sems = {e: ctx.enter_context(nc.semaphore("done_" + e)) for e in ("pe", "dve", "act", "pool")}
        self.scope = self.root = Scope(None, 1)

    def count(self, sem, by):
        c = self.scope.count
        c[sem] = c.get(sem, 0) + by
        return Token(sem, self.scope, c[sem])

    def op(self, eng, fn, waits=()):
        token = self.count(eng, 1)
        self.scope.items.setdefault(eng, []).append((fn, list(waits), eng, 1))
        return token

    def dma(self, eng, fn, sem, waits=()):
        if sem not in self.sems:
            self.sems[sem] = self.ctx.enter_context(self.nc.semaphore("dma_" + sem))
        token = self.count(sem, 16)
        self.scope.items.setdefault(eng, []).append((fn, list(waits), sem, 16))
        return token

    def fence(self, eng, waits):
        self.scope.items.setdefault(eng, []).append((None, list(waits), None, 0))

    def begin_loop(self, n):
        s = Scope(self.scope, n)
        s.start = None
        for e in ("pe", "dve", "act", "pool", "sp"):
            self.scope.items.setdefault(e, []).append(s)
        s.start = dict(self.scope.count)
        self.scope = s
        return s

    def end_loop(self):
        s = self.scope
        self.scope = s.parent
        for sem, c in s.count.items():
            self.scope.count[sem] = self.scope.count.get(sem, 0) + s.n * c

    def begin_if(self, flag, waits):
        s = self.begin_loop(1)
        s.flag, s.flag_waits = flag, list(waits)
        return s

    end_if = end_loop

    def value(self, t, here, regs):
        around = []
        s = here
        while s is not None:
            around.append(s)
            s = s.parent
        val = t.off
        if t.back:
            val = val - t.scope.count[t.sem]
        s = t.scope
        terms = []
        while s.parent is not None:
            val += s.start.get(t.sem, 0)
            per = s.count.get(t.sem, 0)
            if s in around:
                terms.append((s.depth - 1, per))
            else:
                val += (s.n - 1) * per
            s = s.parent
        key = (t.sem, tuple(terms))
        low = val
        expr = val
        for d, per in terms:
            if per:
                expr = regs[d] * per + expr
        assert low > 0, ("a wait on a value that may not be positive", t.sem, low)
        return key, val, expr

    def emit(self, eng, scope=None, regs=(), known=None):
        scope = scope or self.root
        e = self.engines[eng]
        known = {} if known is None else known
        for item in scope.items.get(eng, []):
            if isinstance(item, Scope):
                if item.flag is not None and self.uses(item, eng):
                    self.emit_if(eng, item, known)
                elif self.uses(item, eng):
                    with e.Fori(0, item.n) as i:
                        self.emit(eng, item, regs + (i,), {})
                continue
            fn, waits, sem, by = item
            need = {}
            for t in waits:
                if isinstance(t, Later):
                    t = t.token
                if t is None:
                    continue
                key, val, expr = self.value(t, scope, regs)
                if known.get(key, 0) < val and (key not in need or need[key][0] < val):
                    need[key] = (val, expr)
            for key, (val, expr) in need.items():
                e.wait_ge(self.sems[key[0]], expr)
                known[key] = val
            if fn is not None:
                fn(*regs).then_inc(self.sems[sem], by)

    def emit_if(self, eng, item, known):
        e = self.engines[eng]
        for t in item.flag_waits:
            e.wait_ge(self.sems[t.sem], self.value(t, self.root, ())[1])
        own = [sem for sem, by in item.count.items() if by and (sem == eng or (eng == "sp" and sem.startswith("slot")))]
        for sem in own:
            if item.start.get(sem, 0):
                e.wait_ge(self.sems[sem], item.start[sem])
        flag = e.value_load(item.flag, min_val=0, max_val=S)
        with e.If(flag > 0):
            self.emit(eng, item, (0,), dict(known))
        with e.Else():
            for sem in own:
                e.sem_inc(self.sems[sem], item.count[sem])

    def uses(self, scope, eng):
        return any(self.uses(x, eng) if isinstance(x, Scope) else True for x in scope.items.get(eng, []))


def build(nc, panels, x_in, prm_in, lay_in, post_in, c0_in, c1_in, c2_in, out):
    ctx = ExitStack()
    with ctx:
        def sb(name, cols, dt=F32, parts=P):
            return ctx.enter_context(nc.sbuf_tensor(name, [parts, cols], dt))

        p = Program(nc, ctx)
        V, A, T, G = nc.vector, nc.scalar, nc.tensor, nc.gpsimd

        ring = sb("ring", RING * PANEL)
        x_tok = sb("x_tok", TT * D)
        hT = sb("hT", KT * S)
        ident = sb("ident", P)
        prm = sb("prm", PRM_W)
        cst = sb("cst", max(C1_W, C2_W))
        zin = sb("zin", TT * ZB)
        gates = sb("gates", 16 * S)
        buf_a = sb("buf_a", 1024)
        buf_b = sb("buf_b", 1024)
        keys = sb("keys", 3072)
        buf_c = sb("buf_c", 2048)
        buf_d = sb("buf_d", 2048)
        s_buf = sb("s_buf", 2 * 768)
        pt_buf = sb("pt_buf", 2 * 768)
        scr = sb("scr", 2048)
        stat = sb("stat", 1024)
        ps = ctx.enter_context(nc.psum_tensor("ps", [P, 8, 512], F32))

        def bank(b, n=1):
            return ps[:, b, :] if n == 1 else ps[:, b:b + n, :].rearrange("p a b -> p (a b)")

        free = {b: [] for b in range(8)}

        def bank_waits(*bs):
            return [t for b in bs for t in free[b]]

        def tt(out_, a, b, op, waits=(), eng="dve"):
            f = V if eng == "dve" else G
            return p.op(eng, lambda *i: f.tensor_tensor(out_, a, b, op), waits)

        def ts(out_, a, s1, s2, op0, op1, waits=(), eng="dve"):
            f = V if eng == "dve" else G
            if s2 is None:
                return p.op(eng, lambda *i: f.tensor_scalar(out_, a, s1, None, op0), waits)
            return p.op(eng, lambda *i: f.tensor_scalar(out_, a, s1, s2, op0, op1), waits)

        def stt(out_, a, s1, b, op0, op1, waits=()):
            return p.op("dve", lambda *i: V.scalar_tensor_tensor(out_, a, s1, b, op0, op1), waits)

        def red(out_, a, op, waits=()):
            return p.op("dve", lambda *i: V.tensor_reduce(out_, a, AX, op), waits)

        def copy(out_, a, waits=(), eng="dve"):
            if eng == "act":
                return p.op("act", lambda *i: A.activation(out_, a, ACT.Copy), waits)
            f = V if eng == "dve" else G
            return p.op(eng, lambda *i: f.tensor_copy(out_, a), waits)

        def act(out_, a, func, waits=(), **kw):
            return p.op("act", lambda *i: A.activation(out_, a, func, **kw), waits)

        def memz(ap, waits=(), eng="pool"):
            f = V if eng == "dve" else G
            return p.op(eng, lambda *i: f.memset(ap, 0.0), waits)

        def mms(triples, waits=()):
            def run(*i):
                for o, l, r, s0, s1 in triples:
                    last = T.matmul(o, l, r, start=s0, stop=s1)
                return last
            return p.op("pe", run, waits)

        def transposes(pairs, waits=()):
            def run(*i):
                for o, a, n in pairs:
                    last = T.transpose(o, a, ident[0:n, 0:n])
                return last
            return p.op("pe", run, waits)

        def bc(ap, n):
            return ap.unsqueeze(len(ap.shape)).to_broadcast(list(ap.shape) + [n])

        def prmc(name, a=0, b=None):
            lo, hi = PRM[name]
            return prm[:, lo + a:(hi if b is None else lo + b)]

        slot_ap = [ring[:, s * PANEL:(s + 1) * PANEL] for s in range(RING)]
        slot_free = [[] for _ in range(RING)]
        pos = [0]

        def load_panel(index):
            s = pos[0] % RING
            pos[0] += 1
            dst = slot_ap[s]
            t = p.dma("sp", lambda *i: nc.sync.dma_start(
                dst, panels[index(*i)] if callable(index) else panels[index]), f"slot{s}", slot_free[s])
            return dst, t, s

        def k512(ap):
            return ap.rearrange("p (k n) -> p k n", k=8)

        def k1024(ap):
            return ap.rearrange("p (k n) -> p k n", k=4)

        def fm(ap, k):
            return ap.rearrange("p (k t) -> p k t", k=k)

        def tm(ap):
            return ap.rearrange("p (a n) -> p a n", a=TT)

        hT3 = fm(hT[:, :], KT)
        x3 = tm(x_tok[:, :])

        def proj_token(panel, n, waits, evac):
            w, ready, s = panel
            toks = []
            for a in range(TT):
                t = mms([(ps[:, a, 0:n], hT3[:, k, a * P:(a + 1) * P], k512(w)[:, k, 0:n], k == 0, k == KT - 1)
                         for k in range(KT)], [ready, *waits, *bank_waits(a)])
                free[a] = evac(a, ps[:, a, 0:n], t)
                toks.append(t)
            slot_free[s] = [toks[-1]]
            return toks

        def proj_feature(panel, waits, evac):
            w, ready, s = panel
            for b in range(2):
                t = mms([(ps[:, b, f * S:(f + 1) * S], k512(w)[:, k, (2 * b + f) * P:(2 * b + f + 1) * P],
                          hT3[:, k, :], k == 0, k == KT - 1) for f in range(2) for k in range(KT)],
                        [ready, *waits, *bank_waits(b)])
                free[b] = evac(b, ps[:, b, :], t)
            slot_free[s] = [t]
            return t

        def rstd(out_, ss, n, waits):
            t = ts(out_, ss, 1.0 / n, EPS, ALU.mult, ALU.add, waits)
            e = minus_half[0:out_.shape[0], :]
            for _ in out_.shape[2:]:
                e = e.unsqueeze(2)
            e = e.to_broadcast(list(out_.shape))
            return p.op("pool", lambda *i: G.tensor_tensor(out_, out_, e, ALU.pow), [t, t_mh])

        def norm_transpose(src_tokens, gain, dst_waits):
            ss, rs = stat[:, 0:2], stat[:, 2:4]
            t1 = [act(scr[:, a * D:(a + 1) * D], x3[:, a, :], ACT.Square, [*src_tokens, *dst_waits],
                      accum_out=ss[:, a:a + 1]) for a in range(TT)]
            t2 = rstd(rs, ss, D, t1)
            t3 = [ts(scr[:, a * D:(a + 1) * D], x3[:, a, :], rs[:, a:a + 1], None, ALU.mult, None, [t2, t1[a]])
                  for a in range(TT)]
            outs = []
            for b in range(4):
                q = 4 + b
                t = transposes([(ps[:, q, f * S + a * P:f * S + (a + 1) * P],
                                 scr[:, a * D + (2 * b + f) * P:a * D + (2 * b + f + 1) * P], P)
                                for f in range(2) for a in range(TT)], [*t3, *bank_waits(q)])
                t = tt(hT3[:, 2 * b:2 * b + 2, :], ps[:, q, :].rearrange("p (f t) -> p f t", f=2),
                       bc(gain[:, 2 * b:2 * b + 2], S), ALU.mult, [t, *dst_waits])
                free[q] = [t]
                outs.append(t)
            return outs

        t_x = p.dma("act", lambda *i: A.dma_start(x3, x_in.rearrange("o (a p) d -> p (o a) d", p=P)), "x")
        t_id = p.dma("act", lambda *i: A.dma_start(ident[:, :], c0_in), "ident")
        t_prm = p.dma("act", lambda *i: A.dma_start(prm[:, :], prm_in), "prm")
        t_c1 = p.dma("act", lambda *i: A.dma_start(cst[:, 0:C1_W], c1_in), "cst")

        lay = sb("lay", LAYERS * PL_W)
        t_lay = [p.dma("act", lambda *i, l=l: A.dma_start(lay[:, l * PL_W:l * PL_W + PL_IN], lay_in[l]), "lay")
                 for l in range(LAYERS)]

        minus_half = sb("minus_half", 1)
        t_mh = p.op("pool", lambda *i: G.memset(minus_half[:, :], -0.5))

        def c1(name):
            return cst[:, C1[name][0]:C1[name][1]]

        def c2(name):
            return cst[:, C2[name][0]:C2[name][1]]

        fox_k = keys[:, 0:2048]
        slc_k = keys[:, 2048:2560]
        win_k = keys[:, 2560:3072]
        t_zk = memz(keys[:, :])

        p.fence("pe", [t_id])
        p.fence("dve", [t_prm])
        t_h = norm_transpose([t_x], prmc("g_mix"), [])

        z3 = zin[:, 0:TT * 2848].rearrange("p (a n) -> p a n", a=TT)
        ZFQ, ZFK, ZFV, ZNQ, ZKC, ZVC, ZKS, ZVS, ZKW, ZVW, ZFF, ZNG = (
            0, 512, 1024, 1536, 2048, 2176, 2304, 2432, 2560, 2688, 2816, 2824)
        done_z = {}
        for n in range(6):
            cols = 512 if n < 5 else Z5

            def to_z(a, src, t, n=n, cols=cols):
                e = copy(z3[:, a, n * 512:n * 512 + cols], src, [t], "act" if a == 0 else "dve")
                done_z.setdefault(n, []).append(e)
                return [e]
            proj_token(load_panel(n), cols, t_h, to_z)

        def head_norm(view, heads, waits):
            n = TT * heads
            sq = scr[:, 0:n * HD].rearrange("p (a h d) -> p a h d", a=TT, h=heads)
            ss = stat[:, 32:32 + n].rearrange("p (a h) -> p a h", a=TT)
            t = tt(sq, view, view, ALU.mult, waits)
            t = red(ss, sq, ALU.add, [t])
            t = rstd(ss, ss, HD, [t])
            return tt(view, view, bc(ss, HD), ALU.mult, [t])

        def heads(col, n):
            return z3[:, :, col:col + n * HD].rearrange("p a (h d) -> p a h d", h=n)

        def transpose_pair(dst, src, b, waits):
            pass

        def q_side(col, buf, gain, b, waits):
            t = head_norm(heads(col, 8), 8, waits)
            outs = []
            for i in range(2):
                t1 = transposes([(ps[:, b + i, f * S + a * P:f * S + (a + 1) * P],
                                  z3[:, a, col + (2 * i + f) * P:col + (2 * i + f + 1) * P], P)
                                 for f in range(2) for a in range(TT)], [t, *bank_waits(b + i)])
                t2 = ts(buf[:, i * 512:(i + 1) * 512], ps[:, b + i, :], gain, HD ** -0.5, ALU.mult, ALU.mult, [t1])
                free[b + i] = [t2]
                outs.append(t2)
            return outs

        def k_side(dst, col, npair, gain, b, t):
            outs = []
            per = min(npair, 2)
            for i in range((npair + 1) // 2):
                t1 = transposes([(ps[:, b + i, f * S + a * P:f * S + (a + 1) * P],
                                  z3[:, a, col + (2 * i + f) * P:col + (2 * i + f + 1) * P], P)
                                 for f in range(per) for a in range(TT)], [t, *bank_waits(b + i)])
                for e in range(2):
                    rows = slice(e * HD, (e + 1) * HD)
                    d4 = dst[rows, 2 * i * 512:(2 * i + per) * 512].rearrange("p (f e t) -> p f e t", f=per, e=2)
                    t2 = ts(d4[:, :, e, :], ps[rows, b + i, 0:per * S].rearrange("p (f t) -> p f t", f=per),
                            gain[rows, :], None, ALU.mult, None, [t1, t_zk])
                    outs.append(t2)
                free[b + i] = [t2]
            return outs

        t_fq = q_side(ZFQ, buf_a, prmc("fq_g"), 2, done_z[0])
        t_fk = k_side(fox_k, ZFK, 4, prmc("fk_g"), 4, head_norm(heads(ZFK, 8), 8, done_z[1]))
        t_nq = q_side(ZNQ, buf_b, prmc("nq_g"), 2, done_z[3])
        t_ks = k_side(slc_k, ZKS, 1, prmc("nk_g"), 4, head_norm(heads(ZKS, 2), 2, done_z[4]))
        t_kw = k_side(win_k, ZKW, 1, prmc("nk_g"), 5, head_norm(heads(ZKW, 2), 2, done_z[5]))

        lf = stat[:, 64:80].rearrange("p (a h) -> p a h", a=TT)
        lx = stat[:, 80:96].rearrange("p (a h) -> p a h", a=TT)
        la = stat[:, 96:112].rearrange("p (a h) -> p a h", a=TT)
        t = tt(lx, z3[:, :, ZFF:ZFF + 8], prmc("b_forget").unsqueeze(1).to_broadcast([P, TT, 8]), ALU.add, done_z[5])
        t = ts(la, lx, -1.0, None, ALU.mult, None, [t])
        t = tt(la, la, lx, ALU.min, [t])
        t = act(la, la, ACT.Exp, [t])
        t = act(la, la, ACT.Ln, [t], bias=1.0)
        t1 = ts(lx, lx, 0.0, None, ALU.min, None, [t])
        t_lf = tt(lf, lx, la, ALU.subtract, [t1, t])
        lfb = buf_d[:, :]
        t_lfb = copy(lfb.rearrange("p (a h q) -> p a h q", a=TT, h=8), bc(lf, P), [t_lf], "pool")
        ntri = c1("ntri")
        lf2 = stat[:, 64:80]
        cq = stat[:, 112:128].rearrange("p (a h) -> p a h", a=TT)
        p.fence("pe", [t_c1])
        p.fence("dve", [t_c1])
        t = mms([(ps[:, 6, 0:8], ntri[:, 0:P], lf2[:, 0:8], True, True),
                 (ps[:, 6, 8:16], ntri[:, P:2 * P], lf2[:, 0:8], True, False),
                 (ps[:, 6, 8:16], ntri[:, 0:P], lf2[:, 8:16], False, True)], [t_lf, *bank_waits(6)])
        t_cq = ts(stat[:, 112:128], ps[:, 6, 0:16], -1.0, None, ALU.mult, None, [t])
        free[6] = [t_cq]
        ng = stat[:, 128:176].rearrange("p (a c h) -> p a c h", a=TT, c=3)
        t_ng = act(ng, z3[:, :, ZNG:ZNG + 24].rearrange("p a (c h) -> p a c h", c=3), ACT.Sigmoid, done_z[5])

        g3 = fm(gates[:, :], 16)
        t_gate = {}
        for n in range(4):
            def to_gate(b, src, t, n=n):
                e = act(gates[:, (4 * n + 2 * b) * S:(4 * n + 2 * b + 2) * S], src, ACT.Sigmoid, [t])
                t_gate.setdefault(n // 2, []).append(e)
                return [e]
            proj_feature(load_panel(PN_GATE + n), [], to_gate)

        o_tok = {}
        job_no = [0]

        def scores(q, k, waits, bias, forget=None, sink=None):
            j = job_no[0] % 2
            job_no[0] += 1
            job = {"j": j}
            k2 = k.rearrange("p (e t) -> p e t", e=2)
            last1 = forget is None
            m = [(ps[:, 2, :], q(1), k, True, last1)]
            if forget:
                for e in range(2):
                    l0, l1 = (lfb[:, (a * 8 + forget[0] + e) * P:(a * 8 + forget[0] + e + 1) * P] for a in range(2))
                    m += [(ps[:, 2, e * S:(e + 1) * S], l0, ntri, False, False),
                          (ps[:, 2, e * S + P:(e + 1) * S], l1, ntri[:, 0:P], False, e == 1)]
            m += [(ps[:, 3, 0:S].rearrange("p (e t) -> p e t", e=2), q(0), k2[:, :, 0:P], True, last1)]
            if forget:
                for e in range(2):
                    l0 = lfb[:, (forget[0] + e) * P:(forget[0] + e + 1) * P]
                    m += [(ps[:, 3, e * P:(e + 1) * P], l0, ntri[:, 0:P], False, e == 1)]
            t = mms(m, [*waits, *bank_waits(2, 3)])
            sc = s_buf[:, j * 768:(j + 1) * 768]
            old = s_users[j]
            if forget:
                ts_ = []
                for a, lo, n in ((1, 0, S), (0, 512, P)):
                    for e in range(2):
                        r = slice(lo + e * n, lo + (e + 1) * n)
                        ts_.append(stt(sc[:, r], bank(2, 2)[:, r], cq[:, a, forget[0] + e:forget[0] + e + 1],
                                       bias[:, r], ALU.add, ALU.add, [t, t_cq, *old]))
            else:
                ts_ = [tt(sc, bank(2, 2)[:, 0:768], bias, ALU.add, [t, *old])]
            free[2] = free[3] = [ts_[-1]]
            b0 = 192 + 32 * j
            mx, ng_, sm, ex = (stat[:, b0 + 4 * i:b0 + 4 * i + 4] for i in range(4))
            rec = stat[:, b0 + 16 + 4 * 0:b0 + 20]
            m1 = red(mx[:, 2:4], sc[:, 0:512].rearrange("p (e t) -> p e t", e=2), ALU.max, ts_)
            m0 = red(mx[:, 0:2], sc[:, 512:768].rearrange("p (e t) -> p e t", e=2), ALU.max, ts_)
            if sink is not None:
                mx2 = mx.rearrange("p (a e) -> p a e", a=2)
                sk = sink.unsqueeze(1).to_broadcast([P, 2, 2])
                m0 = tt(mx2, mx2, sk, ALU.max, [m0, m1])
                x1 = tt(ex.rearrange("p (a e) -> p a e", a=2), sk, mx2, ALU.subtract, [m0])
            t = ts(ng_, mx, -1.0, None, ALU.mult, None, [m0, m1])
            last = []
            for c, lo, n in ((2, 0, S), (3, S, S), (0, 512, P), (1, 640, P)):
                last.append(act(sc[:, lo:lo + n], sc[:, lo:lo + n], ACT.Exp, [t], bias=ng_[:, c:c + 1],
                                accum_out=sm[:, c:c + 1]))
            w = [*last]
            if sink is not None:
                x2 = act(ex, ex, ACT.Exp, [x1])
                w = [tt(sm, sm, ex, ALU.add, [x2, *last])]
            job["rec"] = p.op("dve", lambda *i: V.reciprocal(rec, sm), w)
            job["rec_ap"] = rec
            job["probs"] = last
            return job

        s_users, pt_users = [[], []], [[], []]
        o_free = {6: [], 7: []}

        def turn(job):
            j = job["j"]
            sc = s_buf[:, j * 768:(j + 1) * 768]
            t = transposes([(bank(4, 2)[:, i * P:(i + 1) * P], sc[:, i * P:(i + 1) * P], P) for i in range(6)],
                           [*job["probs"], *bank_waits(4, 5)])
            s_users[j] = [t]
            e = act(pt_buf[:, j * 768:(j + 1) * 768], bank(4, 2)[:, 0:768], ACT.Copy, [t, *pt_users[j]])
            free[4] = free[5] = [e]
            job["pt"] = e

        def values(job, v, waits, evac):
            j = job["j"]
            b = 6 + j
            pt = pt_buf[:, j * 768:(j + 1) * 768]
            o = ps[:, b, 0:256].rearrange("p (a e d) -> p a e d", a=TT, e=2)
            m = []
            for e in range(2):
                m.append((o[:, 0, e, :], pt[:, 512 + e * P:512 + (e + 1) * P], v(0, e), True, True))
                for kt in range(2):
                    m.append((o[:, 1, e, :], pt[:, e * S + kt * P:e * S + (kt + 1) * P], v(kt, e), kt == 0, kt == 1))
            t = mms(m, [job["pt"], *waits, *bank_waits(b)])
            pt_users[j] = [t]
            free[b] = evac(o, job["rec_ap"].rearrange("p (a e) -> p a e", a=2), [t, job["rec"]])

        t_fox = []

        def fox_evac(pr):
            def evac(o, rec, w):
                e = tt(z3[:, :, ZFQ + pr * P:ZFQ + (pr + 1) * P].rearrange("p a (e d) -> p a e d", e=2), o,
                       bc(rec, HD), ALU.mult, w)
                t_fox.append(e)
                return [e]
            return evac

        jobs = []
        for pr in range(PAIRS):
            jobs.append((
                lambda pr=pr: scores(lambda a: buf_a[:, pr * S + a * P:pr * S + (a + 1) * P],
                                     fox_k[:, pr * 512:(pr + 1) * 512], [*t_fq, *t_fk, t_lfb], c1("causal"),
                                     forget=(2 * pr,)),
                lambda job, pr=pr: values(job, lambda kt, e: z3[:, kt, ZFV + (2 * pr + e) * HD:
                                                                ZFV + (2 * pr + e + 1) * HD],
                                          done_z[2], fox_evac(pr))))

        t_nsa = {}
        fs = stat[:, 256:264].rearrange("p (a e) -> p a e", a=2)

        def nsa_dst(r):
            return z3[:, :, ZNQ + r * P:ZNQ + (r + 1) * P].rearrange("p a (e d) -> p a e d", e=2)

        def nsa_evac(r, branch):
            def evac(o, rec, w):
                f = stat[:, 256 + 8 * branch:260 + 8 * branch].rearrange("p (a e) -> p a e", a=2)
                tmp = scr[:, 1024 + 256 * branch:1280 + 256 * branch].rearrange("p (a e d) -> p a e d", a=2, e=2)
                e1 = tt(f, rec, ng[:, :, branch, 2 * r:2 * r + 2], ALU.mult, [*w, t_ng])
                e2 = tt(tmp, o, bc(f, HD), ALU.mult, [e1])
                e3 = tt(nsa_dst(r), nsa_dst(r), tmp, ALU.add, [e2, t_nsa[r]])
                t_nsa[r] = e3
                return [e2]
            return evac

        for branch, kk, zv, tk in ((1, slc_k, ZVS, t_ks), (2, win_k, ZVW, t_kw)):
            for r in range(PAIRS):
                jobs.append((
                    lambda r=r, kk=kk, tk=tk: scores(lambda a: buf_b[:, r * S + a * P:r * S + (a + 1) * P], kk,
                                                     [*t_nq, *tk], c1("alibi")[:, r * 768:(r + 1) * 768]),
                    lambda job, r=r, zv=zv, branch=branch: values(
                        job, lambda kt, e: z3[:, kt, zv + e * HD:zv + (e + 1) * HD],
                        [*done_z[4], *done_z[5]], nsa_evac(r, branch))))

        def run_jobs(jobs, between=lambda i: None):
            job = jobs[0][0]()
            for i in range(len(jobs)):
                nxt = jobs[i + 1][0]() if i + 1 < len(jobs) else None
                turn(job)
                between(i)
                jobs[i][1](job)
                job = nxt

        run_jobs(jobs[:PAIRS])

        kv2 = buf_c[:, 0:1024].rearrange("p (c g t) -> p c g t", c=2, g=2)
        blk = [buf_d[:, 0:1024].rearrange("p (m g n) -> p m g n", m=16, g=2),
               buf_d[:, 1024:2048].rearrange("p (m g n) -> p m g n", m=16, g=2)]
        hid_c = scr[:, 0:1024]
        t_blk0 = memz(buf_d[:, :], t_fox)
        t_cmp = []
        cmp_out = []
        for c in range(2):
            zc = (ZKC, ZVC)[c]
            w, ready, s = load_panel(PN_CMP + c)
            t = transposes([(ps[:, c, a * P:(a + 1) * P], z3[:, a, zc:zc + P], P) for a in range(TT)],
                           [*done_z[4], *bank_waits(c)])
            cp = []
            for g in range(2):
                for jp in range(2):
                    cp.append(copy(kv2[jp * HD:(jp + 1) * HD, c, g, 0:S - jp], ps[g * HD:(g + 1) * HD, c, jp:S], [t]))
            free[c] = [cp[-1]]
            src = kv2[:, c, :, :]
            bt = []
            pos_ap = prmc(("pos_k", "pos_v")[c])
            for g in range(2):
                even = src[:, g, :].rearrange("p (n m j) -> p m n j", n=16, j=2)[:, :, :, 0]
                bt.append(tt(blk[c][:, 0:8, g, 0:N_CMP], even[:, :, 0:N_CMP], bc(pos_ap[:, 0:8], N_CMP), ALU.add,
                             [*cp, t_blk0]))
                bt.append(tt(blk[c][:, 8:16, g, 0:N_CMP], even[:, :, 1:N_CMP + 1], bc(pos_ap[:, 8:16], N_CMP),
                             ALU.add, [*cp, t_blk0]))
            w1 = w.rearrange("p (m n) -> p m n", m=16)
            t = mms([(ps[0:64, 2 + c, 0:256], blk[c][:, m, :, :].rearrange("p g n -> p (g n)"), w1[:, m, :],
                      m == 0, m == 15) for m in range(16)], [ready, *bt, *bank_waits(2 + c)])
            slot_free[s] = [t]
            hid = hid_c[0:64, c * 256:(c + 1) * 256]
            t = act(hid, ps[0:64, 2 + c, 0:256], ACT.Gelu_apprx_tanh, [t])
            free[2 + c] = [t]
            t = transposes([(ps[:, 4 + c, i * 64:(i + 1) * 64], hid[:, i * P:(i + 1) * P], 64) for i in range(2)],
                           [t, *bank_waits(4 + c)])
            hT_c = scr[:, 512 + c * 128:512 + (c + 1) * 128]
            t = copy(hT_c, ps[:, 4 + c, 0:128], [t])
            free[4 + c] = [t]
            w2 = prmc(("w2_k", "w2_v")[c])
            t = mms([(ps[0:64, 6 + c, 0:64], hT_c[:, i * 64:(i + 1) * 64], w2[:, i * 64:(i + 1) * 64], i == 0, i == 1)
                     for i in range(2)], [t, *bank_waits(6 + c)])
            cmp_out.append(t)
        kcn = scr[0:64, 768:832]
        sq = scr[0:64, 832:896]
        ss = stat[0:64, 288:289]
        t = act(kcn, ps[0:64, 6, 0:64], ACT.Copy, [cmp_out[0]])
        free[6] = [t]
        t1 = tt(sq, kcn, kcn, ALU.mult, [t])
        t1 = red(ss, sq, ALU.add, [t1])
        t1 = rstd(ss, ss, HD, [t1])
        t1 = ts(kcn, kcn, ss, None, ALU.mult, None, [t1])
        t1 = transposes([(ps[0:64, 4, 0:64], kcn, 64)], [t1, *bank_waits(4)])
        kc_bd = buf_c[:, 1024:1088]
        t_z = memz(buf_c[:, 1024:1216])
        t_kc = [ts(kc_bd[g * HD:(g + 1) * HD, g * 32:(g + 1) * 32], ps[0:64, 4, g * 32:(g + 1) * 32],
                   prmc("nk_g")[0:64, :], None, ALU.mult, None, [t1, t_z]) for g in range(2)]
        free[4] = [t_kc[-1]]
        vc_bd = buf_c[0:64, 1088:1216]
        t_vc = [copy(vc_bd[g * 32:(g + 1) * 32, g * HD:(g + 1) * HD], ps[g * 32:(g + 1) * 32, 7, 0:64],
                     [cmp_out[1], t_z]) for g in range(2)]
        free[7] = [t_vc[-1]]
        qb = lambda r, a: buf_b[:, r * S + a * P:r * S + (a + 1) * P]
        t = mms([(ps[:, 2, (a * 4 + r) * 64:(a * 4 + r + 1) * 64], qb(r, a), kc_bd, True, True)
                 for a in range(TT) for r in range(PAIRS)], [*t_kc, *t_nq, *bank_waits(2)])
        sc = s_buf[:, 0:512]
        t = tt(sc, ps[:, 2, :], c1("cmp"), ALU.add, [t, *s_users[0]])
        free[2] = [t]
        sc3 = sc.rearrange("p (h n) -> p h n", n=CMP_PAD)
        mx = stat[:, 320:336]
        sm = stat[:, 336:352]
        fc = stat[:, 352:368]
        t = red(mx, sc3, ALU.max, [t])
        t = tt(sc3, sc3, bc(mx, CMP_PAD), ALU.subtract, [t])
        t_pc = act(sc, sc, ACT.Exp, [t])
        t = red(sm, sc3, ALU.add, [t_pc])
        t = p.op("dve", lambda *i: V.reciprocal(sm, sm), [t])
        fc3 = fc.rearrange("p (a h) -> p a h", a=TT)
        t = tt(fc3, sm.rearrange("p (a h) -> p a h", a=TT), ng[:, :, 0, :], ALU.mult, [t, t_ng])
        t_fc = tt(fc3, fc3, bc(c1("any"), 8), ALU.mult, [t])
        t = transposes([(ps[0:64, 4 + a, r * P:(r + 1) * P], sc[:, (a * 4 + r) * 64:(a * 4 + r + 1) * 64], P)
                        for a in range(TT) for r in range(PAIRS)], [t_pc, *bank_waits(4, 5)])
        s_users[0] = [t]
        pct = scr[0:64, 1024:2048]
        t = act(pct, bank(4, 2)[0:64, :], ACT.Copy, [t])
        free[4] = free[5] = [t]
        t = mms([(ps[:, 4 + a, r * P:(r + 1) * P], pct[:, (a * 4 + r) * P:(a * 4 + r + 1) * P], vc_bd, True, True)
                 for a in range(TT) for r in range(PAIRS)], [t, *t_vc])
        for a in range(TT):
            e = tt(z3[:, a, ZNQ:ZNQ + 512].rearrange("p (h d) -> p h d", h=8),
                   ps[:, 4 + a, :].rearrange("p (h d) -> p h d", h=8), bc(fc3[:, a, :], HD), ALU.mult, [t, t_fc])
        free[4] = free[5] = [e]
        for r in range(PAIRS):
            t_nsa[r] = e

        run_jobs(jobs[PAIRS:])

        def turn_512(dst, col, waits, b):
            outs = []
            for i in range(2):
                t1 = transposes([(ps[:, b + i, f * S + a * P:f * S + (a + 1) * P],
                                  z3[:, a, col + (2 * i + f) * P:col + (2 * i + f + 1) * P], P)
                                 for f in range(2) for a in range(TT)], [*waits, *bank_waits(b + i)])
                t2 = copy(dst[:, i * 512:(i + 1) * 512], ps[:, b + i, :], [t1], "act" if i else "dve")
                free[b + i] = [t2]
                outs.append(t2)
            return outs

        t_fT = turn_512(buf_a, ZFQ, t_fox, 2)
        t_nT = turn_512(buf_b, ZNQ, list(t_nsa.values()), 4)
        wf, rf, sf = load_panel(PN_FOX_UP)
        wn, rn, sn = load_panel(PN_NSA_UP)
        t_mix = []
        for i in range(4):
            ba, bb = (0, 1) if i % 2 == 0 else (2, 3)
            ta = mms([(ps[:, ba, f * S:(f + 1) * S], k1024(wf)[:, k, (2 * i + f) * P:(2 * i + f + 1) * P],
                       buf_a[:, k * S:(k + 1) * S], k == 0, k == 3) for f in range(2) for k in range(4)],
                     [rf, *t_fT, *bank_waits(ba)])
            tb = mms([(ps[:, bb, f * S:(f + 1) * S], k1024(wn)[:, k, (2 * i + f) * P:(2 * i + f + 1) * P],
                       buf_b[:, k * S:(k + 1) * S], k == 0, k == 3) for f in range(2) for k in range(4)],
                     [rn, *t_nT, *bank_waits(bb)])
            m0 = hT[:, 2 * i * S:(2 * i + 2) * S]
            tmp = scr[:, (i % 2) * 512:(i % 2) * 512 + 512]
            e1 = tt(m0, ps[:, ba, :], gates[:, 2 * i * S:(2 * i + 2) * S], ALU.mult, [ta, *t_gate[0]])
            e2 = tt(tmp, ps[:, bb, :], gates[:, (8 + 2 * i) * S:(8 + 2 * i + 2) * S], ALU.mult, [tb, *t_gate[1]])
            free[ba], free[bb] = [e1], [e2]
            t_mix.append(tt(m0, m0, tmp, ALU.add, [e1, e2]))
        slot_free[sf], slot_free[sn] = [ta], [tb]

        def down(panels_, lhs, waits, b0, nk):
            for n, load in enumerate(panels_):
                w, ready, s = load()
                t = mms([(ps[:, b0 + 2 * a + h, :], lhs(4 * n + k, a), k1024(w)[:, k, h * 512:(h + 1) * 512],
                          n == 0 and k == 0, n == len(panels_) - 1 and k == 3)
                         for k in range(4) for a in range(TT) for h in range(2)],
                        [ready, *waits, *(bank_waits(*range(b0, b0 + 4)) if n == 0 else [])])
                slot_free[s] = [t]
            return t

        t = down([lambda: load_panel(PN_OUT), lambda: load_panel(PN_OUT + 1)], lambda k, a: hT3[:, k, a * P:(a + 1) * P], t_mix, 4, 8)
        t_x1 = []
        for b in range(4):
            xs = x_tok[:, b * 512:(b + 1) * 512]
            e = tt(xs, xs, ps[:, 4 + b, :], ALU.add, [t])
            free[4 + b] = [e]
            t_x1.append(e)

        t_h = norm_transpose(t_x1, prmc("g_ffn"), [])
        wr = prmc("w_route").rearrange("p (k n) -> p k n", k=KT)
        t = mms([(ps[:, 0, a * 20:(a + 1) * 20], hT3[:, k, a * P:(a + 1) * P], wr[:, k, :], k == 0, k == KT - 1)
                 for a in range(TT) for k in range(KT)], [*t_h, *bank_waits(0)])
        at = [384]

        def small(n):
            at[0] += n
            return stat[:, at[0] - n:at[0]]

        lg = small(40).rearrange("p (a n) -> p a n", a=TT)
        t = tt(lg, ps[:, 0, 0:40].rearrange("p (a n) -> p a n", a=TT),
               prmc("b_route").unsqueeze(1).to_broadcast([P, TT, 20]), ALU.add, [t])
        free[0] = [t]

        def softmax4(src, w):
            m, e_, r = small(2), small(8).rearrange("p (a n) -> p a n", a=TT), small(2)
            w = red(m, src, ALU.max, [w])
            w = tt(e_, src, bc(m, 4), ALU.subtract, [w])
            w = act(e_, e_, ACT.Exp, [w])
            w = red(r, e_, ALU.add, [w])
            w = p.op("dve", lambda *i: V.reciprocal(r, r), [w])
            return e_, r, w

        first = c1("first").unsqueeze(1).to_broadcast([P, TT, 4])

        def top1(src, w):
            m, oh, i_ = small(2), small(8).rearrange("p (a n) -> p a n", a=TT), small(2)
            w = red(m, src, ALU.max, [w])
            w = tt(oh, src, bc(m, 4), ALU.is_equal, [w])
            w = tt(oh, oh, first, ALU.mult, [w])
            w = red(i_, oh, ALU.max, [w])
            w = tt(oh, oh, bc(i_, 4), ALU.is_equal, [w])
            return oh, m, w

        ge, gr, tg = softmax4(lg[:, :, 0:4], t)
        goh, gm, tg = top1(ge, tg)
        pg = small(2)
        tg = tt(pg, gm, gr, ALU.mult, [tg])
        sel = small(32).rearrange("p (a g j) -> p a g j", a=TT, g=4)
        e16 = lg[:, :, 4:20].rearrange("p a (g j) -> p a g j", g=4)
        tg = tt(sel, e16, bc(goh, 4), ALU.mult, [tg])
        ein = small(8).rearrange("p (a n) -> p a n", a=TT)
        tg = red(ein, sel.rearrange("p a g j -> p a j g"), ALU.add, [tg])
        pe_, pr_, tg = softmax4(ein, tg)
        pn = small(8).rearrange("p (a n) -> p a n", a=TT)
        tg = tt(pn, pe_, bc(pr_, 4), ALU.mult, [tg])
        oh1, m1, tg = top1(pn, tg)
        pn2 = small(8).rearrange("p (a n) -> p a n", a=TT)
        tg = ts(pn2, oh1, -2.0, None, ALU.mult, None, [tg])
        tg = tt(pn2, pn2, pn, ALU.add, [tg])
        oh2, m2, tg = top1(pn2, tg)
        msum = small(2)
        tg = tt(msum, m1, m2, ALU.add, [tg])
        tg = p.op("dve", lambda *i: V.reciprocal(msum, msum), [tg])
        tg = tt(msum, msum, pg, ALU.mult, [tg])
        tg = tt(oh1, oh1, oh2, ALU.add, [tg])
        tg = tt(oh1, oh1, pn, ALU.mult, [tg])
        tg = tt(oh1, oh1, bc(msum, 4), ALU.mult, [tg])
        goh2 = small(8)
        t_goh = copy(goh2.rearrange("p (a g) -> p a g", a=TT), goh, [tg])
        rank = small(8)
        over = small(4)
        t = mms([(ps[:, 1, 0:4], ntri[:, 0:P], goh2[:, 0:4], True, True),
                 (ps[:, 1, 4:8], ntri[:, P:2 * P], goh2[:, 0:4], True, False),
                 (ps[:, 1, 4:8], ntri[:, 0:P], goh2[:, 4:8], False, True),
                 (ps[:, 1, 8:12], ntri[:, P:2 * P], goh2[:, 0:4], True, False),
                 (ps[:, 1, 8:12], ntri[:, P:2 * P], goh2[:, 4:8], False, True)], [t_goh, *bank_waits(1)])
        t_rank = ts(rank, ps[:, 1, 0:8], -1.0, -1.0, ALU.mult, ALU.add, [t])
        t1 = ts(over, ps[:, 1, 8:12], -1.0, -float(P), ALU.mult, ALU.add, [t])
        free[1] = [t1]
        t1 = ts(over, over, 0.0, None, ALU.max, None, [t1])
        most = small(1)
        t1 = red(most, over, ALU.max, [t1])
        flag = sb("flag", 1, mybir.dt.int32)
        t_flag = copy(flag[:, :], most, [t1])
        comb2 = small(32)
        t_comb2 = [tt(comb2.rearrange("p (a g j) -> p a g j", a=TT, g=4)[:, a, :, :], bc(goh[:, a, :], 4),
                      oh1[:, a, :].unsqueeze(1).to_broadcast([P, 4, 4]), ALU.mult, [tg]) for a in range(TT)]
        assert at[0] <= 768

        sel = buf_a[:, :]
        selT = buf_b[:, :]
        rows_in = gates[:, :]
        rows_out = zin[:, 0:4 * D]
        xg = buf_c[:, 0:1024]
        sg = buf_c[:, 1024:2048]
        hid = buf_d[:, 0:1024]
        hidT = buf_d[:, 1024:2048]
        comb_g = stat[:, 704:768]

        def moe(chunk, waits):
            base = pos[0]
            shifted = stat[:, 1016:1024]
            t = ts(shifted, rank, float(-P * chunk), None, ALU.add, None, [t_rank, *waits])
            t_sel = [ts(sel[:, (a * 4 + g) * P:(a * 4 + g + 1) * P], c1("slot"), shifted[:, a * 4 + g:a * 4 + g + 1],
                        goh2[:, a * 4 + g:a * 4 + g + 1], ALU.is_equal, ALU.mult, [t, t_goh, *waits])
                     for a in range(TT) for g in range(4)]
            t_selT = []
            for i in range(2):
                t = transposes([(ps[:, i, f * S + a * P:f * S + (a + 1) * P],
                                 sel[:, (a * 4 + 2 * i + f) * P:(a * 4 + 2 * i + f + 1) * P], P)
                                for f in range(2) for a in range(TT)], [*t_sel, *bank_waits(i)])
                e = copy(selT[:, i * 512:(i + 1) * 512], ps[:, i, :], [t], "act")
                free[i] = [e]
                t_selT.append(e)
            t = mms([(ps[:, 2, g * 16:(g + 1) * 16], sel[:, (a * 4 + g) * P:(a * 4 + g + 1) * P],
                      comb2[:, a * 16:(a + 1) * 16], a == 0, a == 1) for g in range(4) for a in range(TT)],
                    [*t_sel, *t_comb2, *bank_waits(2)])
            t_cg = copy(comb_g, ps[:, 2, 0:64], [t])
            free[2] = [t_cg]
            t_rows = []
            rin = rows_in.rearrange("p (g k n) -> p k g n", g=4, k=KT)
            for k in range(KT):
                b = 3 + k % 4
                t = mms([(ps[:, b, :], scr[:, a * D + k * P:a * D + (k + 1) * P], sel[:, a * 512:(a + 1) * 512],
                          a == 0, a == 1) for a in range(TT)], [*t_sel, *t_h, *bank_waits(b)])
                src = ps[:, b, :].rearrange("p (g n) -> p g n", g=4)
                if k % 2:
                    e = act(rin[:, k, :, :], src, ACT.Copy, [t], scale=prmc("g_ffn", k, k + 1))
                else:
                    e = ts(rin[:, k, :, :], src, prmc("g_ffn", k, k + 1), None, ALU.mult, None, [t])
                free[b] = [e]
                t_rows.append(e)

            pre = {b: list(free[b]) for b in range(8)}
            slots_pre = [list(x) for x in slot_free]
            carry_bank = [Later() for _ in range(8)]
            carry_slot = [Later() for _ in range(RING)]
            carry_x = Later()
            p.begin_loop(GRP)
            for s in range(RING):
                slot_free[s] = [*slots_pre[s], carry_slot[s]]
            for b in range(8):
                free[b] = [*pre[b], carry_bank[b]]
            t_xg = p.op("pool", lambda *i: G.tensor_copy(xg, rows_in[:, bass.ds(i[-1] * 1024, 1024)]),
                        [*t_rows, carry_x])
            gu = {}
            used_h = [[], []]

            def gate_up(j):
                u = j % 2
                got = []
                for h in range(2):
                    w, ready, s = load_panel(lambda *i, h=h: i[-1] * 12 + (PN_MOE + 3 * j + h))
                    b = 2 * u + h
                    t = mms([(ps[:, b, :], xg[:, k * P:(k + 1) * P], k512(w)[:, k, :], k == 0, k == KT - 1)
                             for k in range(KT)], [ready, t_xg, *bank_waits(b)])
                    slot_free[s] = [t]
                    got.append(t)
                su, hu = sg[:, u * 512:(u + 1) * 512], hid[:, u * 512:(u + 1) * 512]
                e1 = act(su, ps[:, 2 * u, :], ACT.Silu, [got[0]])
                e2 = p.op("dve", lambda *i: V.scalar_tensor_tensor(
                    hu, su, comb_g[:, bass.ds(i[-1] * 20 + j, 1)], ps[:, 2 * u + 1, :], ALU.mult, ALU.mult),
                    [e1, got[1], t_cg, *used_h[u]])
                free[2 * u], free[2 * u + 1] = [e1], [e2]
                gu[j] = (e2, got[1])

            def back(j):
                u = j % 2
                w, ready, s = load_panel(lambda *i: i[-1] * 12 + (PN_MOE + 3 * j + 2))
                hu, tu = hid[:, u * 512:(u + 1) * 512], hidT[:, u * 512:(u + 1) * 512]
                t = transposes([(ps[:, 6, k * P:(k + 1) * P], hu[:, k * P:(k + 1) * P], P) for k in range(4)],
                               [gu[j][0], *bank_waits(6)])
                used_h[u] = [t]
                e = act(tu, ps[:, 6, :], ACT.Copy, [t])
                free[6] = [e]
                t = mms([(ps[:, 4 + h, :], tu[:, k * P:(k + 1) * P], k1024(w)[:, k, h * 512:(h + 1) * 512],
                          j == 0 and k == 0, j == 3 and k == 3) for k in range(4) for h in range(2)],
                        [e, ready, *(bank_waits(4, 5) if j == 0 else [])])
                slot_free[s] = [t]
                return t

            gate_up(0)
            for j in range(EPG):
                if j + 1 < EPG:
                    gate_up(j + 1)
                t = back(j)
            carry_x.token = gu[3][1].prev()
            e4 = p.op("act", lambda *i: A.activation(rows_out[:, bass.ds(i[-1] * D, 512)], ps[:, 4, :], ACT.Copy),
                      [t, *waits])
            e5 = p.op("dve", lambda *i: V.tensor_copy(rows_out[:, bass.ds(i[-1] * D + 512, 512)], ps[:, 5, :]),
                      [t, *waits])
            free[4], free[5] = [e4], [e5]
            for s in range(RING):
                carry_slot[s].token = slot_free[s][0].prev()
            for b in range(7):
                carry_bank[b].token = free[b][0].prev()
            free[7] = pre[7]
            p.end_loop()
            assert (pos[0] - base) % RING == 0

            outs = []
            for a in range(TT):
                for h in range(2):
                    b = 2 * a + h
                    t = mms([(ps[:, b, :], selT[:, g * S + a * P:g * S + (a + 1) * P],
                              rows_out[:, g * D + h * 512:g * D + (h + 1) * 512], g == 0, g == 3)
                             for g in range(4)], [e4, e5, *t_selT, *bank_waits(b)])
                    xs = x_tok[:, b * 512:(b + 1) * 512]
                    e = tt(xs, xs, ps[:, b, :], ALU.add, [t])
                    free[b] = [e]
                    outs.append(e)
            return outs

        t_x2 = moe(0, t_x1)
        keep = pos[0]
        p.begin_if(flag[0:1, 0:1], [t_flag])
        t_x2 = moe(1, t_x2)
        p.end_if()
        pos[0] = keep

        t_c2 = p.dma("act", lambda *i: A.dma_start(cst[:, 0:C2_W], c2_in), "cst", t_x2)
        lbp = prmc("lb").rearrange("p (l h) -> p l h", l=LAYERS)
        e_l, m_l = stat[:, 768:784].rearrange("p (l h) -> p l h", l=LAYERS), stat[:, 784:792]
        t = tt(m_l, lbp[:, 0, :], lbp[:, 1, :], ALU.max)
        t = tt(e_l, lbp, m_l.unsqueeze(1).to_broadcast([P, LAYERS, HG]), ALU.subtract, [t])
        t = act(e_l, e_l, ACT.Exp, [t])
        t = tt(m_l, e_l[:, 0, :], e_l[:, 1, :], ALU.add, [t])
        t = p.op("dve", lambda *i: V.reciprocal(m_l, m_l), [t])
        t = tt(e_l, e_l, m_l.unsqueeze(1).to_broadcast([P, LAYERS, HG]), ALU.mult, [t])
        t = tt(e_l[:, 1, :], e_l[:, 0, :], e_l[:, 1, :], ALU.add, [t])
        t = tt(e_l[:, 1, :], e_l[:, 1, :], e_l[:, 0, :], ALU.subtract, [t])
        t = tt(e_l[:, 0, :], e_l[:, 0, :], e_l[:, 0, :], ALU.subtract, [t])
        lay3 = lay[:, :].rearrange("p (l n) -> p l n", l=LAYERS)
        one_l, fl_l, kf_l = (lay3[:, :, PL_IN + 8 * i:PL_IN + 8 * i + 8] for i in range(3))
        t_l1 = ts(one_l, e_l, -1.0, 1.0, ALU.mult, ALU.add, [t, *t_lay])
        t_l2 = ts(fl_l, e_l, LB_FLOOR, None, ALU.max, None, [t])
        t_l3 = tt(kf_l, e_l, fl_l, ALU.subtract, [t_l2])

        cur = stat[:, 800:800 + PL_W]
        post = keys[:, 1024:2048]
        zb3 = zin[:, :].rearrange("p (a n) -> p a n", a=TT)
        ZI, ZZ, ZQA, ZKA, ZVA, ZZA = 0, 1024, 2048, 3072, 3200, 3328
        level_mask = c2("level").bitcast(U32).rearrange("p (l t) -> p l t", l=LEVELS)

        slots_pre = [list(x) for x in slot_free]
        carry_slot = [Later() for _ in range(RING)]
        carry_x = [Later() for _ in range(4)]
        p.begin_loop(LAYERS)
        pos[0] = 0
        for s in range(RING):
            slot_free[s] = [*slots_pre[s], carry_slot[s]]
        x_old = [*t_x2, *carry_x]
        for b in range(8):
            free[b] = []
        s_users[0], s_users[1], pt_users[0], pt_users[1] = [], [], [], []
        t_cur = p.op("dve", lambda l: V.tensor_copy(cur, lay[:, bass.ds(l * PL_W, PL_W)]),
                     [*x_old, t_l1, t_l2, t_l3])
        t_post = p.dma("act", lambda l: A.dma_start(post, post_in[l].partition_broadcast(P)), "post", x_old)
        t_A0 = memz(buf_c[:, :], x_old, "dve")
        t_h = norm_transpose([*x_old, t_cur], cur[:, 0:8], [])
        nxt_panel = [0]

        def layer_panel():
            n = nxt_panel[0]
            nxt_panel[0] += 1
            return load_panel(lambda l: l * L2_PANELS + (PN_L2 + n))

        def token_panel(col, n, func=None):
            got = []

            def evac(a, src, t):
                dst = zb3[:, a, col:col + n]
                e = act(dst, src, func, [t]) if func is not None else copy(dst, src, [t], "act" if a else "dve")
                got.append(e)
                return [e]
            proj_token(layer_panel(), n, t_h, evac)
            return got

        t_qa = token_panel(ZQA, 512) + token_panel(ZQA + 512, 512)
        t_kva = token_panel(ZKA, 256)

        def rope(col, n, dst, t1, t2, waits):
            half = HD // 2
            v = zb3[:, :, col:col + n * HD].rearrange("p a (h d) -> p a h d", h=n)
            u1, u2 = (x.rearrange("p (a h d) -> p a h d", a=TT, h=n) for x in (t1, t2))
            x1, x2 = v[:, :, :, 0:half], v[:, :, :, half:HD]
            co, si = (c2(x).rearrange("p (a d) -> p a d", a=TT).unsqueeze(2).to_broadcast([P, TT, n, half])
                      for x in ("cos", "sin"))
            a1 = tt(u1, x1, co, ALU.mult, waits)
            a2 = tt(u2, x2, si, ALU.mult, waits)
            b1 = tt(dst[:, :, :, 0:half], u1, u2, ALU.subtract, [a1, a2])
            a1 = tt(u1, x2, co, ALU.mult, [b1])
            a2 = tt(u2, x1, si, ALU.mult, [b1])
            b2 = tt(dst[:, :, :, half:HD], u1, u2, ALU.add, [a1, a2])
            return [b1, b2]

        t_rk = rope(ZKA, 2, pt_buf[:, 1024:1280].rearrange("p (a h d) -> p a h d", a=TT, h=2),
                    s_buf[:, 1024:1152], s_buf[:, 1152:1280], [*t_kva, t_c2])
        t_rq = rope(ZQA, 16, scr[:, :].rearrange("p (a h d) -> p a h d", a=TT, h=16),
                    s_buf[:, 0:1024], pt_buf[:, 0:1024], [*t_qa, t_c2])

        Q, K, FG = gates[:, 0:2048], gates[:, 2048:4096], buf_d[:, :]
        one_m, floor_, kf = (cur[:, PL_IN + 8 * i:PL_IN + 8 * i + 8] for i in range(3))
        t_q, t_f, t_k = {}, {}, {}
        for j in range(2):
            def q_evac(b, src, t, j=j):
                c = (4 * j + 2 * b) * S
                e = act(Q[:, c:c + 512], src, ACT.Silu, [t])
                t_q.setdefault(j, []).append(e)
                return [e]

            def f_evac(b, src, t, j=j):
                h = 4 * j + 2 * b
                c = h * S
                e1 = act(FG[:, c:c + 512], src, ACT.Sigmoid, [t])
                e2 = act(K[:, c:c + 512], src, ACT.Sigmoid, [t], scale=-1.0)
                for i in range(2):
                    r = slice(c + i * S, c + (i + 1) * S)
                    t_f.setdefault(j, []).append(ts(FG[:, r], FG[:, r], one_m[:, h + i:h + i + 1],
                                                    floor_[:, h + i:h + i + 1], ALU.mult, ALU.add, [e1]))
                    t_k.setdefault(j, []).append(ts(K[:, r], K[:, r], one_m[:, h + i:h + i + 1],
                                                    kf[:, h + i:h + i + 1], ALU.mult, ALU.add, [e2]))
                return [e2]
            proj_feature(layer_panel(), t_h, q_evac)
            proj_feature(layer_panel(), t_h, f_evac)
        t_i = token_panel(ZI, 512) + token_panel(ZI + 512, 512)
        t_zh = token_panel(ZZ, 512, ACT.Silu) + token_panel(ZZ + 512, 512, ACT.Silu)
        t_za = token_panel(ZZA, 512, ACT.Silu) + token_panel(ZZA + 512, 512, ACT.Silu)

        t_qT = []
        for a in range(TT):
            for i in range(2):
                b = 4 + 2 * a + i
                t = transposes([(ps[:, b, r * P:(r + 1) * P], scr[:, a * D + (4 * i + r) * P:a * D + (4 * i + r + 1) * P], P)
                                for r in range(4)], [*t_rq, *bank_waits(b)])
                e = ts(zb3[:, a, ZQA + i * 512:ZQA + (i + 1) * 512], ps[:, b, :], HD ** -0.5, None, ALU.mult, None, [t])
                free[b] = [e]
                t_qT.append(e)
        t = transposes([(ps[:, 2, a * P:(a + 1) * P], pt_buf[:, 1024 + a * P:1024 + (a + 1) * P], P)
                        for a in range(TT)], [*t_rk, *bank_waits(2)])
        t_kT = [copy(keys[e * HD:(e + 1) * HD, e * S:(e + 1) * S], ps[e * HD:(e + 1) * HD, 2, 0:S], [t])
                for e in range(2)]
        free[2] = [t_kT[-1]]

        t_swa = []

        def swa_evac(r):
            def evac(o, rec, w):
                e = tt(zb3[:, :, ZQA + r * P:ZQA + (r + 1) * P].rearrange("p a (e d) -> p a e d", e=2), o,
                       bc(rec, HD), ALU.mult, w)
                t_swa.append(e)
                return [e]
            return evac

        run_jobs([(lambda r=r: scores(lambda a: zb3[:, a, ZQA + r * P:ZQA + (r + 1) * P], keys[:, 0:512],
                                      [*t_qT, *t_kT], c2("band"), sink=cur[:, 136 + 2 * r:138 + 2 * r]),
                   lambda job, r=r: values(job, lambda kt, e: zb3[:, kt, ZVA + e * HD:ZVA + (e + 1) * HD],
                                           t_kva, swa_evac(r)))
                  for r in range(SWA_PAIRS)])

        t_A = {}
        for j in range(2):
            q, k, f = (x[:, j * 1024:(j + 1) * 1024] for x in (Q, K, FG))
            am = buf_c[:, j * 1024:(j + 1) * 1024].rearrange("p (n t) -> p n t", n=8)
            tq, tk, tf = t_q[j], t_k[j], t_f[j]
            tot, t_tot = f, tf
            t_am = [t_A0]
            for lv in range(LEVELS):
                b = 2 + 2 * ((lv + j) % 2)
                t = mms([(ps[:, b + n // 4, (n % 4) * P:(n % 4 + 1) * P], k[:, n * P:(n + 1) * P],
                          q[:, n * P:(n + 1) * P], True, True) for n in range(8)], [*tq, *tk, *bank_waits(b, b + 1)])
                if lv == 0:
                    tq = [tt(q, q, f, ALU.mult, [t, *tf, *t_am])]
                else:
                    m = 1 << (lv - 1)
                    qv, kv = (x.rearrange("p (b two m) -> p b two m", two=2, m=m) for x in (q, k))
                    tv = tot.rearrange("p (b two) -> p b two", two=2)
                    tq = [tt(qv[:, :, 1, :], qv[:, :, 1, :], bc(tv[:, :, 0], m), ALU.mult, [t, *t_tot, *t_am])]
                    tk = [tt(kv[:, :, 0, :], kv[:, :, 0, :], bc(tv[:, :, 1], m), ALU.mult, [t, *t_tot])]
                    n = 1024 >> lv
                    new = (buf_b[:, j * 512:j * 512 + n] if lv % 2 else f[:, 0:n])
                    t_tot = [tt(new, tv[:, :, 0], tv[:, :, 1], ALU.mult, t_tot)]
                    tot = new
                mask = level_mask[:, lv, :].unsqueeze(1).to_broadcast([P, 8, P])
                data = bank(b, 2).rearrange("p (n t) -> p n t", n=8)
                e = p.op("dve", lambda *i, am=am, mask=mask, data=data: V.copy_predicated(am, mask, data),
                         [t, *t_am])
                t_am = [e]
                free[b] = free[b + 1] = [e]
            t = mms([(ps[:, 6, h * P:(h + 1) * P], k[:, h * S:h * S + P], q[:, h * S + P:(h + 1) * S], True, True)
                     for h in range(4)], [*tq, *tk, *bank_waits(6)])
            cross = buf_a[:, j * 512:(j + 1) * 512]
            t = act(cross, ps[:, 6, :], ACT.Copy, [t])
            free[6] = [t]
            m = []
            for h in range(4):
                hc = slice(ZI + (4 * j + h) * P, ZI + (4 * j + h + 1) * P)
                m += [(ps[:, 6, h * P:(h + 1) * P], am[:, 2 * h, :], zb3[:, 0, hc], True, True),
                      (ps[:, 7, h * P:(h + 1) * P], am[:, 2 * h + 1, :], zb3[:, 1, hc], True, False),
                      (ps[:, 7, h * P:(h + 1) * P], cross[:, h * P:(h + 1) * P], zb3[:, 0, hc], False, True)]
            t = mms(m, [t, *t_am, *t_i, *bank_waits(6, 7)])
            t_A[j] = []
            for a in range(TT):
                e = act(zb3[:, a, ZI + j * 512:ZI + (j + 1) * 512], ps[:, 6 + a, :], ACT.Copy, [t])
                free[6 + a] = [e]
                t_A[j].append(e)

        oa = zb3[:, :, ZQA:ZQA + 1024]
        t_oa = tt(oa, oa, zb3[:, :, ZZA:ZZA + 1024], ALU.mult, [*t_swa, *t_za], "pool")
        oh = zb3[:, :, ZI:ZI + 1024].rearrange("p a (h d) -> p a h d", h=HG)
        zh = zb3[:, :, ZZ:ZZ + 1024].rearrange("p a (h d) -> p a h d", h=HG)
        g_head = cur[:, 8:136].unsqueeze(1).unsqueeze(1).to_broadcast([P, TT, HG, P])
        t_gz = tt(zh, zh, g_head, ALU.mult, [*t_zh, t_cur], "pool")
        sq = scr[:, :].rearrange("p (a h d) -> p a h d", a=TT, h=HG)
        ss = stat[:, 992:1008].rearrange("p (a h) -> p a h", a=TT)
        t = tt(sq, oh, oh, ALU.mult, [*t_A[0], *t_A[1]])
        t = red(ss, sq, ALU.add, [t])
        t = rstd(ss, ss, P, [t])
        t = tt(oh, oh, bc(ss, P), ALU.mult, [t])
        t_oh = tt(oh, oh, zh, ALU.mult, [t, t_gz])

        oT = gates
        t_oT = []
        for i in range(8):
            b = i % 4
            col = (ZI if i < 4 else ZQA) + (i % 4) * 2 * P
            t = transposes([(ps[:, b, f * S + a * P:f * S + (a + 1) * P], zb3[:, a, col + f * P:col + (f + 1) * P], P)
                            for f in range(2) for a in range(TT)], [t_oh if i < 4 else t_oa, *bank_waits(b)])
            e = copy(oT[:, i * 512:(i + 1) * 512], ps[:, b, :], [t, t_oh], "act" if i % 2 else "dve")
            free[b] = [e]
            t_oT.append(e)
        t = down([layer_panel] * 4, lambda k, a: oT[:, k * S + a * P:k * S + (a + 1) * P], t_oT, 4, 16)
        ssb = stat[:, 1008:1012]
        sst, rst = stat[:, 1012:1014], stat[:, 1014:1016]
        t1 = [act(scr[:, b * 512:(b + 1) * 512], ps[:, 4 + b, :], ACT.Square, [t], accum_out=ssb[:, b:b + 1])
              for b in range(4)]
        t2 = red(sst, ssb.rearrange("p (a h) -> p a h", a=TT), ALU.add, t1)
        t2 = rstd(rst, sst, D, [t2])
        t_x3 = []
        for b in range(4):
            a, h = b // 2, b % 2
            tmp = scr[:, b * 512:(b + 1) * 512]
            xs = x_tok[:, b * 512:(b + 1) * 512]
            e = stt(tmp, ps[:, 4 + b, :], rst[:, a:a + 1], post[:, h * 512:(h + 1) * 512], ALU.mult, ALU.mult,
                    [t2, t1[b], t_post])
            t_x3.append(tt(xs, xs, tmp, ALU.add, [e]))
        for s in range(RING):
            carry_slot[s].token = slot_free[s][0].prev()
        for b in range(4):
            carry_x[b].token = t_x3[b].prev()
        p.end_loop()

        t = p.dma("sp", lambda *i: nc.sync.dma_start(out.rearrange("o (a p) d -> p (o a) d", p=P), x3), "out", t_x3)
        p.fence("sp", [t])

        block = ctx.enter_context(nc.Block())

        @block.sync
        def _(_e):
            p.emit("sp")

        @block.tensor
        def _(_e):
            p.emit("pe")

        @block.vector
        def _(_e):
            p.emit("dve")

        @block.scalar
        def _(_e):
            p.emit("act")

        @block.gpsimd
        def _(_e):
            p.emit("pool")


def shape_constants():
    f = np.float32
    s = np.arange(P)[:, None]
    ident = np.eye(P, dtype=f)
    ntri = -(s <= np.arange(S)[None, :]).astype(f)

    def by_query(fn):
        k2, k1 = np.arange(S)[None, :], np.arange(P)[None, :]
        return np.concatenate([fn(s + P, k2, 0), fn(s + P, k2, 1), fn(s, k1, 0), fn(s, k1, 1)], 1)

    causal = by_query(lambda q, k, e: np.where(k <= q, 0.0, NEG))
    band = by_query(lambda q, k, e: np.where((k <= q) & (q - k < 128), 0.0, NEG))
    slope = lambda g, r: np.float32(2.0 ** (-(g * PAIRS + r + 1)))
    alibi = np.concatenate([by_query(lambda q, k, e: np.where(k <= q, -slope(e, r) * (q - k), NEG))
                            for r in range(PAIRS)], 1)
    n = np.arange(CMP_PAD)[None, :]
    cmp_, any_ = [], []
    for a in range(TT):
        dist = (s + a * P) - (n * 16 + 31)
        ok = (dist >= 0) & (n < N_CMP)
        for r in range(PAIRS):
            for g in range(2):
                cmp_.append(np.where(ok, -slope(g, r) * dist, NEG))
        any_.append(ok.any(1, keepdims=True).astype(f))
    first = np.broadcast_to(np.array([4, 3, 2, 1], f), (P, 4))
    c1 = np.concatenate([ntri, causal, alibi, *cmp_, *any_, first, np.broadcast_to(np.arange(P), (P, P))], 1).astype(f)
    half = HD // 2
    freq = np.float32(10000.0) ** (-np.arange(half, dtype=f) / np.float32(half))
    ang = [((s + a * P).astype(f) * freq[None, :]).astype(f) for a in range(TT)]
    t = np.arange(P)[None, :]
    levels = [(s == t)]
    for lv in range(1, LEVELS):
        m = 1 << (lv - 1)
        levels.append((s // (2 * m) == t // (2 * m)) & (s % (2 * m) < m) & (t % (2 * m) >= m))
    c2 = np.concatenate([band, *[np.cos(x) for x in ang], *[np.sin(x) for x in ang],
                         *[x.astype(f) for x in levels]], 1).astype(f)
    assert c1.shape[1] == C1_W and c2.shape[1] == C2_W
    return ident, c1, c2


def lay_out(x):
    g = {k: np.asarray(v) for k, v in x.items()}
    w = g["w_in"][0]
    cuts = np.cumsum([512, 512, 512, 8, 512, 128, 128, 128, 128, 128, 128, 24, 1024])
    fq, fk, fv, ff, nq, kc, vc, ks, vs, kw, vw, ng, ga, gb = np.split(w, cuts, axis=1)
    nq = nq.reshape(D, 2, 4, HD).transpose(0, 2, 1, 3).reshape(D, 512)
    ng = ng.reshape(D, 2, 4, 3).transpose(0, 3, 2, 1).reshape(D, 24)
    mixed = np.concatenate([kw, vw, ff, ng, np.zeros((D, 512 - Z5), w.dtype)], 1)

    def cols(m):
        n = m.shape[1] // 512
        return list(m.reshape(KT, P, n, 512).transpose(2, 1, 0, 3).reshape(n, P, PANEL))

    def rows(m):
        n = m.shape[0] // 512
        return list(m.reshape(n, 4, P, D).transpose(0, 2, 1, 3).reshape(n, P, PANEL))

    pan = cols(fq) + cols(fk) + cols(fv) + cols(nq) + cols(np.concatenate([kc, vc, ks, vs], 1)) + cols(mixed)
    pan += cols(ga) + cols(gb)
    for nme in ("cmp_k_w1", "cmp_v_w1"):
        pan.append(g[nme][0].reshape(16, P, 256).transpose(1, 0, 2).reshape(P, PANEL))
    pan += rows(g["w_fox_up"][0])
    pan += rows(g["w_nsa_up"][0].reshape(2, 4, HD, D).transpose(1, 0, 2, 3).reshape(512, D))
    pan += rows(g["w_out"][0])
    for e in range(N_EXP):
        pan += cols(g["w_gate"][0, e]) + cols(g["w_up"][0, e]) + rows(g["w_down"][0, e])
    for l in range(LAYERS):
        w2 = g["w_in_2"][l]
        qh, fh, ih, zh, qa, ka, va, za = np.split(w2, np.cumsum([1024, 1024, 1024, 1024, 1024, 128, 128]), axis=1)
        pair = lambda m: m.reshape(-1, 2, 8, HD).transpose(0, 2, 1, 3).reshape(-1, 1024)
        qa, za = pair(qa), pair(za)
        qh, fh = cols(qh), cols(fh)
        pan += cols(qa) + cols(np.concatenate([ka, va, np.zeros((D, 256), w2.dtype)], 1))
        pan += [qh[0], fh[0], qh[1], fh[1]] + cols(ih) + cols(zh) + cols(za)
        wo = g["w_out_2"][l]
        pan += rows(wo[:1024])
        pan += rows(wo[1024:].reshape(2, 8, HD, D).transpose(1, 0, 2, 3).reshape(1024, D))
    panels = np.stack(pan)
    assert panels.shape[0] == N_PANELS

    def feat(v):
        return v.reshape(-1, P).T

    def every(v):
        return np.broadcast_to(v.reshape(1, -1), (P, v.size))

    def twice(v):
        return np.concatenate([v, v]).reshape(P, 1)

    def pos_(v):
        return v.reshape(16, P).T

    def w2_(v):
        return v.reshape(2, P, HD).transpose(1, 0, 2).reshape(P, 128)

    route = np.concatenate([g["w_group"][0], g["w_router"][0]], 1).reshape(KT, P, 20).transpose(1, 0, 2).reshape(P, 160)
    prm = np.concatenate([
        feat(g["norm_mix_g"][0]), feat(g["norm_ffn_g"][0]), twice(g["fox_q_g"][0]), twice(g["fox_k_g"][0]),
        twice(g["nsa_q_g"][0]), twice(g["nsa_k_g"][0]), pos_(g["cmp_k_pos"][0]), pos_(g["cmp_v_pos"][0]),
        every(g["b_forget"][0]), every(np.concatenate([g["b_group"][0], g["b_router"][0]])), route,
        w2_(g["cmp_k_w2"][0]), w2_(g["cmp_v_w2"][0]),
        g["lb_param_2"].reshape(LAYERS, HG, P).transpose(2, 0, 1).reshape(P, 16)], 1)
    lay = np.stack([np.concatenate([
        feat(g["g_pre_2"][l]), every(g["g_head_2"][l]),
        every(g["sinks_2"][l].reshape(2, 8).T)], 1) for l in range(LAYERS)])
    return {"panels": panels, "x": g["x"], "prm": prm, "lay": lay, "post": g["g_post_2"]}


def kernel(**inputs):
    import concourse.bacc as bacc
    from concourse.bass_utils import run_bass_kernel_spmd

    arrays = lay_out(inputs)
    arrays["ident"], arrays["c1"], arrays["c2"] = shape_constants()
    arrays = {"in_" + k: np.ascontiguousarray(v) for k, v in arrays.items()}
    nc = bacc.Bacc("TRN2", target_bir_lowering=False, num_devices=1)
    aps = {k: nc.dram_tensor(k, v.shape, mybir.dt.from_np(v.dtype), kind="ExternalInput").ap()
           for k, v in arrays.items()}
    out = nc.dram_tensor("out", (1, S, D), F32, kind="ExternalOutput").ap()
    build(nc, aps["in_panels"], aps["in_x"], aps["in_prm"], aps["in_lay"], aps["in_post"], aps["in_ident"],
          aps["in_c1"], aps["in_c2"], out)
    r = run_bass_kernel_spmd(nc, [arrays], core_ids=[0])
    return r.results[0]["out"]
```

```python
from contextlib import ExitStack

import numpy as np
import concourse.bass as bass
from concourse import mybir
from concourse.alu_op_type import AluOpType as ALU

ACT = mybir.ActivationFunctionType
F32 = mybir.dt.float32
U32 = mybir.dt.uint32
AX = mybir.AxisListType.X

P = 128
S = 256
TT = S // P
D = 1024
KT = D // P
HD = 64
PAIRS = 4
EPS = 1e-6
NEG = -1e30
N_CMP, CMP_PAD = 15, 32
N_EXP = 16
GRP, EPG = 4, 4
LAYERS = 2
HG = 8
SWA_PAIRS = 8
LB_FLOOR = 1e-20
LEVELS = 8
RING = 3
PANEL = 4096

PN_Z, PN_GATE, PN_CMP, PN_FOX_UP, PN_NSA_UP, PN_OUT, PN_MOE = 0, 6, 10, 12, 13, 14, 16
PN_L2 = PN_MOE + 3 * N_EXP
L2_PANELS = 17
N_PANELS = PN_L2 + LAYERS * L2_PANELS
Z5 = 288

PRM = {}
_n = 0
for _name, _w in (("g_mix", 8), ("g_ffn", 8), ("fq_g", 1), ("fk_g", 1), ("nq_g", 1), ("nk_g", 1),
                  ("pos_k", 16), ("pos_v", 16), ("b_forget", 8), ("b_route", 20), ("w_route", 160),
                  ("w2_k", 128), ("w2_v", 128), ("lb", 16)):
    PRM[_name] = (_n, _n + _w)
    _n += _w
PRM_W = _n
PL = {"g_pre": (0, 8), "g_head": (8, 136), "sinks": (136, 152)}
PL_IN = 152
PL_W = PL_IN + 3 * 8
ZB = 4352
C1 = {"ntri": (0, 256), "causal": (256, 1024), "alibi": (1024, 4096), "cmp": (4096, 4608), "any": (4608, 4610),
      "first": (4610, 4614), "slot": (4614, 4742)}
C1_W = 4742
C2 = {"band": (0, 768), "cos": (768, 832), "sin": (832, 896), "level": (896, 896 + LEVELS * P)}
C2_W = 896 + LEVELS * P


class Token:

    def __init__(self, sem, scope, off, back=0):
        self.sem, self.scope, self.off, self.back = sem, scope, off, back

    def prev(self):
        return Token(self.sem, self.scope, self.off, 1)


class Later:

    def __init__(self):
        self.token = None


class Scope:
    def __init__(self, parent, n):
        self.parent, self.n, self.flag = parent, n, None
        self.count, self.start, self.items = {}, {}, {}
        self.depth = 0 if parent is None else parent.depth + 1


class Program:

    def __init__(self, nc, ctx):
        self.nc, self.ctx = nc, ctx
        self.engines = {"pe": nc.tensor, "dve": nc.vector, "act": nc.scalar, "pool": nc.gpsimd, "sp": nc.sync}
        self.sems = {e: ctx.enter_context(nc.semaphore("done_" + e)) for e in ("pe", "dve", "act", "pool")}
        self.scope = self.root = Scope(None, 1)

    def count(self, sem, by):
        c = self.scope.count
        c[sem] = c.get(sem, 0) + by
        return Token(sem, self.scope, c[sem])

    def op(self, eng, fn, waits=()):
        token = self.count(eng, 1)
        self.scope.items.setdefault(eng, []).append((fn, list(waits), eng, 1))
        return token

    def dma(self, eng, fn, sem, waits=()):
        if sem not in self.sems:
            self.sems[sem] = self.ctx.enter_context(self.nc.semaphore("dma_" + sem))
        token = self.count(sem, 16)
        self.scope.items.setdefault(eng, []).append((fn, list(waits), sem, 16))
        return token

    def fence(self, eng, waits):
        self.scope.items.setdefault(eng, []).append((None, list(waits), None, 0))

    def begin_loop(self, n):
        s = Scope(self.scope, n)
        s.start = None
        for e in ("pe", "dve", "act", "pool", "sp"):
            self.scope.items.setdefault(e, []).append(s)
        s.start = dict(self.scope.count)
        self.scope = s
        return s

    def end_loop(self):
        s = self.scope
        self.scope = s.parent
        for sem, c in s.count.items():
            self.scope.count[sem] = self.scope.count.get(sem, 0) + s.n * c

    def begin_if(self, flag, waits):
        s = self.begin_loop(1)
        s.flag, s.flag_waits = flag, list(waits)
        return s

    end_if = end_loop

    def value(self, t, here, regs):
        around = []
        s = here
        while s is not None:
            around.append(s)
            s = s.parent
        val = t.off
        if t.back:
            val = val - t.scope.count[t.sem]
        s = t.scope
        terms = []
        while s.parent is not None:
            val += s.start.get(t.sem, 0)
            per = s.count.get(t.sem, 0)
            if s in around:
                terms.append((s.depth - 1, per))
            else:
                val += (s.n - 1) * per
            s = s.parent
        key = (t.sem, tuple(terms))
        low = val
        expr = val
        for d, per in terms:
            if per:
                expr = regs[d] * per + expr
        assert low > 0, ("a wait on a value that may not be positive", t.sem, low)
        return key, val, expr

    def emit(self, eng, scope=None, regs=(), known=None):
        scope = scope or self.root
        e = self.engines[eng]
        known = {} if known is None else known
        for item in scope.items.get(eng, []):
            if isinstance(item, Scope):
                if item.flag is not None and self.uses(item, eng):
                    self.emit_if(eng, item, known)
                elif self.uses(item, eng):
                    with e.Fori(0, item.n) as i:
                        self.emit(eng, item, regs + (i,), {})
                continue
            fn, waits, sem, by = item
            need = {}
            for t in waits:
                if isinstance(t, Later):
                    t = t.token
                if t is None:
                    continue
                key, val, expr = self.value(t, scope, regs)
                if known.get(key, 0) < val and (key not in need or need[key][0] < val):
                    need[key] = (val, expr)
            for key, (val, expr) in need.items():
                e.wait_ge(self.sems[key[0]], expr)
                known[key] = val
            if fn is not None:
                fn(*regs).then_inc(self.sems[sem], by)

    def emit_if(self, eng, item, known):
        e = self.engines[eng]
        for t in item.flag_waits:
            e.wait_ge(self.sems[t.sem], self.value(t, self.root, ())[1])
        own = [sem for sem, by in item.count.items() if by and (sem == eng or (eng == "sp" and sem.startswith("slot")))]
        for sem in own:
            if item.start.get(sem, 0):
                e.wait_ge(self.sems[sem], item.start[sem])
        flag = e.value_load(item.flag, min_val=0, max_val=S)
        with e.If(flag > 0):
            self.emit(eng, item, (0,), dict(known))
        with e.Else():
            for sem in own:
                e.sem_inc(self.sems[sem], item.count[sem])

    def uses(self, scope, eng):
        return any(self.uses(x, eng) if isinstance(x, Scope) else True for x in scope.items.get(eng, []))


def build(nc, panels, x_in, prm_in, lay_in, post_in, c0_in, c1_in, c2_in, out):
    ctx = ExitStack()
    with ctx:
        def sb(name, cols, dt=F32, parts=P):
            return ctx.enter_context(nc.sbuf_tensor(name, [parts, cols], dt))

        p = Program(nc, ctx)
        V, A, T, G = nc.vector, nc.scalar, nc.tensor, nc.gpsimd

        ring = sb("ring", RING * PANEL)
        x_tok = sb("x_tok", TT * D)
        hT = sb("hT", KT * S)
        ident = sb("ident", P)
        prm = sb("prm", PRM_W)
        cst = sb("cst", max(C1_W, C2_W))
        zin = sb("zin", TT * ZB)
        gates = sb("gates", 16 * S)
        buf_a = sb("buf_a", 1024)
        buf_b = sb("buf_b", 1024)
        keys = sb("keys", 3072)
        buf_c = sb("buf_c", 2048)
        buf_d = sb("buf_d", 2048)
        s_buf = sb("s_buf", 2 * 768)
        pt_buf = sb("pt_buf", 2 * 768)
        scr = sb("scr", 2048)
        stat = sb("stat", 1024)
        s_extra = sb("s_extra", 1024)
        ps = ctx.enter_context(nc.psum_tensor("ps", [P, 8, 512], F32))

        def bank(b, n=1):
            return ps[:, b, :] if n == 1 else ps[:, b:b + n, :].rearrange("p a b -> p (a b)")

        free = {b: [] for b in range(8)}

        def bank_waits(*bs):
            return [t for b in bs for t in free[b]]

        def tt(out_, a, b, op, waits=(), eng="dve"):
            f = V if eng == "dve" else G
            return p.op(eng, lambda *i: f.tensor_tensor(out_, a, b, op), waits)

        def ts(out_, a, s1, s2, op0, op1, waits=(), eng="dve"):
            f = V if eng == "dve" else G
            if s2 is None:
                return p.op(eng, lambda *i: f.tensor_scalar(out_, a, s1, None, op0), waits)
            return p.op(eng, lambda *i: f.tensor_scalar(out_, a, s1, s2, op0, op1), waits)

        def stt(out_, a, s1, b, op0, op1, waits=()):
            return p.op("dve", lambda *i: V.scalar_tensor_tensor(out_, a, s1, b, op0, op1), waits)

        def red(out_, a, op, waits=()):
            return p.op("dve", lambda *i: V.tensor_reduce(out_, a, AX, op), waits)

        def copy(out_, a, waits=(), eng="dve"):
            if eng == "act":
                return p.op("act", lambda *i: A.activation(out_, a, ACT.Copy), waits)
            f = V if eng == "dve" else G
            return p.op(eng, lambda *i: f.tensor_copy(out_, a), waits)

        def act(out_, a, func, waits=(), **kw):
            return p.op("act", lambda *i: A.activation(out_, a, func, **kw), waits)

        def memz(ap, waits=(), eng="pool"):
            f = V if eng == "dve" else G
            return p.op(eng, lambda *i: f.memset(ap, 0.0), waits)

        def mms(triples, waits=()):
            def run(*i):
                for o, l, r, s0, s1 in triples:
                    last = T.matmul(o, l, r, start=s0, stop=s1)
                return last
            return p.op("pe", run, waits)

        def transposes(pairs, waits=()):
            def run(*i):
                for o, a, n in pairs:
                    last = T.transpose(o, a, ident[0:n, 0:n])
                return last
            return p.op("pe", run, waits)

        def bc(ap, n):
            return ap.unsqueeze(len(ap.shape)).to_broadcast(list(ap.shape) + [n])

        def prmc(name, a=0, b=None):
            lo, hi = PRM[name]
            return prm[:, lo + a:(hi if b is None else lo + b)]

        slot_ap = [ring[:, s * PANEL:(s + 1) * PANEL] for s in range(RING)]
        slot_free = [[] for _ in range(RING)]
        pos = [0]

        def load_panel(index):
            s = pos[0] % RING
            pos[0] += 1
            dst = slot_ap[s]
            t = p.dma("sp", lambda *i: nc.sync.dma_start(
                dst, panels[index(*i)] if callable(index) else panels[index]), f"slot{s}", slot_free[s])
            return dst, t, s

        def k512(ap):
            return ap.rearrange("p (k n) -> p k n", k=8)

        def k1024(ap):
            return ap.rearrange("p (k n) -> p k n", k=4)

        def fm(ap, k):
            return ap.rearrange("p (k t) -> p k t", k=k)

        def tm(ap):
            return ap.rearrange("p (a n) -> p a n", a=TT)

        hT3 = fm(hT[:, :], KT)
        x3 = tm(x_tok[:, :])

        between = []

        def fill():
            for g in list(between):
                if next(g, "end") == "end":
                    between.remove(g)

        def fill_all():
            while between:
                fill()

        def proj_token(panel, n, waits, evac):
            w, ready, s = panel
            toks = []
            for a in range(TT):
                t = mms([(ps[:, a, 0:n], hT3[:, k, a * P:(a + 1) * P], k512(w)[:, k, 0:n], k == 0, k == KT - 1)
                         for k in range(KT)], [ready, *waits, *bank_waits(a)])
                free[a] = evac(a, ps[:, a, 0:n], t)
                toks.append(t)
                slot_free[s] = [t]
                fill()
            return toks

        def proj_feature(panel, waits, evac):
            w, ready, s = panel
            for b in range(2):
                t = mms([(ps[:, b, f * S:(f + 1) * S], k512(w)[:, k, (2 * b + f) * P:(2 * b + f + 1) * P],
                          hT3[:, k, :], k == 0, k == KT - 1) for f in range(2) for k in range(KT)],
                        [ready, *waits, *bank_waits(b)])
                free[b] = evac(b, ps[:, b, :], t)
                slot_free[s] = [t]
                fill()
            return t

        def rstd(out_, ss, n, waits):
            t = ts(out_, ss, 1.0 / n, EPS, ALU.mult, ALU.add, waits)
            e = minus_half[0:out_.shape[0], :]
            for _ in out_.shape[2:]:
                e = e.unsqueeze(2)
            e = e.to_broadcast(list(out_.shape))
            return p.op("pool", lambda *i: G.tensor_tensor(out_, out_, e, ALU.pow), [t, t_mh])

        def norm_transpose(src_tokens, gain, dst_waits):
            ss, rs = stat[:, 0:2], stat[:, 2:4]
            t1 = [act(scr[:, a * D:(a + 1) * D], x3[:, a, :], ACT.Square, [*src_tokens, *dst_waits],
                      accum_out=ss[:, a:a + 1]) for a in range(TT)]
            t2 = rstd(rs, ss, D, t1)
            t3 = [ts(scr[:, a * D:(a + 1) * D], x3[:, a, :], rs[:, a:a + 1], None, ALU.mult, None, [t2, t1[a]])
                  for a in range(TT)]
            outs = []
            for b in range(4):
                q = 4 + b
                t = transposes([(ps[:, q, f * S + a * P:f * S + (a + 1) * P],
                                 scr[:, a * D + (2 * b + f) * P:a * D + (2 * b + f + 1) * P], P)
                                for f in range(2) for a in range(TT)], [*t3, *bank_waits(q)])
                t = tt(hT3[:, 2 * b:2 * b + 2, :], ps[:, q, :].rearrange("p (f t) -> p f t", f=2),
                       bc(gain[:, 2 * b:2 * b + 2], S), ALU.mult, [t, *dst_waits])
                free[q] = [t]
                outs.append(t)
            return outs

        t_x = p.dma("act", lambda *i: A.dma_start(x3, x_in.rearrange("o (a p) d -> p (o a) d", p=P)), "x")
        t_id = p.dma("act", lambda *i: A.dma_start(ident[:, :], c0_in), "ident")
        t_prm = p.dma("act", lambda *i: A.dma_start(prm[:, :], prm_in), "prm")
        t_c1 = p.dma("act", lambda *i: A.dma_start(cst[:, 0:C1_W], c1_in), "cst")

        lay = sb("lay", LAYERS * PL_W)
        t_lay = [p.dma("act", lambda *i, l=l: A.dma_start(lay[:, l * PL_W:l * PL_W + PL_IN], lay_in[l]), "lay")
                 for l in range(LAYERS)]

        minus_half = sb("minus_half", 1)
        t_mh = p.op("pool", lambda *i: G.memset(minus_half[:, :], -0.5))

        def c1(name):
            return cst[:, C1[name][0]:C1[name][1]]

        def c2(name):
            return cst[:, C2[name][0]:C2[name][1]]

        fox_k = keys[:, 0:2048]
        slc_k = keys[:, 2048:2560]
        win_k = keys[:, 2560:3072]
        t_zk = memz(keys[:, :])

        p.fence("pe", [t_id])
        p.fence("dve", [t_prm])
        t_h = norm_transpose([t_x], prmc("g_mix"), [])

        z3 = zin[:, 0:TT * 2848].rearrange("p (a n) -> p a n", a=TT)
        ZFQ, ZFK, ZFV, ZNQ, ZKC, ZVC, ZKS, ZVS, ZKW, ZVW, ZFF, ZNG = (
            0, 512, 1024, 1536, 2048, 2176, 2304, 2432, 2560, 2688, 2816, 2824)
        done_z = {}

        def z_panel(n, at_):
            cols = 512 if n < 5 else Z5

            def to_z(a, src, t, n=n, cols=cols):
                e = copy(z3[:, a, n * 512:n * 512 + cols], src, [t], "act" if a == 0 else "dve")
                done_z.setdefault(n, []).append(e)
                return [e]
            proj_token(load_panel(at_), cols, t_h, to_z)

        def head_norm(view, heads, waits):
            n = TT * heads
            sq = scr[:, 0:n * HD].rearrange("p (a h d) -> p a h d", a=TT, h=heads)
            ss = stat[:, 32:32 + n].rearrange("p (a h) -> p a h", a=TT)
            t = tt(sq, view, view, ALU.mult, waits)
            t = red(ss, sq, ALU.add, [t])
            t = rstd(ss, ss, HD, [t])
            return tt(view, view, bc(ss, HD), ALU.mult, [t])

        def heads(col, n):
            return z3[:, :, col:col + n * HD].rearrange("p a (h d) -> p a h d", h=n)

        def transpose_pair(dst, src, b, waits):
            pass

        def q_side(col, buf, gain, b, waits):
            outs = []
            for i in range(2):
                t1 = transposes([(ps[:, b + i, f * S + a * P:f * S + (a + 1) * P],
                                  z3[:, a, col + (2 * i + f) * P:col + (2 * i + f + 1) * P], P)
                                 for f in range(2) for a in range(TT)], [*waits, *bank_waits(b + i)])
                t2 = ts(buf[:, i * 512:(i + 1) * 512], ps[:, b + i, :], gain, HD ** -0.5, ALU.mult, ALU.mult, [t1])
                free[b + i] = [t2]
                outs.append(t2)
            return outs

        def k_side(dst, col, npair, gain, b, t):
            outs = []
            per = min(npair, 2)
            for i in range((npair + 1) // 2):
                t1 = transposes([(ps[:, b + i, f * S + a * P:f * S + (a + 1) * P],
                                  z3[:, a, col + (2 * i + f) * P:col + (2 * i + f + 1) * P], P)
                                 for f in range(per) for a in range(TT)], [t, *bank_waits(b + i)])
                for e in range(2):
                    rows = slice(e * HD, (e + 1) * HD)
                    d4 = dst[rows, 2 * i * 512:(2 * i + per) * 512].rearrange("p (f e t) -> p f e t", f=per, e=2)
                    t2 = ts(d4[:, :, e, :], ps[rows, b + i, 0:per * S].rearrange("p (f t) -> p f t", f=per),
                            gain[rows, :], None, ALU.mult, None, [t1, t_zk])
                    outs.append(t2)
                free[b + i] = [t2]
            return outs

        lfb = buf_d[:, :]
        ntri = c1("ntri")
        cq = stat[:, 112:128].rearrange("p (a h) -> p a h", a=TT)
        o_tok = {}
        job_no = [0]

        def scores(q, k, waits, bias, forget=None, sink=None):
            j = job_no[0] % 2
            job_no[0] += 1
            job = {"j": j}
            k2 = k.rearrange("p (e t) -> p e t", e=2)
            last1 = forget is None
            m = [(ps[:, 2, :], q(1), k, True, last1)]
            if forget:
                for e in range(2):
                    l0, l1 = (lfb[:, (a * 8 + forget[0] + e) * P:(a * 8 + forget[0] + e + 1) * P] for a in range(2))
                    m += [(ps[:, 2, e * S:(e + 1) * S], l0, ntri, False, False),
                          (ps[:, 2, e * S + P:(e + 1) * S], l1, ntri[:, 0:P], False, e == 1)]
            m += [(ps[:, 3, 0:S].rearrange("p (e t) -> p e t", e=2), q(0), k2[:, :, 0:P], True, last1)]
            if forget:
                for e in range(2):
                    l0 = lfb[:, (forget[0] + e) * P:(forget[0] + e + 1) * P]
                    m += [(ps[:, 3, e * P:(e + 1) * P], l0, ntri[:, 0:P], False, e == 1)]
            t = mms(m, [*waits, *bank_waits(2, 3)])
            sc = s_buf[:, j * 768:(j + 1) * 768]
            old = s_users[j]
            if forget:
                ts_ = []
                for a, lo, n in ((1, 0, S), (0, 512, P)):
                    for e in range(2):
                        r = slice(lo + e * n, lo + (e + 1) * n)
                        ts_.append(stt(sc[:, r], bank(2, 2)[:, r], cq[:, a, forget[0] + e:forget[0] + e + 1],
                                       bias[:, r], ALU.add, ALU.add, [t, fox["cum"], *old]))
            else:
                ts_ = [tt(sc, bank(2, 2)[:, 0:768], bias, ALU.add, [t, *old])]
            free[2] = free[3] = [ts_[-1]]
            b0 = 192 + 32 * j
            mx, ng_, sm, ex = (stat[:, b0 + 4 * i:b0 + 4 * i + 4] for i in range(4))
            rec = stat[:, b0 + 16 + 4 * 0:b0 + 20]
            m1 = red(mx[:, 2:4], sc[:, 0:512].rearrange("p (e t) -> p e t", e=2), ALU.max, ts_)
            m0 = red(mx[:, 0:2], sc[:, 512:768].rearrange("p (e t) -> p e t", e=2), ALU.max, ts_)
            if sink is not None:
                mx2 = mx.rearrange("p (a e) -> p a e", a=2)
                sk = sink.unsqueeze(1).to_broadcast([P, 2, 2])
                m0 = tt(mx2, mx2, sk, ALU.max, [m0, m1])
                x1 = tt(ex.rearrange("p (a e) -> p a e", a=2), sk, mx2, ALU.subtract, [m0])
            t = ts(ng_, mx, -1.0, None, ALU.mult, None, [m0, m1])
            last = []
            for c, lo, n in ((2, 0, S), (3, S, S), (0, 512, P), (1, 640, P)):
                last.append(act(sc[:, lo:lo + n], sc[:, lo:lo + n], ACT.Exp, [t], bias=ng_[:, c:c + 1],
                                accum_out=sm[:, c:c + 1]))
            w = [*last]
            if sink is not None:
                x2 = act(ex, ex, ACT.Exp, [x1])
                w = [tt(sm, sm, ex, ALU.add, [x2, *last])]
            job["rec"] = p.op("dve", lambda *i: V.reciprocal(rec, sm), w)
            job["rec_ap"] = rec
            job["probs"] = last
            return job

        s_users, pt_users = [[], []], [[], []]
        o_free = {6: [], 7: []}

        def turn(job):
            j = job["j"]
            sc = s_buf[:, j * 768:(j + 1) * 768]
            t = transposes([(bank(4, 2)[:, i * P:(i + 1) * P], sc[:, i * P:(i + 1) * P], P) for i in range(6)],
                           [*job["probs"], *bank_waits(4, 5)])
            s_users[j] = [t]
            e = act(pt_buf[:, j * 768:(j + 1) * 768], bank(4, 2)[:, 0:768], ACT.Copy, [t, *pt_users[j]])
            free[4] = free[5] = [e]
            job["pt"] = e

        def values(job, v, waits, evac):
            j = job["j"]
            b = 6
            pt = pt_buf[:, j * 768:(j + 1) * 768]
            o = ps[:, b, 0:256].rearrange("p (a e d) -> p a e d", a=TT, e=2)
            m = []
            for e in range(2):
                m.append((o[:, 0, e, :], pt[:, 512 + e * P:512 + (e + 1) * P], v(0, e), True, True))
                for kt in range(2):
                    m.append((o[:, 1, e, :], pt[:, e * S + kt * P:e * S + (kt + 1) * P], v(kt, e), kt == 0, kt == 1))
            t = mms(m, [job["pt"], *waits, *bank_waits(b)])
            pt_users[j] = [t]
            free[b] = evac(o, job["rec_ap"].rearrange("p (a e) -> p a e", a=2), [t, job["rec"]])

        t_fox = []
        fox = {}

        def fox_evac(pr):
            def evac(o, rec, w):
                e = tt(z3[:, :, ZFQ + pr * P:ZFQ + (pr + 1) * P].rearrange("p a (e d) -> p a e d", e=2), o,
                       bc(rec, HD), ALU.mult, w)
                t_fox.append(e)
                return [e]
            return evac

        jobs = []
        for pr in range(PAIRS):
            jobs.append((
                lambda pr=pr: scores(lambda a: buf_a[:, pr * S + a * P:pr * S + (a + 1) * P],
                                     fox_k[:, pr * 512:(pr + 1) * 512], fox["sides"], c1("causal"),
                                     forget=(2 * pr,)),
                lambda job, pr=pr: values(job, lambda kt, e: z3[:, kt, ZFV + (2 * pr + e) * HD:
                                                                ZFV + (2 * pr + e + 1) * HD],
                                          done_z[2], fox_evac(pr))))

        nsa = {"first": [], "last": []}

        def nsa_dst(r):
            return z3[:, :, ZNQ + r * P:ZNQ + (r + 1) * P].rearrange("p a (e d) -> p a e d", e=2)

        def nsa_evac(r, branch):
            def evac(o, rec, w):
                f = stat[:, 256 + 8 * branch:260 + 8 * branch].rearrange("p (a e) -> p a e", a=2)
                tmp = s_extra[:, 0:256].rearrange("p (a e d) -> p a e d", a=2, e=2)
                e1 = tt(f, rec, nsa["gates"][:, :, branch, 2 * r:2 * r + 2], ALU.mult, [*w, nsa["t_gates"]])
                if branch == 1:
                    e2 = tt(nsa_dst(r), o, bc(f, HD), ALU.mult, [e1])
                    nsa["first"].append(e2)
                else:
                    e2 = tt(tmp, o, bc(f, HD), ALU.mult, [e1, *nsa["last"][-1:]])
                    nsa["last"].append(tt(nsa_dst(r), nsa_dst(r), tmp, ALU.add, [e2, *nsa["first"]]))
                return [e2]
            return evac

        for branch, kk, zv in ((1, slc_k, ZVS), (2, win_k, ZVW)):
            for r in range(PAIRS):
                jobs.append((
                    lambda r=r, kk=kk: scores(lambda a: buf_b[:, r * S + a * P:r * S + (a + 1) * P], kk,
                                                     nsa["sides"], c1("alibi")[:, r * 768:(r + 1) * 768]),
                    lambda job, r=r, zv=zv, branch=branch: values(
                        job, lambda kt, e: z3[:, kt, zv + e * HD:zv + (e + 1) * HD],
                        [*done_z[4], *done_z[5]], nsa_evac(r, branch))))

        def pipeline(jobs):
            live = {}
            for i in range(len(jobs) + 2):
                if i >= 2:
                    jobs[i - 2][1](live[i - 2])
                if 1 <= i <= len(jobs):
                    turn(live[i - 1])
                if i < len(jobs):
                    live[i] = jobs[i][0]()
                yield

        kv2 = buf_c[:, 0:1024].rearrange("p (c g t) -> p c g t", c=2, g=2)
        blk = [buf_d[:, c * 1024:(c + 1) * 1024].rearrange("p (m g n) -> p m g n", m=16, g=2) for c in range(2)]
        kc_bd = buf_c[:, 1024:1088]
        vc_bd = buf_c[0:64, 1088:1216]
        tmp_n = s_extra[:, :]

        def compression():
            t_blk0 = memz(buf_d[:, :], t_fox)
            t_z = memz(buf_c[:, 1024:1216])
            cp = []
            for c in range(2):
                zc = (ZKC, ZVC)[c]
                t = transposes([(ps[:, 7, a * P:(a + 1) * P], z3[:, a, zc:zc + P], P) for a in range(TT)],
                               [*done_z[4], *bank_waits(7)])
                for g in range(2):
                    for jp in range(2):
                        cp.append(copy(kv2[jp * HD:(jp + 1) * HD, c, g, 0:S - jp],
                                       ps[g * HD:(g + 1) * HD, 7, jp:S], [t]))
                free[7] = [cp[-1]]
                yield
            bt = {0: [], 1: []}
            for c in range(2):
                pos_ap = prmc(("pos_k", "pos_v")[c])
                for g in range(2):
                    even = kv2[:, c, g, :].rearrange("p (n m j) -> p m n j", n=16, j=2)[:, :, :, 0]
                    bt[c].append(tt(blk[c][:, 0:8, g, 0:N_CMP], even[:, :, 0:N_CMP], bc(pos_ap[:, 0:8], N_CMP),
                                    ALU.add, [*cp, t_blk0]))
                    bt[c].append(tt(blk[c][:, 8:16, g, 0:N_CMP], even[:, :, 1:N_CMP + 1],
                                    bc(pos_ap[:, 8:16], N_CMP), ALU.add, [*cp, t_blk0]))
            yield
            hid = scr[0:64, 0:512]
            hidT_c = scr[:, 512:768]
            t_hid = []
            for c in range(2):
                w, ready, s = load_panel(PN_CMP + c)
                w1 = w.rearrange("p (m n) -> p m n", m=16)
                t = mms([(ps[0:64, 7, 0:256], blk[c][:, m, :, :].rearrange("p g n -> p (g n)"), w1[:, m, :],
                          m == 0, m == 15) for m in range(16)], [ready, *bt[c], *bank_waits(7)])
                slot_free[s] = [t]
                t = act(hid[:, c * 256:(c + 1) * 256], ps[0:64, 7, 0:256], ACT.Gelu_apprx_tanh, [t, *nsa["sides"]])
                free[7] = [t]
                t_hid.append(t)
                yield
            t = transposes([(ps[:, 7, i * 64:(i + 1) * 64], hid[:, i * P:(i + 1) * P], 64) for i in range(4)],
                           [*t_hid, *bank_waits(7)])
            t = copy(hidT_c, ps[:, 7, 0:256], [t])
            free[7] = [t]
            yield
            m = []
            for c in range(2):
                w2 = prmc(("w2_k", "w2_v")[c])
                m += [(ps[0:64, 7, c * 64:(c + 1) * 64], hidT_c[:, (2 * c + i) * 64:(2 * c + i + 1) * 64],
                       w2[:, i * 64:(i + 1) * 64], i == 0, i == 1) for i in range(2)]
            t = mms(m, [t, *bank_waits(7)])
            t_vc = [copy(vc_bd[g * 32:(g + 1) * 32, g * HD:(g + 1) * HD], ps[g * 32:(g + 1) * 32, 7, 64:128],
                         [t, t_z]) for g in range(2)]
            kcn, sq, ss = scr[0:64, 768:832], scr[0:64, 832:896], stat[0:64, 288:289]
            t = copy(kcn, ps[0:64, 7, 0:64], [t])
            free[7] = [t]
            t1 = tt(sq, kcn, kcn, ALU.mult, [t])
            t1 = red(ss, sq, ALU.add, [t1])
            t1 = rstd(ss, ss, HD, [t1])
            t1 = ts(kcn, kcn, ss, None, ALU.mult, None, [t1])
            yield
            t1 = transposes([(ps[0:64, 7, 0:64], kcn, 64)], [t1, *bank_waits(7)])
            t_kc = [ts(kc_bd[g * HD:(g + 1) * HD, g * 32:(g + 1) * 32], ps[0:64, 7, g * 32:(g + 1) * 32],
                       prmc("nk_g")[0:64, :], None, ALU.mult, None, [t1, t_z]) for g in range(2)]
            free[7] = [t_kc[-1]]
            yield
            t = mms([(ps[:, 7, (a * 4 + r) * 64:(a * 4 + r + 1) * 64], buf_b[:, r * S + a * P:r * S + (a + 1) * P],
                      kc_bd, True, True) for a in range(TT) for r in range(PAIRS)], [*t_kc, *bank_waits(7)])
            sc = scr[:, 1024:1536]
            t = tt(sc, ps[:, 7, :], c1("cmp"), ALU.add, [t])
            free[7] = [t]
            sc3 = sc.rearrange("p (h n) -> p h n", n=CMP_PAD)
            mx, sm, fc = stat[:, 320:336], stat[:, 336:352], stat[:, 352:368]
            t = red(mx, sc3, ALU.max, [t])
            t = tt(sc3, sc3, bc(mx, CMP_PAD), ALU.subtract, [t])
            t_pc = act(sc, sc, ACT.Exp, [t])
            t = red(sm, sc3, ALU.add, [t_pc])
            t = p.op("dve", lambda *i: V.reciprocal(sm, sm), [t])
            fc3 = fc.rearrange("p (a h) -> p a h", a=TT)
            t = tt(fc3, sm.rearrange("p (a h) -> p a h", a=TT), nsa["gates"][:, :, 0, :], ALU.mult, [t, nsa["t_gates"]])
            t_fc = tt(fc3, fc3, bc(c1("any"), 8), ALU.mult, [t])
            yield
            pct = scr[0:64, 0:1024]
            t_p = []
            for a in range(TT):
                t = transposes([(ps[0:64, 7, r * P:(r + 1) * P], sc[:, (a * 4 + r) * 64:(a * 4 + r + 1) * 64], P)
                                for r in range(PAIRS)], [t_pc, *bank_waits(7)])
                t = act(pct[:, a * 512:(a + 1) * 512], ps[0:64, 7, :], ACT.Copy, [t, t_fc])
                free[7] = [t]
                t_p.append(t)
                yield
            for a in range(TT):
                t = mms([(ps[:, 7, r * P:(r + 1) * P], pct[:, (a * 4 + r) * P:(a * 4 + r + 1) * P], vc_bd, True, True)
                         for r in range(PAIRS)], [*t_p, *t_vc, *bank_waits(7)])
                e = tt(tmp_n[:, 512:1024].rearrange("p (h d) -> p h d", h=8),
                       ps[:, 7, :].rearrange("p (h d) -> p h d", h=8), bc(fc3[:, a, :], HD), ALU.mult,
                       [t, t_fc, *nsa["last"][-1:]])
                free[7] = [e]
                dst = z3[:, a, ZNQ:ZNQ + 512]
                e = tt(dst, dst, tmp_n[:, 512:1024], ALU.add, [e, *nsa["first"]])
                nsa["last"].append(e)
                yield

        def fox_sides():
            tq = head_norm(heads(ZFQ, 8), 8, done_z[0])
            tk = head_norm(heads(ZFK, 8), 8, done_z[1])
            yield
            t_fq = q_side(ZFQ, buf_a, prmc("fq_g"), 2, [tq])
            lf = stat[:, 64:80].rearrange("p (a h) -> p a h", a=TT)
            lx = stat[:, 80:96].rearrange("p (a h) -> p a h", a=TT)
            la = stat[:, 96:112].rearrange("p (a h) -> p a h", a=TT)
            t = tt(lx, z3[:, :, ZFF:ZFF + 8], prmc("b_forget").unsqueeze(1).to_broadcast([P, TT, 8]), ALU.add, done_z[5])
            t = ts(la, lx, -1.0, None, ALU.mult, None, [t])
            t = tt(la, la, lx, ALU.min, [t])
            t = act(la, la, ACT.Exp, [t])
            t = act(la, la, ACT.Ln, [t], bias=1.0)
            t1 = ts(lx, lx, 0.0, None, ALU.min, None, [t])
            t_lf = tt(lf, lx, la, ALU.subtract, [t1, t])
            t_lfb = copy(lfb.rearrange("p (a h q) -> p a h q", a=TT, h=8), bc(lf, P), [t_lf], "pool")
            lf2 = stat[:, 64:80]
            p.fence("pe", [t_c1])
            p.fence("dve", [t_c1])
            t = mms([(ps[:, 6, 0:8], ntri[:, 0:P], lf2[:, 0:8], True, True),
                     (ps[:, 6, 8:16], ntri[:, P:2 * P], lf2[:, 0:8], True, False),
                     (ps[:, 6, 8:16], ntri[:, 0:P], lf2[:, 8:16], False, True)], [t_lf, *bank_waits(6)])
            t_cq = ts(stat[:, 112:128], ps[:, 6, 0:16], -1.0, None, ALU.mult, None, [t])
            free[6] = [t_cq]
            fox["cum"] = t_cq
            yield
            t_fk = k_side(fox_k, ZFK, 4, prmc("fk_g"), 4, tk)
            fox["sides"] = [*t_fq, *t_fk, t_lfb]
            yield

        def nsa_sides():
            ng = nsa["gates"] = stat[:, 128:176].rearrange("p (a c h) -> p a c h", a=TT, c=3)
            nsa["t_gates"] = act(ng, z3[:, :, ZNG:ZNG + 24].rearrange("p a (c h) -> p a c h", c=3), ACT.Sigmoid,
                                 done_z[5])
            tq = head_norm(heads(ZNQ, 8), 8, done_z[3])
            ts_ = head_norm(heads(ZKS, 2), 2, done_z[4])
            tw = head_norm(heads(ZKW, 2), 2, done_z[5])
            yield
            nsa["sides"] = (q_side(ZNQ, buf_b, prmc("nq_g"), 0, [tq]) + k_side(slc_k, ZKS, 1, prmc("nk_g"), 7, ts_)
                            + k_side(win_k, ZKW, 1, prmc("nk_g"), 7, tw))
            yield

        def block1_between():
            yield from fox_sides()
            yield from pipeline(jobs[:PAIRS])
            between.append(compression())
            yield from pipeline(jobs[PAIRS:])

        z_panel(0, 0)
        z_panel(1, 1)
        z_panel(5, 2)
        between.append(block1_between())
        z_panel(2, 3)
        z_panel(3, 4)
        z_panel(4, 5)
        between.append(nsa_sides())
        g3 = fm(gates[:, :], 16)
        t_gate = {}
        for n in range(4):
            def to_gate(b, src, t, n=n):
                e = act(gates[:, (4 * n + 2 * b) * S:(4 * n + 2 * b + 2) * S], src, ACT.Sigmoid, [t])
                t_gate.setdefault(n // 2, []).append(e)
                return [e]
            proj_feature(load_panel(PN_GATE + n), [], to_gate)


        def turn_512(dst, col, waits, b):
            outs = []
            for i in range(2):
                t1 = transposes([(ps[:, b + i, f * S + a * P:f * S + (a + 1) * P],
                                  z3[:, a, col + (2 * i + f) * P:col + (2 * i + f + 1) * P], P)
                                 for f in range(2) for a in range(TT)], [*waits, *bank_waits(b + i)])
                t2 = copy(dst[:, i * 512:(i + 1) * 512], ps[:, b + i, :], [t1], "act" if i else "dve")
                free[b + i] = [t2]
                outs.append(t2)
            return outs

        def up(panel, src, waits, which):
            w, ready, s = panel
            outs = []
            for i in range(4):
                b = i % 2
                t = mms([(ps[:, b, f * S:(f + 1) * S], k1024(w)[:, k, (2 * i + f) * P:(2 * i + f + 1) * P],
                          src[:, k * S:(k + 1) * S], k == 0, k == 3) for f in range(2) for k in range(4)],
                        [ready, *waits, *bank_waits(b)])
                m0 = hT[:, 2 * i * S:(2 * i + 2) * S]
                g0 = gates[:, (8 * which + 2 * i) * S:(8 * which + 2 * i + 2) * S]
                tmp = s_extra[:, (i % 2) * 512:(i % 2) * 512 + 512] if which else m0
                e = tt(tmp, ps[:, b, :], g0, ALU.mult, [t, *t_gate[which], *outs[-2:-1]])
                free[b] = [e]
                if which:
                    e = tt(m0, m0, tmp, ALU.add, [e])
                outs.append(e)
                slot_free[s] = [t]
                fill()
            return outs

        while len(t_fox) < PAIRS:
            fill()
        up(load_panel(PN_FOX_UP), buf_a, turn_512(buf_a, ZFQ, t_fox, 0), 0)
        fill_all()
        t_mix = up(load_panel(PN_NSA_UP), buf_b, turn_512(buf_b, ZNQ, nsa["last"], 0), 1)

        def down(panels_, lhs, waits, b0, nk):
            for n, load in enumerate(panels_):
                w, ready, s = load()
                t = mms([(ps[:, b0 + 2 * a + h, :], lhs(4 * n + k, a), k1024(w)[:, k, h * 512:(h + 1) * 512],
                          n == 0 and k == 0, n == len(panels_) - 1 and k == 3)
                         for k in range(4) for a in range(TT) for h in range(2)],
                        [ready, *waits, *(bank_waits(*range(b0, b0 + 4)) if n == 0 else [])])
                slot_free[s] = [t]
            return t

        t = down([lambda: load_panel(PN_OUT), lambda: load_panel(PN_OUT + 1)], lambda k, a: hT3[:, k, a * P:(a + 1) * P], t_mix, 4, 8)
        t_x1 = []
        for b in range(4):
            xs = x_tok[:, b * 512:(b + 1) * 512]
            e = tt(xs, xs, ps[:, 4 + b, :], ALU.add, [t])
            free[4 + b] = [e]
            t_x1.append(e)

        t_h = norm_transpose(t_x1, prmc("g_ffn"), [])
        wr = prmc("w_route").rearrange("p (k n) -> p k n", k=KT)
        t = mms([(ps[:, 0, a * 20:(a + 1) * 20], hT3[:, k, a * P:(a + 1) * P], wr[:, k, :], k == 0, k == KT - 1)
                 for a in range(TT) for k in range(KT)], [*t_h, *bank_waits(0)])
        at = [384]

        def small(n):
            at[0] += n
            return stat[:, at[0] - n:at[0]]

        lg = small(40).rearrange("p (a n) -> p a n", a=TT)
        t = tt(lg, ps[:, 0, 0:40].rearrange("p (a n) -> p a n", a=TT),
               prmc("b_route").unsqueeze(1).to_broadcast([P, TT, 20]), ALU.add, [t])
        free[0] = [t]

        def softmax4(src, w):
            m, e_, r = small(2), small(8).rearrange("p (a n) -> p a n", a=TT), small(2)
            w = red(m, src, ALU.max, [w])
            w = tt(e_, src, bc(m, 4), ALU.subtract, [w])
            w = act(e_, e_, ACT.Exp, [w])
            w = red(r, e_, ALU.add, [w])
            w = p.op("dve", lambda *i: V.reciprocal(r, r), [w])
            return e_, r, w

        first = c1("first").unsqueeze(1).to_broadcast([P, TT, 4])

        def top1(src, w):
            m, oh, i_ = small(2), small(8).rearrange("p (a n) -> p a n", a=TT), small(2)
            w = red(m, src, ALU.max, [w])
            w = tt(oh, src, bc(m, 4), ALU.is_equal, [w])
            w = tt(oh, oh, first, ALU.mult, [w])
            w = red(i_, oh, ALU.max, [w])
            w = tt(oh, oh, bc(i_, 4), ALU.is_equal, [w])
            return oh, m, w

        ge, gr, tg = softmax4(lg[:, :, 0:4], t)
        goh, gm, tg = top1(ge, tg)
        pg = small(2)
        tg = tt(pg, gm, gr, ALU.mult, [tg])
        sel = small(32).rearrange("p (a g j) -> p a g j", a=TT, g=4)
        e16 = lg[:, :, 4:20].rearrange("p a (g j) -> p a g j", g=4)
        tg = tt(sel, e16, bc(goh, 4), ALU.mult, [tg])
        ein = small(8).rearrange("p (a n) -> p a n", a=TT)
        tg = red(ein, sel.rearrange("p a g j -> p a j g"), ALU.add, [tg])
        pe_, pr_, tg = softmax4(ein, tg)
        pn = small(8).rearrange("p (a n) -> p a n", a=TT)
        tg = tt(pn, pe_, bc(pr_, 4), ALU.mult, [tg])
        oh1, m1, tg = top1(pn, tg)
        pn2 = small(8).rearrange("p (a n) -> p a n", a=TT)
        tg = ts(pn2, oh1, -2.0, None, ALU.mult, None, [tg])
        tg = tt(pn2, pn2, pn, ALU.add, [tg])
        oh2, m2, tg = top1(pn2, tg)
        msum = small(2)
        tg = tt(msum, m1, m2, ALU.add, [tg])
        tg = p.op("dve", lambda *i: V.reciprocal(msum, msum), [tg])
        tg = tt(msum, msum, pg, ALU.mult, [tg])
        tg = tt(oh1, oh1, oh2, ALU.add, [tg])
        tg = tt(oh1, oh1, pn, ALU.mult, [tg])
        tg = tt(oh1, oh1, bc(msum, 4), ALU.mult, [tg])
        goh2 = small(8)
        t_goh = copy(goh2.rearrange("p (a g) -> p a g", a=TT), goh, [tg])
        rank = small(8)
        over = small(4)
        t = mms([(ps[:, 1, 0:4], ntri[:, 0:P], goh2[:, 0:4], True, True),
                 (ps[:, 1, 4:8], ntri[:, P:2 * P], goh2[:, 0:4], True, False),
                 (ps[:, 1, 4:8], ntri[:, 0:P], goh2[:, 4:8], False, True),
                 (ps[:, 1, 8:12], ntri[:, P:2 * P], goh2[:, 0:4], True, False),
                 (ps[:, 1, 8:12], ntri[:, P:2 * P], goh2[:, 4:8], False, True)], [t_goh, *bank_waits(1)])
        t_rank = ts(rank, ps[:, 1, 0:8], -1.0, -1.0, ALU.mult, ALU.add, [t])
        t1 = ts(over, ps[:, 1, 8:12], -1.0, -float(P), ALU.mult, ALU.add, [t])
        free[1] = [t1]
        t1 = ts(over, over, 0.0, None, ALU.max, None, [t1])
        most = small(1)
        t1 = red(most, over, ALU.max, [t1])
        flag = sb("flag", 1, mybir.dt.int32)
        t_flag = copy(flag[:, :], most, [t1])
        comb2 = small(32)
        t_comb2 = [tt(comb2.rearrange("p (a g j) -> p a g j", a=TT, g=4)[:, a, :, :], bc(goh[:, a, :], 4),
                      oh1[:, a, :].unsqueeze(1).to_broadcast([P, 4, 4]), ALU.mult, [tg]) for a in range(TT)]
        assert at[0] <= 768

        sel = buf_a[:, :]
        selT = buf_b[:, :]
        rows_in = gates[:, :]
        rows_out = zin[:, 0:4 * D]
        xg = buf_c[:, 0:1024]
        sg = buf_c[:, 1024:2048]
        hid = buf_d[:, 0:1024]
        hidT = buf_d[:, 1024:2048]
        comb_g = stat[:, 704:768]

        def moe(chunk, waits):
            base = pos[0]
            shifted = stat[:, 1016:1024]
            t = ts(shifted, rank, float(-P * chunk), None, ALU.add, None, [t_rank, *waits])
            t_sel = [ts(sel[:, (a * 4 + g) * P:(a * 4 + g + 1) * P], c1("slot"), shifted[:, a * 4 + g:a * 4 + g + 1],
                        goh2[:, a * 4 + g:a * 4 + g + 1], ALU.is_equal, ALU.mult, [t, t_goh, *waits])
                     for a in range(TT) for g in range(4)]
            t_selT = []
            for i in range(2):
                t = transposes([(ps[:, i, f * S + a * P:f * S + (a + 1) * P],
                                 sel[:, (a * 4 + 2 * i + f) * P:(a * 4 + 2 * i + f + 1) * P], P)
                                for f in range(2) for a in range(TT)], [*t_sel, *bank_waits(i)])
                e = copy(selT[:, i * 512:(i + 1) * 512], ps[:, i, :], [t], "act")
                free[i] = [e]
                t_selT.append(e)
            t = mms([(ps[:, 2, g * 16:(g + 1) * 16], sel[:, (a * 4 + g) * P:(a * 4 + g + 1) * P],
                      comb2[:, a * 16:(a + 1) * 16], a == 0, a == 1) for g in range(4) for a in range(TT)],
                    [*t_sel, *t_comb2, *bank_waits(2)])
            t_cg = copy(comb_g, ps[:, 2, 0:64], [t])
            free[2] = [t_cg]
            t_rows = []
            rin = rows_in.rearrange("p (g k n) -> p k g n", g=4, k=KT)
            for k in range(KT):
                b = 3 + k % 4
                t = mms([(ps[:, b, :], scr[:, a * D + k * P:a * D + (k + 1) * P], sel[:, a * 512:(a + 1) * 512],
                          a == 0, a == 1) for a in range(TT)], [*t_sel, *t_h, *bank_waits(b)])
                src = ps[:, b, :].rearrange("p (g n) -> p g n", g=4)
                if k % 2:
                    e = act(rin[:, k, :, :], src, ACT.Copy, [t], scale=prmc("g_ffn", k, k + 1))
                else:
                    e = ts(rin[:, k, :, :], src, prmc("g_ffn", k, k + 1), None, ALU.mult, None, [t])
                free[b] = [e]
                t_rows.append(e)

            pre = {b: list(free[b]) for b in range(8)}
            slots_pre = [list(x) for x in slot_free]
            carry_bank = [Later() for _ in range(8)]
            carry_slot = [Later() for _ in range(RING)]
            carry_x = Later()
            p.begin_loop(GRP)
            for s in range(RING):
                slot_free[s] = [*slots_pre[s], carry_slot[s]]
            for b in range(8):
                free[b] = [*pre[b], carry_bank[b]]
            t_xg = p.op("pool", lambda *i: G.tensor_copy(xg, rows_in[:, bass.ds(i[-1] * 1024, 1024)]),
                        [*t_rows, carry_x])
            gu = {}
            used_h = [[], []]

            def gate_up(j):
                u = j % 2
                got = []
                for h in range(2):
                    w, ready, s = load_panel(lambda *i, h=h: i[-1] * 12 + (PN_MOE + 3 * j + h))
                    b = 2 * u + h
                    t = mms([(ps[:, b, :], xg[:, k * P:(k + 1) * P], k512(w)[:, k, :], k == 0, k == KT - 1)
                             for k in range(KT)], [ready, t_xg, *bank_waits(b)])
                    slot_free[s] = [t]
                    got.append(t)
                su, hu = sg[:, u * 512:(u + 1) * 512], hid[:, u * 512:(u + 1) * 512]
                e1 = act(su, ps[:, 2 * u, :], ACT.Silu, [got[0]])
                e2 = p.op("dve", lambda *i: V.scalar_tensor_tensor(
                    hu, su, comb_g[:, bass.ds(i[-1] * 20 + j, 1)], ps[:, 2 * u + 1, :], ALU.mult, ALU.mult),
                    [e1, got[1], t_cg, *used_h[u]])
                free[2 * u], free[2 * u + 1] = [e1], [e2]
                gu[j] = (e2, got[1])

            def back(j):
                u = j % 2
                w, ready, s = load_panel(lambda *i: i[-1] * 12 + (PN_MOE + 3 * j + 2))
                hu, tu = hid[:, u * 512:(u + 1) * 512], hidT[:, u * 512:(u + 1) * 512]
                t = transposes([(ps[:, 6, k * P:(k + 1) * P], hu[:, k * P:(k + 1) * P], P) for k in range(4)],
                               [gu[j][0], *bank_waits(6)])
                used_h[u] = [t]
                e = act(tu, ps[:, 6, :], ACT.Copy, [t])
                free[6] = [e]
                t = mms([(ps[:, 4 + h, :], tu[:, k * P:(k + 1) * P], k1024(w)[:, k, h * 512:(h + 1) * 512],
                          j == 0 and k == 0, j == 3 and k == 3) for k in range(4) for h in range(2)],
                        [e, ready, *(bank_waits(4, 5) if j == 0 else [])])
                slot_free[s] = [t]
                return t

            gate_up(0)
            for j in range(EPG):
                if j + 1 < EPG:
                    gate_up(j + 1)
                t = back(j)
            carry_x.token = gu[3][1].prev()
            e4 = p.op("act", lambda *i: A.activation(rows_out[:, bass.ds(i[-1] * D, 512)], ps[:, 4, :], ACT.Copy),
                      [t, *waits])
            e5 = p.op("dve", lambda *i: V.tensor_copy(rows_out[:, bass.ds(i[-1] * D + 512, 512)], ps[:, 5, :]),
                      [t, *waits])
            free[4], free[5] = [e4], [e5]
            for s in range(RING):
                carry_slot[s].token = slot_free[s][0].prev()
            for b in range(7):
                carry_bank[b].token = free[b][0].prev()
            free[7] = pre[7]
            p.end_loop()
            assert (pos[0] - base) % RING == 0

            outs = []
            for a in range(TT):
                for h in range(2):
                    b = 2 * a + h
                    t = mms([(ps[:, b, :], selT[:, g * S + a * P:g * S + (a + 1) * P],
                              rows_out[:, g * D + h * 512:g * D + (h + 1) * 512], g == 0, g == 3)
                             for g in range(4)], [e4, e5, *t_selT, *bank_waits(b)])
                    xs = x_tok[:, b * 512:(b + 1) * 512]
                    e = tt(xs, xs, ps[:, b, :], ALU.add, [t])
                    free[b] = [e]
                    outs.append(e)
            return outs

        t_x2 = moe(0, t_x1)
        keep = pos[0]
        p.begin_if(flag[0:1, 0:1], [t_flag])
        t_x2 = moe(1, t_x2)
        p.end_if()
        pos[0] = keep

        t_c2 = p.dma("act", lambda *i: A.dma_start(cst[:, 0:C2_W], c2_in), "cst", t_x2)
        lbp = prmc("lb").rearrange("p (l h) -> p l h", l=LAYERS)
        e_l, m_l = stat[:, 768:784].rearrange("p (l h) -> p l h", l=LAYERS), stat[:, 784:792]
        t = tt(m_l, lbp[:, 0, :], lbp[:, 1, :], ALU.max)
        t = tt(e_l, lbp, m_l.unsqueeze(1).to_broadcast([P, LAYERS, HG]), ALU.subtract, [t])
        t = act(e_l, e_l, ACT.Exp, [t])
        t = tt(m_l, e_l[:, 0, :], e_l[:, 1, :], ALU.add, [t])
        t = p.op("dve", lambda *i: V.reciprocal(m_l, m_l), [t])
        t = tt(e_l, e_l, m_l.unsqueeze(1).to_broadcast([P, LAYERS, HG]), ALU.mult, [t])
        t = tt(e_l[:, 1, :], e_l[:, 0, :], e_l[:, 1, :], ALU.add, [t])
        t = tt(e_l[:, 1, :], e_l[:, 1, :], e_l[:, 0, :], ALU.subtract, [t])
        t = tt(e_l[:, 0, :], e_l[:, 0, :], e_l[:, 0, :], ALU.subtract, [t])
        lay3 = lay[:, :].rearrange("p (l n) -> p l n", l=LAYERS)
        one_l, fl_l, kf_l = (lay3[:, :, PL_IN + 8 * i:PL_IN + 8 * i + 8] for i in range(3))
        t_l1 = ts(one_l, e_l, -1.0, 1.0, ALU.mult, ALU.add, [t, *t_lay])
        t_l2 = ts(fl_l, e_l, LB_FLOOR, None, ALU.max, None, [t])
        t_l3 = tt(kf_l, e_l, fl_l, ALU.subtract, [t_l2])

        cur = stat[:, 800:800 + PL_W]
        post = keys[:, 1024:2048]
        zb3 = zin[:, :].rearrange("p (a n) -> p a n", a=TT)
        ZI, ZZ, ZQA, ZKA, ZVA, ZZA = 0, 1024, 2048, 3072, 3200, 3328
        level_mask = c2("level").bitcast(U32).rearrange("p (l t) -> p l t", l=LEVELS)

        slots_pre = [list(x) for x in slot_free]
        carry_slot = [Later() for _ in range(RING)]
        carry_x = [Later() for _ in range(4)]
        p.begin_loop(LAYERS)
        pos[0] = 0
        for s in range(RING):
            slot_free[s] = [*slots_pre[s], carry_slot[s]]
        x_old = [*t_x2, *carry_x]
        for b in range(8):
            free[b] = []
        s_users[0], s_users[1], pt_users[0], pt_users[1] = [], [], [], []
        t_cur = p.op("dve", lambda l: V.tensor_copy(cur, lay[:, bass.ds(l * PL_W, PL_W)]),
                     [*x_old, t_l1, t_l2, t_l3])
        t_post = p.dma("act", lambda l: A.dma_start(post, post_in[l].partition_broadcast(P)), "post", x_old)
        t_A0 = memz(buf_c[:, :], x_old, "dve")
        t_h = norm_transpose([*x_old, t_cur], cur[:, 0:8], [])
        nxt_panel = [0]

        def layer_panel():
            n = nxt_panel[0]
            nxt_panel[0] += 1
            return load_panel(lambda l: l * L2_PANELS + (PN_L2 + n))

        def token_panel(col, n, func=None):
            got = []

            def evac(a, src, t):
                dst = zb3[:, a, col:col + n]
                e = act(dst, src, func, [t]) if func is not None else copy(dst, src, [t], "act" if a else "dve")
                got.append(e)
                return [e]
            proj_token(layer_panel(), n, t_h, evac)
            return got

        t_qa = token_panel(ZQA, 512) + token_panel(ZQA + 512, 512)
        t_kva = token_panel(ZKA, 256)

        def rope(col, n, dst, t1, t2, waits):
            half = HD // 2
            v = zb3[:, :, col:col + n * HD].rearrange("p a (h d) -> p a h d", h=n)
            u1, u2 = (x.rearrange("p (a h d) -> p a h d", a=TT, h=n) for x in (t1, t2))
            x1, x2 = v[:, :, :, 0:half], v[:, :, :, half:HD]
            co, si = (c2(x).rearrange("p (a d) -> p a d", a=TT).unsqueeze(2).to_broadcast([P, TT, n, half])
                      for x in ("cos", "sin"))
            a1 = tt(u1, x1, co, ALU.mult, waits)
            a2 = tt(u2, x2, si, ALU.mult, waits)
            b1 = tt(dst[:, :, :, 0:half], u1, u2, ALU.subtract, [a1, a2])
            a1 = tt(u1, x2, co, ALU.mult, [b1])
            a2 = tt(u2, x1, si, ALU.mult, [b1])
            b2 = tt(dst[:, :, :, half:HD], u1, u2, ALU.add, [a1, a2])
            return [b1, b2]

        t_rk = rope(ZKA, 2, pt_buf[:, 1024:1280].rearrange("p (a h d) -> p a h d", a=TT, h=2),
                    s_buf[:, 1024:1152], s_buf[:, 1152:1280], [*t_kva, t_c2])
        t_rq = rope(ZQA, 16, scr[:, :].rearrange("p (a h d) -> p a h d", a=TT, h=16),
                    s_buf[:, 0:1024], pt_buf[:, 0:1024], [*t_qa, t_c2])

        swa = {"out": []}

        def swa_evac(r):
            def evac(o, rec, w):
                e = tt(zb3[:, :, ZQA + r * P:ZQA + (r + 1) * P].rearrange("p a (e d) -> p a e d", e=2), o,
                       bc(rec, HD), ALU.mult, w)
                swa["out"].append(e)
                return [e]
            return evac

        def sliding():
            yield
            t_qT = []
            for a in range(TT):
                for i in range(2):
                    b = 4 + 2 * a + i
                    t = transposes([(ps[:, b, r * P:(r + 1) * P], scr[:, a * D + (4 * i + r) * P:a * D + (4 * i + r + 1) * P], P)
                                    for r in range(4)], [*t_rq, *bank_waits(b)])
                    e = ts(zb3[:, a, ZQA + i * 512:ZQA + (i + 1) * 512], ps[:, b, :], HD ** -0.5, None, ALU.mult, None, [t])
                    free[b] = [e]
                    t_qT.append(e)
            t = transposes([(ps[:, 2, a * P:(a + 1) * P], pt_buf[:, 1024 + a * P:1024 + (a + 1) * P], P)
                            for a in range(TT)], [*t_rk, *bank_waits(2)])
            t_kT = [copy(keys[e * HD:(e + 1) * HD, e * S:(e + 1) * S], ps[e * HD:(e + 1) * HD, 2, 0:S], [t])
                    for e in range(2)]
            free[2] = [t_kT[-1]]
            swa["sides"] = [*t_qT, *t_kT]
            yield
            yield from pipeline([
                (lambda r=r: scores(lambda a: zb3[:, a, ZQA + r * P:ZQA + (r + 1) * P], keys[:, 0:512],
                                    swa["sides"], c2("band"), sink=cur[:, 136 + 2 * r:138 + 2 * r]),
                 lambda job, r=r: values(job, lambda kt, e: zb3[:, kt, ZVA + e * HD:ZVA + (e + 1) * HD],
                                         t_kva, swa_evac(r)))
                for r in range(SWA_PAIRS)])

        Q, K, FG = gates[:, 0:2048], gates[:, 2048:4096], buf_d[:, :]
        one_m, floor_, kf = (cur[:, PL_IN + 8 * i:PL_IN + 8 * i + 8] for i in range(3))
        t_q, t_f, t_k = {}, {}, {}
        between.append(sliding())
        for j in range(2):
            def q_evac(b, src, t, j=j):
                c = (4 * j + 2 * b) * S
                e = act(Q[:, c:c + 512], src, ACT.Silu, [t])
                t_q.setdefault(j, []).append(e)
                return [e]

            def f_evac(b, src, t, j=j):
                h = 4 * j + 2 * b
                c = h * S
                e1 = act(FG[:, c:c + 512], src, ACT.Sigmoid, [t])
                e2 = act(K[:, c:c + 512], src, ACT.Sigmoid, [t], scale=-1.0)
                for i in range(2):
                    r = slice(c + i * S, c + (i + 1) * S)
                    t_f.setdefault(j, []).append(ts(FG[:, r], FG[:, r], one_m[:, h + i:h + i + 1],
                                                    floor_[:, h + i:h + i + 1], ALU.mult, ALU.add, [e1]))
                    t_k.setdefault(j, []).append(ts(K[:, r], K[:, r], one_m[:, h + i:h + i + 1],
                                                    kf[:, h + i:h + i + 1], ALU.mult, ALU.add, [e2]))
                return [e2]
            proj_feature(layer_panel(), t_h, q_evac)
            proj_feature(layer_panel(), t_h, f_evac)

        rec_ = [{"q": t_q[j], "k": t_k[j], "tot": FG[:, j * 1024:(j + 1) * 1024], "t_tot": t_f[j], "am": [t_A0]}
                for j in range(2)]

        def q_of(j):
            return Q[:, j * 1024:(j + 1) * 1024]

        def k_of(j):
            return K[:, j * 1024:(j + 1) * 1024]

        def am_of(j):
            return buf_c[:, j * 1024:(j + 1) * 1024].rearrange("p (n t) -> p n t", n=8)

        def level(j, lv):
            r, q, k, f = rec_[j], q_of(j), k_of(j), FG[:, j * 1024:(j + 1) * 1024]
            b = 2 + 2 * j
            t = mms([(ps[:, b + n // 4, (n % 4) * P:(n % 4 + 1) * P], k[:, n * P:(n + 1) * P],
                      q[:, n * P:(n + 1) * P], True, True) for n in range(8)],
                    [*r["q"], *r["k"], *bank_waits(b, b + 1)])
            if lv == 0:
                r["q"] = [tt(q, q, f, ALU.mult, [t, *t_f[j], *r["am"]])]
            else:
                m = 1 << (lv - 1)
                qv, kv = (x.rearrange("p (b two m) -> p b two m", two=2, m=m) for x in (q, k))
                tv = r["tot"].rearrange("p (b two) -> p b two", two=2)
                r["q"] = [tt(qv[:, :, 1, :], qv[:, :, 1, :], bc(tv[:, :, 0], m), ALU.mult,
                             [t, *r["t_tot"], *r["am"]])]
                r["k"] = [tt(kv[:, :, 0, :], kv[:, :, 0, :], bc(tv[:, :, 1], m), ALU.mult, [t, *r["t_tot"]])]
                n = 1024 >> lv
                tot = buf_b[:, j * 512:j * 512 + n] if lv % 2 else f[:, 0:n]
                r["t_tot"] = [tt(tot, tv[:, :, 0], tv[:, :, 1], ALU.mult, r["t_tot"])]
                r["tot"] = tot
            mask = level_mask[:, lv, :].unsqueeze(1).to_broadcast([P, 8, P])
            data = bank(b, 2).rearrange("p (n t) -> p n t", n=8)
            am = am_of(j)
            e = p.op("dve", lambda *i: V.copy_predicated(am, mask, data), [t, *r["am"]])
            r["am"] = [e]
            free[b] = free[b + 1] = [e]

        def cross(j):
            b = 2 + j
            t = mms([(ps[:, b, h * P:(h + 1) * P], k_of(j)[:, h * S:h * S + P], q_of(j)[:, h * S + P:(h + 1) * S],
                      True, True) for h in range(4)], [*rec_[j]["q"], *rec_[j]["k"], *bank_waits(b)])
            t = act(buf_a[:, j * 512:(j + 1) * 512], ps[:, b, :], ACT.Copy, [t])
            free[b] = [t]
            rec_[j]["cross"] = t

        def hgrn_values(j):
            m0, m1 = [], []
            b = 2 * j
            am = am_of(j)
            for h in range(4):
                hc = slice(ZI + (4 * j + h) * P, ZI + (4 * j + h + 1) * P)
                c = slice(h * P, (h + 1) * P)
                m0 += [(ps[:, b, c], am[:, 2 * h, :], zb3[:, 0, hc], True, True)]
                m1 += [(ps[:, b + 1, c], am[:, 2 * h + 1, :], zb3[:, 1, hc], True, False),
                       (ps[:, b + 1, c], buf_a[:, (j * 4 + h) * P:(j * 4 + h + 1) * P], zb3[:, 0, hc], False, True)]
            t = mms(m0 + m1, [rec_[j]["cross"], *rec_[j]["am"], *t_i, *bank_waits(b, b + 1)])
            for a in range(TT):
                e = act(zb3[:, a, ZI + j * 512:ZI + (j + 1) * 512], ps[:, b + a, :], ACT.Copy, [t])
                free[b + a] = [e]
                hg["out"].append(e)

        hg = {"out": []}

        def turn_half(dst, col, waits):
            outs = []
            for i in range(4):
                b = i
                t = transposes([(ps[:, b, f * S + a * P:f * S + (a + 1) * P],
                                 zb3[:, a, col + (2 * i + f) * P:col + (2 * i + f + 1) * P], P)
                                for f in range(2) for a in range(TT)], [*waits, *bank_waits(b)])
                e = copy(dst[:, i * 512:(i + 1) * 512], ps[:, b, :], [t], "act" if i % 2 else "dve")
                free[b] = [e]
                outs.append(e)
            return outs

        def hgrn():
            for lv in range(LEVELS):
                for j in range(2):
                    level(j, lv)
                yield
            for j in range(2):
                cross(j)
            yield
            for j in range(2):
                hgrn_values(j)
                yield
            oh = zb3[:, :, ZI:ZI + 1024].rearrange("p a (h d) -> p a h d", h=HG)
            zh = zb3[:, :, ZZ:ZZ + 1024].rearrange("p a (h d) -> p a h d", h=HG)
            g_head = cur[:, 8:136].unsqueeze(1).unsqueeze(1).to_broadcast([P, TT, HG, P])
            t_gz = tt(zh, zh, g_head, ALU.mult, [*t_zh, t_cur], "pool")
            sq = buf_d[:, :].rearrange("p (a h d) -> p a h d", a=TT, h=HG)
            ss = stat[:, 992:1008].rearrange("p (a h) -> p a h", a=TT)
            t = tt(sq, oh, oh, ALU.mult, hg["out"])
            t = red(ss, sq, ALU.add, [t])
            t = rstd(ss, ss, P, [t])
            t = tt(oh, oh, bc(ss, P), ALU.mult, [t])
            t = tt(oh, oh, zh, ALU.mult, [t, t_gz])
            hg["normed"] = t
            for _ in range(3):
                yield
            hg["oT"] = turn_half(Q, ZI, [t])
            yield

        t_za = token_panel(ZZA, 512, ACT.Silu) + token_panel(ZZA + 512, 512, ACT.Silu)
        while len(swa["out"]) < SWA_PAIRS:
            fill()
        oa = zb3[:, :, ZQA:ZQA + 1024]
        t_oa = tt(oa, oa, zb3[:, :, ZZA:ZZA + 1024], ALU.mult, [*swa["out"], *t_za], "pool")
        between.append(hgrn())
        t_i = token_panel(ZI, 512) + token_panel(ZI + 512, 512)
        t_zh = token_panel(ZZ, 512, ACT.Silu) + token_panel(ZZ + 512, 512, ACT.Silu)

        t_oaT = turn_half(scr, ZQA, [t_oa])
        bank_waits_y = bank_waits(4, 5, 6, 7)

        def out_part(src, waits, first, last):
            for n in range(2):
                w, ready, s = layer_panel()
                for k in range(4):
                    t = mms([(ps[:, 4 + 2 * a + h, :], src[:, (4 * n + k) * S + a * P:(4 * n + k) * S + (a + 1) * P],
                              k1024(w)[:, k, h * 512:(h + 1) * 512], first and n == 0 and k == 0,
                              last and n == 1 and k == 3) for a in range(TT) for h in range(2)],
                            [ready, *waits, *(bank_waits_y if first else [])])
                    slot_free[s] = [t]
                    fill()
            return t

        out_part(scr, t_oaT, True, False)
        fill_all()
        t = out_part(Q, hg["oT"], False, True)
        ssb = stat[:, 1008:1012]
        sst, rst = stat[:, 1012:1014], stat[:, 1014:1016]
        t1 = [act(scr[:, b * 512:(b + 1) * 512], ps[:, 4 + b, :], ACT.Square, [t], accum_out=ssb[:, b:b + 1])
              for b in range(4)]
        t2 = red(sst, ssb.rearrange("p (a h) -> p a h", a=TT), ALU.add, t1)
        t2 = rstd(rst, sst, D, [t2])
        t_x3 = []
        for b in range(4):
            a, h = b // 2, b % 2
            tmp = scr[:, b * 512:(b + 1) * 512]
            xs = x_tok[:, b * 512:(b + 1) * 512]
            e = stt(tmp, ps[:, 4 + b, :], rst[:, a:a + 1], post[:, h * 512:(h + 1) * 512], ALU.mult, ALU.mult,
                    [t2, t1[b], t_post])
            t_x3.append(tt(xs, xs, tmp, ALU.add, [e]))
        for s in range(RING):
            carry_slot[s].token = slot_free[s][0].prev()
        for b in range(4):
            carry_x[b].token = t_x3[b].prev()
        p.end_loop()

        t = p.dma("sp", lambda *i: nc.sync.dma_start(out.rearrange("o (a p) d -> p (o a) d", p=P), x3), "out", t_x3)
        p.fence("sp", [t])

        block = ctx.enter_context(nc.Block())

        @block.sync
        def _(_e):
            p.emit("sp")

        @block.tensor
        def _(_e):
            p.emit("pe")

        @block.vector
        def _(_e):
            p.emit("dve")

        @block.scalar
        def _(_e):
            p.emit("act")

        @block.gpsimd
        def _(_e):
            p.emit("pool")


def shape_constants():
    f = np.float32
    s = np.arange(P)[:, None]
    ident = np.eye(P, dtype=f)
    ntri = -(s <= np.arange(S)[None, :]).astype(f)

    def by_query(fn):
        k2, k1 = np.arange(S)[None, :], np.arange(P)[None, :]
        return np.concatenate([fn(s + P, k2, 0), fn(s + P, k2, 1), fn(s, k1, 0), fn(s, k1, 1)], 1)

    causal = by_query(lambda q, k, e: np.where(k <= q, 0.0, NEG))
    band = by_query(lambda q, k, e: np.where((k <= q) & (q - k < 128), 0.0, NEG))
    slope = lambda g, r: np.float32(2.0 ** (-(g * PAIRS + r + 1)))
    alibi = np.concatenate([by_query(lambda q, k, e: np.where(k <= q, -slope(e, r) * (q - k), NEG))
                            for r in range(PAIRS)], 1)
    n = np.arange(CMP_PAD)[None, :]
    cmp_, any_ = [], []
    for a in range(TT):
        dist = (s + a * P) - (n * 16 + 31)
        ok = (dist >= 0) & (n < N_CMP)
        for r in range(PAIRS):
            for g in range(2):
                cmp_.append(np.where(ok, -slope(g, r) * dist, NEG))
        any_.append(ok.any(1, keepdims=True).astype(f))
    first = np.broadcast_to(np.array([4, 3, 2, 1], f), (P, 4))
    c1 = np.concatenate([ntri, causal, alibi, *cmp_, *any_, first, np.broadcast_to(np.arange(P), (P, P))], 1).astype(f)
    half = HD // 2
    freq = np.float32(10000.0) ** (-np.arange(half, dtype=f) / np.float32(half))
    ang = [((s + a * P).astype(f) * freq[None, :]).astype(f) for a in range(TT)]
    t = np.arange(P)[None, :]
    levels = [(s == t)]
    for lv in range(1, LEVELS):
        m = 1 << (lv - 1)
        levels.append((s // (2 * m) == t // (2 * m)) & (s % (2 * m) < m) & (t % (2 * m) >= m))
    c2 = np.concatenate([band, *[np.cos(x) for x in ang], *[np.sin(x) for x in ang],
                         *[x.astype(f) for x in levels]], 1).astype(f)
    assert c1.shape[1] == C1_W and c2.shape[1] == C2_W
    return ident, c1, c2


def lay_out(x):
    g = {k: np.asarray(v) for k, v in x.items()}
    w = g["w_in"][0]
    cuts = np.cumsum([512, 512, 512, 8, 512, 128, 128, 128, 128, 128, 128, 24, 1024])
    fq, fk, fv, ff, nq, kc, vc, ks, vs, kw, vw, ng, ga, gb = np.split(w, cuts, axis=1)
    nq = nq.reshape(D, 2, 4, HD).transpose(0, 2, 1, 3).reshape(D, 512)
    ng = ng.reshape(D, 2, 4, 3).transpose(0, 3, 2, 1).reshape(D, 24)
    mixed = np.concatenate([kw, vw, ff, ng, np.zeros((D, 512 - Z5), w.dtype)], 1)

    def cols(m):
        n = m.shape[1] // 512
        return list(m.reshape(KT, P, n, 512).transpose(2, 1, 0, 3).reshape(n, P, PANEL))

    def rows(m):
        n = m.shape[0] // 512
        return list(m.reshape(n, 4, P, D).transpose(0, 2, 1, 3).reshape(n, P, PANEL))

    pan = cols(fq) + cols(fk) + cols(mixed) + cols(fv) + cols(nq) + cols(np.concatenate([kc, vc, ks, vs], 1))
    pan += cols(ga) + cols(gb)
    for nme in ("cmp_k_w1", "cmp_v_w1"):
        pan.append(g[nme][0].reshape(16, P, 256).transpose(1, 0, 2).reshape(P, PANEL))
    pan += rows(g["w_fox_up"][0])
    pan += rows(g["w_nsa_up"][0].reshape(2, 4, HD, D).transpose(1, 0, 2, 3).reshape(512, D))
    pan += rows(g["w_out"][0])
    for e in range(N_EXP):
        pan += cols(g["w_gate"][0, e]) + cols(g["w_up"][0, e]) + rows(g["w_down"][0, e])
    for l in range(LAYERS):
        w2 = g["w_in_2"][l]
        qh, fh, ih, zh, qa, ka, va, za = np.split(w2, np.cumsum([1024, 1024, 1024, 1024, 1024, 128, 128]), axis=1)
        pair = lambda m: m.reshape(-1, 2, 8, HD).transpose(0, 2, 1, 3).reshape(-1, 1024)
        qa, za = pair(qa), pair(za)
        qh, fh = cols(qh), cols(fh)
        pan += cols(qa) + cols(np.concatenate([ka, va, np.zeros((D, 256), w2.dtype)], 1))
        pan += [qh[0], fh[0], qh[1], fh[1]] + cols(za) + cols(ih) + cols(zh)
        wo = g["w_out_2"][l]
        pan += rows(wo[1024:].reshape(2, 8, HD, D).transpose(1, 0, 2, 3).reshape(1024, D))
        pan += rows(wo[:1024])
    panels = np.stack(pan)
    assert panels.shape[0] == N_PANELS

    def feat(v):
        return v.reshape(-1, P).T

    def every(v):
        return np.broadcast_to(v.reshape(1, -1), (P, v.size))

    def twice(v):
        return np.concatenate([v, v]).reshape(P, 1)

    def pos_(v):
        return v.reshape(16, P).T

    def w2_(v):
        return v.reshape(2, P, HD).transpose(1, 0, 2).reshape(P, 128)

    route = np.concatenate([g["w_group"][0], g["w_router"][0]], 1).reshape(KT, P, 20).transpose(1, 0, 2).reshape(P, 160)
    prm = np.concatenate([
        feat(g["norm_mix_g"][0]), feat(g["norm_ffn_g"][0]), twice(g["fox_q_g"][0]), twice(g["fox_k_g"][0]),
        twice(g["nsa_q_g"][0]), twice(g["nsa_k_g"][0]), pos_(g["cmp_k_pos"][0]), pos_(g["cmp_v_pos"][0]),
        every(g["b_forget"][0]), every(np.concatenate([g["b_group"][0], g["b_router"][0]])), route,
        w2_(g["cmp_k_w2"][0]), w2_(g["cmp_v_w2"][0]),
        g["lb_param_2"].reshape(LAYERS, HG, P).transpose(2, 0, 1).reshape(P, 16)], 1)
    lay = np.stack([np.concatenate([
        feat(g["g_pre_2"][l]), every(g["g_head_2"][l]),
        every(g["sinks_2"][l].reshape(2, 8).T)], 1) for l in range(LAYERS)])
    return {"panels": panels, "x": g["x"], "prm": prm, "lay": lay, "post": g["g_post_2"]}


def kernel(**inputs):
    import concourse.bacc as bacc
    from concourse.bass_utils import run_bass_kernel_spmd

    arrays = lay_out(inputs)
    arrays["ident"], arrays["c1"], arrays["c2"] = shape_constants()
    arrays = {"in_" + k: np.ascontiguousarray(v) for k, v in arrays.items()}
    nc = bacc.Bacc("TRN2", target_bir_lowering=False, num_devices=1)
    aps = {k: nc.dram_tensor(k, v.shape, mybir.dt.from_np(v.dtype), kind="ExternalInput").ap()
           for k, v in arrays.items()}
    out = nc.dram_tensor("out", (1, S, D), F32, kind="ExternalOutput").ap()
    build(nc, aps["in_panels"], aps["in_x"], aps["in_prm"], aps["in_lay"], aps["in_post"], aps["in_ident"],
          aps["in_c1"], aps["in_c2"], out)
    r = run_bass_kernel_spmd(nc, [arrays], core_ids=[0])
    return r.results[0]["out"]
```

```python
from contextlib import ExitStack

import numpy as np
import concourse.bass as bass
from concourse import mybir
from concourse.alu_op_type import AluOpType as ALU

ACT = mybir.ActivationFunctionType
F32 = mybir.dt.float32
F32R = mybir.dt.float32r
U32 = mybir.dt.uint32
AX = mybir.AxisListType.X

P = 128
S = 256
TT = S // P
D = 1024
KT = D // P
HD = 64
PAIRS = 4
EPS = 1e-6
NEG = -1e30
N_CMP, CMP_PAD = 15, 32
N_EXP = 16
GRP, EPG = 4, 4
LAYERS = 2
HG = 8
SWA_PAIRS = 8
LB_FLOOR = 1e-20
LEVELS = 8
PANEL = 4096
HALF = PANEL // 2
RING = 4
PIECE = 512
PIECES = 9

PN_Z, PN_GATE, PN_CMP, PN_FOX_UP, PN_NSA_UP, PN_OUT, PN_MOE = 0, 6, 10, 12, 13, 14, 16
PN_L2 = PN_MOE + 3 * N_EXP
L2_PANELS = 17
N_PANELS = PN_L2 + LAYERS * L2_PANELS
Z5 = 288

PRM = {}
_n = 0
for _name, _w in (("g_mix", 8), ("g_ffn", 8), ("fq_g", 1), ("fk_g", 1), ("nq_g", 1), ("nk_g", 1),
                  ("pos_k", 16), ("pos_v", 16), ("b_forget", 8), ("b_route", 20), ("w_route", 160),
                  ("w2_k", 128), ("w2_v", 128), ("lb", 16)):
    PRM[_name] = (_n, _n + _w)
    _n += _w
PRM_W = _n
PL = {"g_pre": (0, 8), "g_head": (8, 136), "sinks": (136, 152)}
PL_IN = 152
PL_W = PL_IN + 3 * 8
ZB = 3328
C1 = {"ntri": (0, 256), "causal": (256, 1024), "dist": (1024, 1792), "cmp": (1792, 2304), "any": (2304, 2306),
      "first": (2306, 2310), "slot": (2310, 2438)}
C1_W = 2438
C2 = {"band": (0, 768), "cos": (768, 832), "sin": (832, 896), "level": (896, 896 + LEVELS * P)}
C2_W = 896 + LEVELS * P


class Token:

    def __init__(self, sem, scope, off, back=0):
        self.sem, self.scope, self.off, self.back = sem, scope, off, back

    def prev(self):
        return Token(self.sem, self.scope, self.off, 1)


class Later:

    def __init__(self):
        self.token = None


class Scope:
    def __init__(self, parent, n):
        self.parent, self.n, self.flag = parent, n, None
        self.count, self.start, self.items = {}, {}, {}
        self.depth = 0 if parent is None else parent.depth + 1


class Program:

    def __init__(self, nc, ctx):
        self.nc, self.ctx = nc, ctx
        self.engines = {"pe": nc.tensor, "dve": nc.vector, "act": nc.scalar, "pool": nc.gpsimd, "sp": nc.sync}
        self.sems = {e: ctx.enter_context(nc.semaphore("done_" + e)) for e in ("pe", "dve", "act", "pool")}
        self.scope = self.root = Scope(None, 1)

    def count(self, sem, by):
        c = self.scope.count
        c[sem] = c.get(sem, 0) + by
        return Token(sem, self.scope, c[sem])

    def op(self, eng, fn, waits=()):
        token = self.count(eng, 1)
        self.scope.items.setdefault(eng, []).append((fn, list(waits), eng, 1))
        return token

    def dma(self, eng, fn, sem, waits=()):
        if sem not in self.sems:
            self.sems[sem] = self.ctx.enter_context(self.nc.semaphore("dma_" + sem))
        token = self.count(sem, 16)
        self.scope.items.setdefault(eng, []).append((fn, list(waits), sem, 16))
        return token

    def fence(self, eng, waits):
        self.scope.items.setdefault(eng, []).append((None, list(waits), None, 0))

    def begin_loop(self, n):
        s = Scope(self.scope, n)
        s.start = None
        for e in ("pe", "dve", "act", "pool", "sp"):
            self.scope.items.setdefault(e, []).append(s)
        s.start = dict(self.scope.count)
        self.scope = s
        return s

    def end_loop(self):
        s = self.scope
        self.scope = s.parent
        for sem, c in s.count.items():
            self.scope.count[sem] = self.scope.count.get(sem, 0) + s.n * c

    def begin_if(self, flag, waits):
        s = self.begin_loop(1)
        s.flag, s.flag_waits = flag, list(waits)
        return s

    end_if = end_loop

    def value(self, t, here, regs):
        around = []
        s = here
        while s is not None:
            around.append(s)
            s = s.parent
        val = t.off
        if t.back:
            val = val - t.scope.count[t.sem]
        s = t.scope
        terms = []
        while s.parent is not None:
            val += s.start.get(t.sem, 0)
            per = s.count.get(t.sem, 0)
            if s in around:
                terms.append((s.depth - 1, per))
            else:
                val += (s.n - 1) * per
            s = s.parent
        key = (t.sem, tuple(terms))
        low = val
        expr = val
        for d, per in terms:
            if per:
                expr = regs[d] * per + expr
        assert low > 0, ("a wait on a value that may not be positive", t.sem, low)
        return key, val, expr

    def emit(self, eng, scope=None, regs=(), known=None):
        scope = scope or self.root
        e = self.engines[eng]
        known = {} if known is None else known
        for item in scope.items.get(eng, []):
            if isinstance(item, Scope):
                if item.flag is not None and self.uses(item, eng):
                    self.emit_if(eng, item, known)
                elif self.uses(item, eng):
                    with e.Fori(0, item.n) as i:
                        self.emit(eng, item, regs + (i,), {})
                continue
            fn, waits, sem, by = item
            need = {}
            for t in waits:
                if isinstance(t, Later):
                    t = t.token
                if t is None:
                    continue
                key, val, expr = self.value(t, scope, regs)
                if known.get(key, 0) < val and (key not in need or need[key][0] < val):
                    need[key] = (val, expr)
            for key, (val, expr) in need.items():
                e.wait_ge(self.sems[key[0]], expr)
                known[key] = val
            if fn is not None:
                fn(*regs).then_inc(self.sems[sem], by)

    def emit_if(self, eng, item, known):
        e = self.engines[eng]
        for t in item.flag_waits:
            e.wait_ge(self.sems[t.sem], self.value(t, self.root, ())[1])
        own = [sem for sem, by in item.count.items() if by and (sem == eng or (eng == "sp" and sem.startswith("slot")))]
        for sem in own:
            if item.start.get(sem, 0):
                e.wait_ge(self.sems[sem], item.start[sem])
        flag = e.value_load(item.flag, min_val=0, max_val=S)
        with e.If(flag > 0):
            self.emit(eng, item, (0,), dict(known))
        with e.Else():
            for sem in own:
                e.sem_inc(self.sems[sem], item.count[sem])

    def uses(self, scope, eng):
        return any(self.uses(x, eng) if isinstance(x, Scope) else True for x in scope.items.get(eng, []))


def build(nc, panels, x_in, prm_in, lay_in, post_in, c0_in, c1_in, c2_in, out):
    ctx = ExitStack()
    with ctx:
        def sb(name, cols, dt=F32, parts=P):
            return ctx.enter_context(nc.sbuf_tensor(name, [parts, cols], dt))

        p = Program(nc, ctx)
        V, A, T, G = nc.vector, nc.scalar, nc.tensor, nc.gpsimd

        ring = sb("ring", RING * HALF)
        x_tok = sb("x_tok", TT * D)
        op_hi = sb("op_hi", KT * S, F32R)
        op_lo = sb("op_lo", KT * S, F32R)
        w_hi = sb("w_hi", PIECES * PIECE, F32R)
        w_lo = sb("w_lo", PIECES * PIECE, F32R)
        wr_hi, wr_lo = sb("wr_hi", 160, F32R), sb("wr_lo", 160, F32R)
        ident = sb("ident", P)
        prm = sb("prm", PRM_W)
        cst = sb("cst", max(C1_W, C2_W))
        zin = sb("zin", TT * ZB)
        gates = sb("gates", 16 * S)
        buf_a = sb("buf_a", 1024)
        buf_b = sb("buf_b", 1024)
        keys = sb("keys", 2560)
        buf_c = sb("buf_c", 2048)
        buf_d = sb("buf_d", 2048)
        s_buf = sb("s_buf", 2 * 768)
        pt_buf = sb("pt_buf", 2 * 768)
        scr = sb("scr", 2048)
        stat = sb("stat", 1024)
        ps = ctx.enter_context(nc.psum_tensor("ps", [P, 8, 512], F32))

        def bank(b, n=1):
            return ps[:, b, :] if n == 1 else ps[:, b:b + n, :].rearrange("p a b -> p (a b)")

        free = {b: [] for b in range(8)}

        def bank_waits(*bs):
            return [t for b in bs for t in free[b]]

        def tt(out_, a, b, op, waits=(), eng="dve"):
            f = V if eng == "dve" else G
            return p.op(eng, lambda *i: f.tensor_tensor(out_, a, b, op), waits)

        def ts(out_, a, s1, s2, op0, op1, waits=(), eng="dve"):
            f = V if eng == "dve" else G
            if s2 is None:
                return p.op(eng, lambda *i: f.tensor_scalar(out_, a, s1, None, op0), waits)
            return p.op(eng, lambda *i: f.tensor_scalar(out_, a, s1, s2, op0, op1), waits)

        def stt(out_, a, s1, b, op0, op1, waits=()):
            return p.op("dve", lambda *i: V.scalar_tensor_tensor(out_, a, s1, b, op0, op1), waits)

        def red(out_, a, op, waits=()):
            return p.op("dve", lambda *i: V.tensor_reduce(out_, a, AX, op), waits)

        def copy(out_, a, waits=(), eng="dve"):
            if eng == "act":
                return p.op("act", lambda *i: A.activation(out_, a, ACT.Copy), waits)
            f = V if eng == "dve" else G
            return p.op(eng, lambda *i: f.tensor_copy(out_, a), waits)

        def act(out_, a, func, waits=(), **kw):
            return p.op("act", lambda *i: A.activation(out_, a, func, **kw), waits)

        def memz(ap, waits=(), eng="pool"):
            f = V if eng == "dve" else G
            return p.op(eng, lambda *i: f.memset(ap, 0.0), waits)

        def mms(triples, waits=()):
            def run(*i):
                for o, l, r, s0, s1 in triples:
                    last = T.matmul(o, l, r, start=s0, stop=s1)
                return last
            return p.op("pe", run, waits)

        def transposes(pairs, waits=()):
            def run(*i):
                for o, a, n in pairs:
                    last = T.transpose(o, a, ident[0:n, 0:n])
                return last
            return p.op("pe", run, waits)

        def bc(ap, n):
            return ap.unsqueeze(len(ap.shape)).to_broadcast(list(ap.shape) + [n])

        def prmc(name, a=0, b=None):
            lo, hi = PRM[name]
            return prm[:, lo + a:(hi if b is None else lo + b)]

        slot_ap = [ring[:, s * HALF:(s + 1) * HALF] for s in range(RING)]
        slot_free = [[] for _ in range(RING)]
        pos = [0]

        def load_half(index):
            s = pos[0] % RING
            pos[0] += 1
            dst = slot_ap[s]
            t = p.dma("sp", lambda *i: nc.sync.dma_start(
                dst, panels[index(*i)] if callable(index) else panels[index]), f"slot{s}", slot_free[s])
            return dst, t, s

        def fm(ap, k):
            return ap.rearrange("p (k t) -> p k t", k=k)

        def tm(ap):
            return ap.rearrange("p (a n) -> p a n", a=TT)

        hi3, lo3 = fm(op_hi[:, :], KT), fm(op_lo[:, :], KT)
        x3 = tm(x_tok[:, :])

        between = []

        def fill():
            for g in list(between):
                if next(g, "end") == "end":
                    between.remove(g)

        def fill_all():
            while between:
                fill()

        def split(hi, lo, src, waits, engines=("act", "dve"), before=()):
            t1 = copy(hi, src, waits, engines[0])
            return [t1, tt(lo, src, hi.bitcast(F32), ALU.subtract, [t1, *waits, *before], engines[1])]

        def three(o, l, r, start, stop):
            return [(o, l[0], r[0], start, False), (o, l[0], r[1], False, False), (o, l[1], r[0], False, stop)]

        def operand(lo_col, n):
            return op_hi[:, lo_col:lo_col + n], op_lo[:, lo_col:lo_col + n]

        plan = []
        current = []
        parts = []
        piece_free = [[] for _ in range(PIECES)]
        n_piece = [0]
        beside_attention = [[("act", "pool")] * 4]
        beside_experts = [[("act", "pool"), ("act", "dve"), ("dve", "dve"), ("act", "pool")],
                          [("act", "dve"), ("act", "dve"), ("act", "dve"), ("act", "pool")]]
        splitters = [beside_attention]

        def plan_panel(index, cols=PIECE, halves=2):
            for h in range(halves):
                plan.append(((lambda *i, h=h: index(*i) * 2 + h) if callable(index) else 2 * index + h, cols))

        def ahead(n):
            while len(parts) < n and (current or plan):
                if not current:
                    index, cols = plan.pop(0)
                    w, ready, s = load_half(index)
                    which = splitters[0].pop(0)
                    splitters[0].append(which)
                    current.extend((w[:, i * PIECE:i * PIECE + cols], ready, s, cols, e) for i, e in enumerate(which))
                    slot_free[s] = []
                v, ready, s, cols, engines = current.pop(0)
                b = n_piece[0] % PIECES
                n_piece[0] += 1
                hi, lo = (x[:, b * PIECE:b * PIECE + cols] for x in (w_hi, w_lo))
                before = [] if current else [t for t in slot_free[s] if t.sem != engines[1]]
                done = split(hi, lo, v, [ready, *piece_free[b]], engines, before)
                slot_free[s] = [*slot_free[s], done[1]] if current else done[1:]
                parts.append((hi, lo, done, b))

        def take():
            ahead(PIECES)
            two = [parts.pop(0), parts.pop(0)]

            def used(t):
                for x in two:
                    piece_free[x[3]] = [t]
            return [(x[0], x[1]) for x in two], [t for x in two for t in x[2]], used

        def proj_token(n, waits, evac):
            toks = []
            per = 2 if 2 * n == PIECE else 1
            for k0 in range(0, KT, 2 * per):
                w, ready, used = take()
                for a in range(TT):
                    m = []
                    for j in range(2 * per):
                        k = k0 + j
                        x = (hi3[:, k, a * P:(a + 1) * P], lo3[:, k, a * P:(a + 1) * P])
                        c = j % per * n
                        m += three(ps[:, a, 0:n], x, tuple(v[:, c:c + n] for v in w[j // per]), k == 0, k == KT - 1)
                    t = mms(m, [*ready, *waits, *(bank_waits(a) if k0 == 0 else [])])
                    if k0 + 2 * per == KT:
                        free[a] = evac(a, ps[:, a, 0:n], t)
                        toks.append(t)
                used(t)
                fill()
            return toks

        def proj_feature(waits, evac):
            for b in range(2):
                for f in range(2):
                    w, ready, used = take()
                    m = []
                    for k in range(KT):
                        c = slice(k % 4 * P, (k % 4 + 1) * P)
                        w_k = tuple(x[:, c] for x in w[k // 4])
                        m += three(ps[:, b, f * S:(f + 1) * S], w_k, (hi3[:, k, :], lo3[:, k, :]), k == 0, k == KT - 1)
                    t = mms(m, [*ready, *waits, *(bank_waits(b) if f == 0 else [])])
                    used(t)
                    if f == 1:
                        free[b] = evac(b, ps[:, b, :], t)
                    fill()
            return t

        def rstd(out_, ss, n, waits):
            t = ts(out_, ss, 1.0 / n, EPS, ALU.mult, ALU.add, waits)
            e = minus_half[0:out_.shape[0], :]
            for _ in out_.shape[2:]:
                e = e.unsqueeze(2)
            e = e.to_broadcast(list(out_.shape))
            return p.op("pool", lambda *i: G.tensor_tensor(out_, out_, e, ALU.pow), [t, t_mh])

        def norm_transpose(src_tokens, gain, gain_waits, pieces=0):
            ss, rs = stat[:, 0:2], stat[:, 2:4]
            t1 = [act(scr[:, a * D:(a + 1) * D], x3[:, a, :], ACT.Square, src_tokens[a],
                      accum_out=ss[:, a:a + 1]) for a in range(TT)]
            t2 = rstd(rs, ss, D, t1)
            ahead(pieces)
            t3 = [ts(scr[:, a * D:(a + 1) * D], x3[:, a, :], rs[:, a:a + 1], None, ALU.mult, None, [t2, t1[a]])
                  for a in range(TT)]
            outs = []
            for b in range(4):
                q = 4 + b
                t = transposes([(ps[:, q, f * S + a * P:f * S + (a + 1) * P],
                                 scr[:, a * D + (2 * b + f) * P:a * D + (2 * b + f + 1) * P], P)
                                for f in range(2) for a in range(TT)], [*t3, *bank_waits(q)])
                his = [act(hi3[:, 2 * b + f, :], ps[:, q, f * S:(f + 1) * S], ACT.Copy, [t, *gain_waits],
                           scale=gain[:, 2 * b + f:2 * b + f + 1]) for f in range(2)]
                los = [stt(lo3[:, 2 * b + f, :], ps[:, q, f * S:(f + 1) * S], gain[:, 2 * b + f:2 * b + f + 1],
                           hi3[:, 2 * b + f, :].bitcast(F32), ALU.mult, ALU.subtract, [*his, *gain_waits])
                       for f in range(2)]
                free[q] = los
                outs += his + los
            return outs

        t_x = p.dma("act", lambda *i: A.dma_start(x3, x_in.rearrange("o (a p) d -> p (o a) d", p=P)), "x")
        t_id = p.dma("act", lambda *i: A.dma_start(ident[:, :], c0_in), "ident")
        t_prm = p.dma("act", lambda *i: A.dma_start(prm[:, :], prm_in), "prm")
        t_c1 = p.dma("act", lambda *i: A.dma_start(cst[:, 0:C1_W], c1_in), "cst")

        lay = sb("lay", LAYERS * PL_W)
        t_lay = [p.dma("act", lambda *i, l=l: A.dma_start(lay[:, l * PL_W:l * PL_W + PL_IN], lay_in[l]), "lay")
                 for l in range(LAYERS)]

        minus_half = sb("minus_half", 1)
        t_mh = p.op("pool", lambda *i: G.memset(minus_half[:, :], -0.5))

        def c1(name):
            return cst[:, C1[name][0]:C1[name][1]]

        def c2(name):
            return cst[:, C2[name][0]:C2[name][1]]

        fox_k = keys[:, 0:2048]
        win_k = keys[:, 2048:2560]
        slc_k = zin[:, TT * 2848:TT * 2848 + 512]
        memz(keys[:, :])
        t_zk = memz(slc_k)

        p.fence("pe", [t_id])
        for i in range(PN_CMP):
            plan_panel(i, PIECE if i != 2 else Z5)
        t_h = norm_transpose([[t_x], [t_x]], prmc("g_mix"), [t_prm], 5)

        z3 = zin[:, 0:TT * 2848].rearrange("p (a n) -> p a n", a=TT)
        ZFQ, ZFK, ZFV, ZNQ, ZKC, ZVC, ZKS, ZVS, ZKW, ZVW, ZFF, ZNG = (
            0, 512, 1024, 1536, 2048, 2176, 2304, 2432, 2560, 2688, 2816, 2824)
        done_z = {}

        def z_panel(n):
            cols = 512 if n < 5 else Z5

            def to_z(a, src, t, n=n, cols=cols):
                e = copy(z3[:, a, n * 512:n * 512 + cols], src, [t], "act" if a == 0 else "dve")
                done_z.setdefault(n, []).append(e)
                return [e]
            proj_token(cols, t_h, to_z)

        def head_norm(view, heads, waits):
            n = TT * heads
            sq = scr[:, 0:n * HD].rearrange("p (a h d) -> p a h d", a=TT, h=heads)
            ss = stat[:, 32:32 + n].rearrange("p (a h) -> p a h", a=TT)
            t = tt(sq, view, view, ALU.mult, waits)
            t = red(ss, sq, ALU.add, [t])
            t = rstd(ss, ss, HD, [t])
            return tt(view, view, bc(ss, HD), ALU.mult, [t])

        def heads(col, n):
            return z3[:, :, col:col + n * HD].rearrange("p a (h d) -> p a h d", h=n)

        def q_side(col, buf, gain, banks, waits):
            outs = []
            for i, b in enumerate(banks):
                t1 = transposes([(ps[:, b, f * S + a * P:f * S + (a + 1) * P],
                                  z3[:, a, col + (2 * i + f) * P:col + (2 * i + f + 1) * P], P)
                                 for f in range(2) for a in range(TT)], [*waits, *bank_waits(b)])
                t2 = ts(buf[:, i * 512:(i + 1) * 512], ps[:, b, :], gain, HD ** -0.5, ALU.mult, ALU.mult, [t1])
                free[b] = [t2]
                outs.append(t2)
            return outs

        def k_side(dst, col, npair, gain, b, t):
            outs = []
            per = min(npair, 2)
            for i in range((npair + 1) // 2):
                t1 = transposes([(ps[:, b + i, f * S + a * P:f * S + (a + 1) * P],
                                  z3[:, a, col + (2 * i + f) * P:col + (2 * i + f + 1) * P], P)
                                 for f in range(per) for a in range(TT)], [t, *bank_waits(b + i)])
                for e in range(2):
                    rows = slice(e * HD, (e + 1) * HD)
                    d4 = dst[rows, 2 * i * 512:(2 * i + per) * 512].rearrange("p (f e t) -> p f e t", f=per, e=2)
                    t2 = ts(d4[:, :, e, :], ps[rows, b + i, 0:per * S].rearrange("p (f t) -> p f t", f=per),
                            gain[rows, :], None, ALU.mult, None, [t1, t_zk])
                    outs.append(t2)
                free[b + i] = [t2]
            return outs

        lfb = buf_d[:, :]
        ntri = c1("ntri")
        cq = stat[:, 112:128].rearrange("p (a h) -> p a h", a=TT)
        o_tok = {}
        job_no = [0]

        def scores(q, k, waits, bias, forget=None, sink=None, slopes=None):
            j = job_no[0] % 2
            job_no[0] += 1
            job = {"j": j}
            k2 = k.rearrange("p (e t) -> p e t", e=2)
            last1 = forget is None
            m = [(ps[:, 2, :], q(1), k, True, last1)]
            if forget:
                for e in range(2):
                    l0, l1 = (lfb[:, (a * 8 + forget[0] + e) * P:(a * 8 + forget[0] + e + 1) * P] for a in range(2))
                    m += [(ps[:, 2, e * S:(e + 1) * S], l0, ntri, False, False),
                          (ps[:, 2, e * S + P:(e + 1) * S], l1, ntri[:, 0:P], False, e == 1)]
            m += [(ps[:, 3, 0:S].rearrange("p (e t) -> p e t", e=2), q(0), k2[:, :, 0:P], True, last1)]
            if forget:
                for e in range(2):
                    l0 = lfb[:, (forget[0] + e) * P:(forget[0] + e + 1) * P]
                    m += [(ps[:, 3, e * P:(e + 1) * P], l0, ntri[:, 0:P], False, e == 1)]
            t = mms(m, [*waits, *bank_waits(2, 3)])
            yield job
            sc = s_buf[:, j * 768:(j + 1) * 768]
            old = s_users[j]
            if forget:
                ts_ = []
                for a, lo, n in ((1, 0, S), (0, 512, P)):
                    for e in range(2):
                        r = slice(lo + e * n, lo + (e + 1) * n)
                        ts_.append(stt(sc[:, r], bank(2, 2)[:, r], cq[:, a, forget[0] + e:forget[0] + e + 1],
                                       bias[:, r], ALU.add, ALU.add, [t, fox["cum"], *old]))
            elif slopes:
                ts_ = [stt(sc[:, lo:lo + n], bias[:, lo:lo + n], slopes[e], bank(2, 2)[:, lo:lo + n], ALU.mult,
                           ALU.add, [t, *old]) for e, lo, n in ((0, 0, S), (1, S, S), (0, 512, P), (1, 640, P))]
            else:
                ts_ = [tt(sc, bank(2, 2)[:, 0:768], bias, ALU.add, [t, *old])]
            free[2] = free[3] = [ts_[-1]]
            b0 = 192 + 32 * j
            mx, ng_, sm, ex = (stat[:, b0 + 4 * i:b0 + 4 * i + 4] for i in range(4))
            rec = stat[:, b0 + 16 + 4 * 0:b0 + 20]
            m1 = red(mx[:, 2:4], sc[:, 0:512].rearrange("p (e t) -> p e t", e=2), ALU.max, ts_)
            m0 = red(mx[:, 0:2], sc[:, 512:768].rearrange("p (e t) -> p e t", e=2), ALU.max, ts_)
            if sink is not None:
                mx2 = mx.rearrange("p (a e) -> p a e", a=2)
                sk = sink.unsqueeze(1).to_broadcast([P, 2, 2])
                m0 = tt(mx2, mx2, sk, ALU.max, [m0, m1])
                x1 = tt(ex.rearrange("p (a e) -> p a e", a=2), sk, mx2, ALU.subtract, [m0])
            t = ts(ng_, mx, -1.0, None, ALU.mult, None, [m0, m1])
            last = []
            for c, lo, n in ((2, 0, S), (3, S, S), (0, 512, P), (1, 640, P)):
                last.append(act(sc[:, lo:lo + n], sc[:, lo:lo + n], ACT.Exp, [t], bias=ng_[:, c:c + 1],
                                accum_out=sm[:, c:c + 1]))
            if sink is not None:
                last.append(act(ex, ex, ACT.Exp, [x1]))
            job["sums"], job["probs"] = (sm, ex if sink is not None else None), last
            job["rec_ap"] = rec
            yield

        s_users, pt_users = [[], []], [[], []]
        o_free = {6: [], 7: []}

        def turn(job):
            j = job["j"]
            sc = s_buf[:, j * 768:(j + 1) * 768]
            t = transposes([(bank(4, 2)[:, i * P:(i + 1) * P], sc[:, i * P:(i + 1) * P], P) for i in range(6)],
                           [*job["probs"], *bank_waits(4, 5)])
            s_users[j] = [t]
            yield
            sm, ex = job["sums"]
            w = job["probs"]
            if ex is not None:
                w = [tt(sm, sm, ex, ALU.add, w)]
            job["rec"] = p.op("dve", lambda *i: V.reciprocal(job["rec_ap"], sm), w)
            e = act(pt_buf[:, j * 768:(j + 1) * 768], bank(4, 2)[:, 0:768], ACT.Copy, [t, *pt_users[j]])
            free[4] = free[5] = [e]
            job["pt"] = e
            yield

        def values(job, v, waits, evac):
            j = job["j"]
            b = 6
            pt = pt_buf[:, j * 768:(j + 1) * 768]
            o = ps[:, b, 0:256].rearrange("p (a e d) -> p a e d", a=TT, e=2)
            m = []
            for e in range(2):
                m.append((o[:, 0, e, :], pt[:, 512 + e * P:512 + (e + 1) * P], v(0, e), True, True))
                for kt in range(2):
                    m.append((o[:, 1, e, :], pt[:, e * S + kt * P:e * S + (kt + 1) * P], v(kt, e), kt == 0, kt == 1))
            t = mms(m, [job["pt"], *waits, *bank_waits(b)])
            pt_users[j] = [t]
            yield
            free[b] = evac(o, job["rec_ap"].rearrange("p (a e) -> p a e", a=2), [t, job["rec"]])
            yield

        t_fox = []
        fox = {}

        def fox_evac(pr):
            def evac(o, rec, w):
                e = tt(z3[:, :, ZFQ + pr * P:ZFQ + (pr + 1) * P].rearrange("p a (e d) -> p a e d", e=2), o,
                       bc(rec, HD), ALU.mult, w)
                t_fox.append(e)
                return [e]
            return evac

        jobs = []
        for pr in range(PAIRS):
            jobs.append((
                lambda pr=pr: scores(lambda a: buf_a[:, pr * S + a * P:pr * S + (a + 1) * P],
                                     fox_k[:, pr * 512:(pr + 1) * 512], fox["sides"], c1("causal"),
                                     forget=(2 * pr,)),
                lambda job, pr=pr: values(job, lambda kt, e: z3[:, kt, ZFV + (2 * pr + e) * HD:
                                                                ZFV + (2 * pr + e + 1) * HD],
                                          done_z[2], fox_evac(pr))))

        nsa = {"first": [], "last": []}

        def nsa_dst(r):
            return z3[:, :, ZNQ + r * P:ZNQ + (r + 1) * P].rearrange("p a (e d) -> p a e d", e=2)

        def nsa_evac(r, branch):
            def evac(o, rec, w):
                f = stat[:, 256 + 8 * branch:260 + 8 * branch].rearrange("p (a e) -> p a e", a=2)
                tmp = buf_c[:, 1216:1472].rearrange("p (a e d) -> p a e d", a=2, e=2)
                e1 = tt(f, rec, nsa["gates"][:, :, branch, 2 * r:2 * r + 2], ALU.mult, [*w, nsa["t_gates"]])
                if branch == 1:
                    e2 = tt(nsa_dst(r), o, bc(f, HD), ALU.mult, [e1])
                    nsa["first"].append(e2)
                else:
                    e2 = tt(tmp, o, bc(f, HD), ALU.mult, [e1, *nsa["last"][-1:]])
                    nsa["last"].append(tt(nsa_dst(r), nsa_dst(r), tmp, ALU.add, [e2, *nsa["first"]]))
                return [e2]
            return evac

        for branch, kk, zv in ((1, slc_k, ZVS), (2, win_k, ZVW)):
            for r in range(PAIRS):
                jobs.append((
                    lambda r=r, kk=kk: scores(lambda a: buf_b[:, r * S + a * P:r * S + (a + 1) * P], kk,
                                             nsa["sides"], c1("dist"), slopes=[slope(e, r) for e in range(2)]),
                    lambda job, r=r, zv=zv, branch=branch: values(
                        job, lambda kt, e: z3[:, kt, zv + e * HD:zv + (e + 1) * HD],
                        [*done_z[4], *done_z[5]], nsa_evac(r, branch))))

        def pipeline(jobs, ready=lambda i: True):
            live = {}
            for i in range(len(jobs) + 2):
                stages = []
                if i >= 2:
                    stages.append(jobs[i - 2][1](live[i - 2]))
                    next(stages[-1])
                if 1 <= i <= len(jobs):
                    stages.append(turn(live[i - 1]))
                    next(stages[-1])
                while i < len(jobs) and not ready(i):
                    yield
                if i < len(jobs):
                    stages.append(jobs[i][0]())
                    live[i] = next(stages[-1])
                yield
                for stage in stages:
                    next(stage)
                yield

        kv2 = buf_c[:, 0:1024].rearrange("p (c g t) -> p c g t", c=2, g=2)
        blk = [buf_d[:, c * 1024:(c + 1) * 1024].rearrange("p (m g n) -> p m g n", m=16, g=2) for c in range(2)]
        kc_bd = buf_c[:, 1024:1088]
        vc_bd = buf_c[0:64, 1088:1216]
        tmp_n = buf_c[:, 1472:1984]

        def compression():
            t_blk0 = memz(buf_d[:, :], t_fox)
            t_z = memz(buf_c[:, 1024:1216])
            cp = []
            for c in range(2):
                zc = (ZKC, ZVC)[c]
                t = transposes([(ps[:, 7, a * P:(a + 1) * P], z3[:, a, zc:zc + P], P) for a in range(TT)],
                               [*done_z[4], *bank_waits(7)])
                for g in range(2):
                    for jp in range(2):
                        cp.append(copy(kv2[jp * HD:(jp + 1) * HD, c, g, 0:S - jp],
                                       ps[g * HD:(g + 1) * HD, 7, jp:S], [t]))
                free[7] = [cp[-1]]
                yield
            bt = {0: [], 1: []}
            for c in range(2):
                pos_ap = prmc(("pos_k", "pos_v")[c])
                for g in range(2):
                    even = kv2[:, c, g, :].rearrange("p (n m j) -> p m n j", n=16, j=2)[:, :, :, 0]
                    bt[c].append(tt(blk[c][:, 0:8, g, 0:N_CMP], even[:, :, 0:N_CMP], bc(pos_ap[:, 0:8], N_CMP),
                                    ALU.add, [*cp, t_blk0]))
                    bt[c].append(tt(blk[c][:, 8:16, g, 0:N_CMP], even[:, :, 1:N_CMP + 1],
                                    bc(pos_ap[:, 8:16], N_CMP), ALU.add, [*cp, t_blk0]))
            yield
            hid = scr[0:64, 0:512]
            hidT_c = scr[:, 512:768]
            t_hid = []
            for c in range(2):
                for h in range(2):
                    w, ready, s = load_half(2 * (PN_CMP + c) + h)
                    w1 = w.rearrange("p (m n) -> p m n", m=8)
                    t = mms([(ps[0:64, 7, 0:256], blk[c][:, 8 * h + m, :, :].rearrange("p g n -> p (g n)"), w1[:, m, :],
                              h == 0 and m == 0, h == 1 and m == 7) for m in range(8)],
                            [ready, *bt[c], *bank_waits(7)])
                    slot_free[s] = [t]
                t = act(hid[:, c * 256:(c + 1) * 256], ps[0:64, 7, 0:256], ACT.Gelu_apprx_tanh, [t, *nsa["sides"]])
                free[7] = [t]
                t_hid.append(t)
                yield
            t = transposes([(ps[:, 7, i * 64:(i + 1) * 64], hid[:, i * P:(i + 1) * P], 64) for i in range(4)],
                           [*t_hid, *bank_waits(7)])
            t = copy(hidT_c, ps[:, 7, 0:256], [t])
            free[7] = [t]
            yield
            m = []
            for c in range(2):
                w2 = prmc(("w2_k", "w2_v")[c])
                m += [(ps[0:64, 7, c * 64:(c + 1) * 64], hidT_c[:, (2 * c + i) * 64:(2 * c + i + 1) * 64],
                       w2[:, i * 64:(i + 1) * 64], i == 0, i == 1) for i in range(2)]
            t = mms(m, [t, *bank_waits(7)])
            t_vc = [copy(vc_bd[g * 32:(g + 1) * 32, g * HD:(g + 1) * HD], ps[g * 32:(g + 1) * 32, 7, 64:128],
                         [t, t_z]) for g in range(2)]
            kcn, sq, ss = scr[0:64, 768:832], scr[0:64, 832:896], stat[0:64, 288:289]
            t = copy(kcn, ps[0:64, 7, 0:64], [t])
            free[7] = [t]
            t1 = tt(sq, kcn, kcn, ALU.mult, [t])
            t1 = red(ss, sq, ALU.add, [t1])
            t1 = rstd(ss, ss, HD, [t1])
            t1 = ts(kcn, kcn, ss, None, ALU.mult, None, [t1])
            yield
            t1 = transposes([(ps[0:64, 7, 0:64], kcn, 64)], [t1, *bank_waits(7)])
            t_kc = [ts(kc_bd[g * HD:(g + 1) * HD, g * 32:(g + 1) * 32], ps[0:64, 7, g * 32:(g + 1) * 32],
                       prmc("nk_g")[0:64, :], None, ALU.mult, None, [t1, t_z]) for g in range(2)]
            free[7] = [t_kc[-1]]
            yield
            t = mms([(ps[:, 7, (a * 4 + r) * 64:(a * 4 + r + 1) * 64], buf_b[:, r * S + a * P:r * S + (a + 1) * P],
                      kc_bd, True, True) for a in range(TT) for r in range(PAIRS)], [*t_kc, *bank_waits(7)])
            sc = scr[:, 1024:1536]
            t = tt(sc, ps[:, 7, :], c1("cmp"), ALU.add, [t])
            free[7] = [t]
            sc3 = sc.rearrange("p (h n) -> p h n", n=CMP_PAD)
            mx, sm, fc = stat[:, 320:336], stat[:, 336:352], stat[:, 352:368]
            t = red(mx, sc3, ALU.max, [t])
            t = tt(sc3, sc3, bc(mx, CMP_PAD), ALU.subtract, [t])
            t_pc = act(sc, sc, ACT.Exp, [t])
            t = red(sm, sc3, ALU.add, [t_pc])
            t = p.op("dve", lambda *i: V.reciprocal(sm, sm), [t])
            fc3 = fc.rearrange("p (a h) -> p a h", a=TT)
            t = tt(fc3, sm.rearrange("p (a h) -> p a h", a=TT), nsa["gates"][:, :, 0, :], ALU.mult, [t, nsa["t_gates"]])
            t_fc = tt(fc3, fc3, bc(c1("any"), 8), ALU.mult, [t])
            yield
            pct = scr[0:64, 0:1024]
            t_p = []
            for a in range(TT):
                t = transposes([(ps[0:64, 7, r * P:(r + 1) * P], sc[:, (a * 4 + r) * 64:(a * 4 + r + 1) * 64], P)
                                for r in range(PAIRS)], [t_pc, *bank_waits(7)])
                t = act(pct[:, a * 512:(a + 1) * 512], ps[0:64, 7, :], ACT.Copy, [t, t_fc])
                free[7] = [t]
                t_p.append(t)
                yield
            for a in range(TT):
                t = mms([(ps[:, 7, r * P:(r + 1) * P], pct[:, (a * 4 + r) * P:(a * 4 + r + 1) * P], vc_bd, True, True)
                         for r in range(PAIRS)], [*t_p, *t_vc, *bank_waits(7)])
                e = tt(tmp_n.rearrange("p (h d) -> p h d", h=8),
                       ps[:, 7, :].rearrange("p (h d) -> p h d", h=8), bc(fc3[:, a, :], HD), ALU.mult,
                       [t, t_fc, *nsa["last"][-1:]])
                free[7] = [e]
                dst = z3[:, a, ZNQ:ZNQ + 512]
                e = tt(dst, dst, tmp_n, ALU.add, [e, *nsa["first"]])
                nsa["last"].append(e)
                yield

        low, t_wr = {}, []

        def lower_bounds():
            lbp = prmc("lb").rearrange("p (l h) -> p l h", l=LAYERS)
            e_l, m_l = stat[:, 768:784].rearrange("p (l h) -> p l h", l=LAYERS), stat[:, 784:792]
            t = tt(m_l, lbp[:, 0, :], lbp[:, 1, :], ALU.max)
            t = tt(e_l, lbp, m_l.unsqueeze(1).to_broadcast([P, LAYERS, HG]), ALU.subtract, [t])
            t = act(e_l, e_l, ACT.Exp, [t])
            t = tt(m_l, e_l[:, 0, :], e_l[:, 1, :], ALU.add, [t])
            t = p.op("dve", lambda *i: V.reciprocal(m_l, m_l), [t])
            t = tt(e_l, e_l, m_l.unsqueeze(1).to_broadcast([P, LAYERS, HG]), ALU.mult, [t])
            t = tt(e_l[:, 1, :], e_l[:, 0, :], e_l[:, 1, :], ALU.add, [t])
            t = tt(e_l[:, 1, :], e_l[:, 1, :], e_l[:, 0, :], ALU.subtract, [t])
            t = tt(e_l[:, 0, :], e_l[:, 0, :], e_l[:, 0, :], ALU.subtract, [t])
            lay3 = lay[:, :].rearrange("p (l n) -> p l n", l=LAYERS)
            one_l, fl_l, kf_l = (lay3[:, :, PL_IN + 8 * i:PL_IN + 8 * i + 8] for i in range(3))
            low["one"] = ts(one_l, e_l, -1.0, 1.0, ALU.mult, ALU.add, [t, *t_lay])
            low["floor"] = ts(fl_l, e_l, LB_FLOOR, None, ALU.max, None, [t])
            low["kf"] = tt(kf_l, e_l, fl_l, ALU.subtract, [low["floor"]])

        def fox_sides():
            tq = head_norm(heads(ZFQ, 8), 8, done_z[0])
            tk = head_norm(heads(ZFK, 8), 8, done_z[1])
            yield
            t_fq = q_side(ZFQ, buf_a, prmc("fq_g"), (2, 3), [tq])
            lf = stat[:, 64:80].rearrange("p (a h) -> p a h", a=TT)
            lx = stat[:, 80:96].rearrange("p (a h) -> p a h", a=TT)
            la = stat[:, 96:112].rearrange("p (a h) -> p a h", a=TT)
            t = tt(lx, z3[:, :, ZFF:ZFF + 8], prmc("b_forget").unsqueeze(1).to_broadcast([P, TT, 8]), ALU.add, done_z[5])
            t = ts(la, lx, -1.0, None, ALU.mult, None, [t])
            t = tt(la, la, lx, ALU.min, [t])
            t = act(la, la, ACT.Exp, [t])
            t = act(la, la, ACT.Ln, [t], bias=1.0)
            t1 = ts(lx, lx, 0.0, None, ALU.min, None, [t])
            t_lf = tt(lf, lx, la, ALU.subtract, [t1, t])
            t_lfb = copy(lfb.rearrange("p (a h q) -> p a h q", a=TT, h=8), bc(lf, P), [t_lf], "pool")
            lf2 = stat[:, 64:80]
            p.fence("pe", [t_c1])
            p.fence("dve", [t_c1])
            t = mms([(ps[:, 6, 0:8], ntri[:, 0:P], lf2[:, 0:8], True, True),
                     (ps[:, 6, 8:16], ntri[:, P:2 * P], lf2[:, 0:8], True, False),
                     (ps[:, 6, 8:16], ntri[:, 0:P], lf2[:, 8:16], False, True)], [t_lf, *bank_waits(6)])
            t_cq = ts(stat[:, 112:128], ps[:, 6, 0:16], -1.0, None, ALU.mult, None, [t])
            free[6] = [t_cq]
            fox["cum"] = t_cq
            yield
            t_fk = k_side(fox_k, ZFK, 4, prmc("fk_g"), 4, tk)
            fox["sides"] = [*t_fq, *t_fk, t_lfb]
            lower_bounds()
            t_wr.extend(split(wr_hi[:, :], wr_lo[:, :], prmc("w_route"), []))
            yield

        def nsa_sides():
            ng = nsa["gates"] = stat[:, 128:176].rearrange("p (a c h) -> p a c h", a=TT, c=3)
            nsa["t_gates"] = act(ng, z3[:, :, ZNG:ZNG + 24].rearrange("p a (c h) -> p a c h", c=3), ACT.Sigmoid,
                                 done_z[5])
            tq = head_norm(heads(ZNQ, 8), 8, done_z[3])
            ts_ = head_norm(heads(ZKS, 2), 2, done_z[4])
            tw = head_norm(heads(ZKW, 2), 2, done_z[5])
            yield
            nsa["sides"] = (q_side(ZNQ, buf_b, prmc("nq_g"), (7, 7), [tq]) + k_side(slc_k, ZKS, 1, prmc("nk_g"), 7, ts_)
                            + k_side(win_k, ZKW, 1, prmc("nk_g"), 7, tw))
            yield

        def block1_between():
            yield from fox_sides()
            for _ in pipeline(jobs, lambda i: i < PAIRS or "sides" in nsa):
                if len(t_fox) == PAIRS and "compression" not in nsa:
                    nsa["compression"] = True
                    between.append(compression())
                yield

        z_panel(0)
        z_panel(1)
        z_panel(5)
        between.append(block1_between())
        z_panel(2)
        z_panel(3)
        z_panel(4)
        between.append(nsa_sides())
        g3 = fm(gates[:, :], 16)
        t_gate = {}
        for n in range(4):
            def to_gate(b, src, t, n=n):
                e = act(gates[:, (4 * n + 2 * b) * S:(4 * n + 2 * b + 2) * S], src, ACT.Sigmoid, [t])
                t_gate.setdefault(n // 2, []).append(e)
                return [e]
            proj_feature([], to_gate)


        def turn_512(at_, col, waits, b):
            outs = []
            for i in range(2):
                t1 = transposes([(ps[:, b + i, f * S + a * P:f * S + (a + 1) * P],
                                  z3[:, a, col + (2 * i + f) * P:col + (2 * i + f + 1) * P], P)
                                 for f in range(2) for a in range(TT)], [*waits, *bank_waits(b + i)])
                t2 = split(*operand(at_ + i * 512, 512), ps[:, b + i, :], [t1])
                free[b + i] = t2
                outs += t2
            return outs

        def up(at_, waits, which):
            outs, mixed, products = [], [], []
            for i in range(4):
                b = i % 2
                w, ready, used = take()
                m = []
                for f in range(2):
                    for k in range(4):
                        m += three(ps[:, b, f * S:(f + 1) * S], tuple(x[:, k * P:(k + 1) * P] for x in w[f]),
                                   operand(at_ + k * S, S), k == 0, k == 3)
                t = mms(m, [*ready, *waits, *bank_waits(b)])
                used(t)
                products.append(t)
                g = [gates[:, (8 * n + 2 * i) * S:(8 * n + 2 * i + 2) * S] for n in range(2)]
                e = tt(g[which], ps[:, b, :], g[which], ALU.mult, [t, *t_gate[which]])
                free[b] = [e]
                if which:
                    e = tt(g[0], g[0], g[1], ALU.add, [e, t_up0[i]])
                    mixed.append((g[0], e))
                outs.append(e)
                if which and i < 2:
                    outs += split(*operand(i * 512, 512), g[0], [e])
                fill()
            if which:
                for i in (2, 3):
                    outs += split(*operand(i * 512, 512), mixed[i][0], [mixed[i][1], products[-1]])
            return outs

        while len(t_fox) < PAIRS:
            fill()
        for i in (PN_FOX_UP, PN_NSA_UP, PN_OUT, PN_OUT + 1):
            plan_panel(i)
        t_up0 = up(0, turn_512(0, ZFQ, t_fox, 0), 0)
        fill_all()
        t_mix = up(1024, turn_512(1024, ZNQ, nsa["last"], 0), 1)

        def out_product(waits, first, last):
            for k in range(KT):
                w, ready, used = take()
                m = []
                for h in range(2):
                    for a in range(TT):
                        x = (hi3[:, k, a * P:(a + 1) * P], lo3[:, k, a * P:(a + 1) * P])
                        m += three(ps[:, 4 + 2 * a + h, :], x, w[h], first and k == 0, last and k == KT - 1)
                t = mms(m, [*ready, *waits, *(bank_waits(4, 5, 6, 7) if first and k == 0 else [])])
                used(t)
                fill()
            return t

        t = out_product(t_mix, True, True)
        t_x1 = []
        for b in range(4):
            xs = x_tok[:, b * 512:(b + 1) * 512]
            e = tt(xs, xs, ps[:, 4 + b, :], ALU.add, [t])
            free[4 + b] = [e]
            t_x1.append(e)

        t_h = norm_transpose([t_x1[0:2], t_x1[2:4]], prmc("g_ffn"), [])
        wr = [x[:, :].rearrange("p (k n) -> p k n", k=KT) for x in (wr_hi, wr_lo)]
        m = []
        for a in range(TT):
            for k in range(KT):
                m += three(ps[:, 0, a * 20:(a + 1) * 20], (hi3[:, k, a * P:(a + 1) * P], lo3[:, k, a * P:(a + 1) * P]),
                           (wr[0][:, k, :], wr[1][:, k, :]), k == 0, k == KT - 1)
        t = t_route = mms(m, [*t_h, *t_wr, *bank_waits(0)])

        def rows_split(waits):
            return [x for i in range(4) for x in split(*operand(i * 512, 512), scr[:, i * 512:(i + 1) * 512],
                                                       [*t_h, *waits])]
        at = [384]

        def small(n):
            at[0] += n
            return stat[:, at[0] - n:at[0]]

        lg = small(40).rearrange("p (a n) -> p a n", a=TT)
        t = tt(lg, ps[:, 0, 0:40].rearrange("p (a n) -> p a n", a=TT),
               prmc("b_route").unsqueeze(1).to_broadcast([P, TT, 20]), ALU.add, [t])
        free[0] = [t]

        def softmax4(src, w):
            m, e_, r = small(2), small(8).rearrange("p (a n) -> p a n", a=TT), small(2)
            w = red(m, src, ALU.max, [w])
            w = tt(e_, src, bc(m, 4), ALU.subtract, [w])
            w = act(e_, e_, ACT.Exp, [w])
            w = red(r, e_, ALU.add, [w])
            w = p.op("dve", lambda *i: V.reciprocal(r, r), [w])
            return e_, r, w

        first = c1("first").unsqueeze(1).to_broadcast([P, TT, 4])

        def top1(src, w):
            m, oh, i_ = small(2), small(8).rearrange("p (a n) -> p a n", a=TT), small(2)
            w = red(m, src, ALU.max, [w])
            w = tt(oh, src, bc(m, 4), ALU.is_equal, [w])
            w = tt(oh, oh, first, ALU.mult, [w])
            w = red(i_, oh, ALU.max, [w])
            w = tt(oh, oh, bc(i_, 4), ALU.is_equal, [w])
            return oh, m, w

        ge, gr, tg = softmax4(lg[:, :, 0:4], t)
        goh, gm, tg = top1(ge, tg)
        t_scr = rows_split([t_route])
        goh2 = small(8)
        t_goh = copy(goh2.rearrange("p (a g) -> p a g", a=TT), goh, [tg])
        rank = small(8)
        over = small(4)
        t = mms([(ps[:, 1, 0:4], ntri[:, 0:P], goh2[:, 0:4], True, True),
                 (ps[:, 1, 4:8], ntri[:, P:2 * P], goh2[:, 0:4], True, False),
                 (ps[:, 1, 4:8], ntri[:, 0:P], goh2[:, 4:8], False, True),
                 (ps[:, 1, 8:12], ntri[:, P:2 * P], goh2[:, 0:4], True, False),
                 (ps[:, 1, 8:12], ntri[:, P:2 * P], goh2[:, 4:8], False, True)], [t_goh, *bank_waits(1)])
        t_rank = ts(rank, ps[:, 1, 0:8], -1.0, -1.0, ALU.mult, ALU.add, [t])
        t1 = ts(over, ps[:, 1, 8:12], -1.0, -float(P), ALU.mult, ALU.add, [t])
        free[1] = [t1]
        t1 = ts(over, over, 0.0, None, ALU.max, None, [t1])
        most = small(1)
        t1 = red(most, over, ALU.max, [t1])
        flag = sb("flag", 1, mybir.dt.int32)
        t_flag = copy(flag[:, :], most, [t1])
        comb2 = small(32)

        def expert_weights(tg):
            pg = small(2)
            tg = tt(pg, gm, gr, ALU.mult, [tg])
            sel = small(32).rearrange("p (a g j) -> p a g j", a=TT, g=4)
            e16 = lg[:, :, 4:20].rearrange("p a (g j) -> p a g j", g=4)
            tg = tt(sel, e16, bc(goh, 4), ALU.mult, [tg])
            ein = small(8).rearrange("p (a n) -> p a n", a=TT)
            tg = red(ein, sel.rearrange("p a g j -> p a j g"), ALU.add, [tg])
            pe_, pr_, tg = softmax4(ein, tg)
            pn = small(8).rearrange("p (a n) -> p a n", a=TT)
            tg = tt(pn, pe_, bc(pr_, 4), ALU.mult, [tg])
            oh1, m1, tg = top1(pn, tg)
            pn2 = small(8).rearrange("p (a n) -> p a n", a=TT)
            tg = ts(pn2, oh1, -2.0, None, ALU.mult, None, [tg])
            tg = tt(pn2, pn2, pn, ALU.add, [tg])
            oh2, m2, tg = top1(pn2, tg)
            msum = small(2)
            tg = tt(msum, m1, m2, ALU.add, [tg])
            tg = p.op("dve", lambda *i: V.reciprocal(msum, msum), [tg])
            tg = tt(msum, msum, pg, ALU.mult, [tg])
            tg = tt(oh1, oh1, oh2, ALU.add, [tg])
            tg = tt(oh1, oh1, pn, ALU.mult, [tg])
            tg = tt(oh1, oh1, bc(msum, 4), ALU.mult, [tg])
            t_comb2 = [tt(comb2.rearrange("p (a g j) -> p a g j", a=TT, g=4)[:, a, :, :], bc(goh[:, a, :], 4),
                          oh1[:, a, :].unsqueeze(1).to_broadcast([P, 4, 4]), ALU.mult, [tg]) for a in range(TT)]
            assert at[0] <= 768
            return t_comb2


        sel_r = w_hi[:, (PIECES - 2) * PIECE:PIECES * PIECE]
        sel = sel_r.bitcast(F32)
        selT = buf_b[:, :]
        rows_in = gates[:, :]
        rows_out = zin[:, 0:4 * D]
        sg = buf_c[:, 1024:2048]
        hid = buf_d[:, 0:1024]
        comb_g = stat[:, 704:768]

        t_comb2 = []

        def moe(chunk, waits):
            shifted = stat[:, 1016:1024]
            t = ts(shifted, rank, float(-P * chunk), None, ALU.add, None, [t_rank, *waits])
            t_sel = [ts(sel_r[:, (a * 4 + g) * P:(a * 4 + g + 1) * P], c1("slot"), shifted[:, a * 4 + g:a * 4 + g + 1],
                        goh2[:, a * 4 + g:a * 4 + g + 1], ALU.is_equal, ALU.mult, [t, t_goh, *waits])
                     for a in range(TT) for g in range(4)]
            t_rs = t_scr if chunk == 0 else rows_split(waits)
            if chunk == 0:
                t_comb2.extend(expert_weights(tg))
            t_selT = []
            for i in range(2):
                t = transposes([(ps[:, i, f * S + a * P:f * S + (a + 1) * P],
                                 sel[:, (a * 4 + 2 * i + f) * P:(a * 4 + 2 * i + f + 1) * P], P)
                                for f in range(2) for a in range(TT)], [*t_sel, *bank_waits(i)])
                e = copy(selT[:, i * 512:(i + 1) * 512], ps[:, i, :], [t], "act")
                free[i] = [e]
                t_selT.append(e)
            t_rows = []
            rin = rows_in.rearrange("p (g k n) -> p k g n", g=4, k=KT)
            for k in range(KT):
                b = 3 + k % 4
                t = mms([(ps[:, b, :], x[:, a * D + k * P:a * D + (k + 1) * P], sel_r[:, a * 512:(a + 1) * 512],
                          a == 0 and x is op_hi, a == 1 and x is op_lo) for x in (op_hi, op_lo) for a in range(TT)],
                        [*t_sel, *t_rs, *bank_waits(b)])
                src = ps[:, b, :].rearrange("p (g n) -> p g n", g=4)
                e = act(rin[:, k, :, :], src, ACT.Copy, [t], scale=prmc("g_ffn", k, k + 1))
                free[b] = [e]
                t_rows.append(e)
            t = t_comb = mms([(ps[:, 2, g * 16:(g + 1) * 16], sel[:, (a * 4 + g) * P:(a * 4 + g + 1) * P],
                      comb2[:, a * 16:(a + 1) * 16], a == 0, a == 1) for g in range(4) for a in range(TT)],
                    [*t_sel, *t_comb2, *bank_waits(2)])
            t_cg = copy(comb_g, ps[:, 2, 0:64], [t])
            free[2] = [t_cg]

            pre = {b: list(free[b]) for b in range(8)}
            slots_pre = [list(x) for x in slot_free]
            carry_bank = [Later() for _ in range(8)]
            carry_slot = [Later() for _ in range(RING)]
            carry_w, carry_x = [Later() for _ in range(PIECES)], Later()
            w_pre = [t_comb, *(t for b in range(PIECES) for t in piece_free[b])]
            splitters[0] = beside_experts
            p.begin_loop(GRP)
            pos[0] = n_piece[0] = 0
            for s in range(RING):
                slot_free[s] = [*slots_pre[s], carry_slot[s]]
            for b in range(8):
                free[b] = [*pre[b], carry_bank[b]]
            for b in range(PIECES):
                piece_free[b] = [*w_pre, carry_w[b]]
            for j, m in ((0, 0), (0, 1), (1, 0), (1, 1), (0, 2), (2, 0), (2, 1), (1, 2), (3, 0), (3, 1), (2, 2), (3, 2)):
                plan_panel(lambda *i, n=3 * j + m: i[-1] * 12 + (PN_MOE + n))
            t_xg = []
            for h in range(4):
                xh, xl = operand(h * 256, 256)
                t1 = p.op("act", lambda *i, h=h, xh=xh: A.activation(
                    xh, rows_in[:, bass.ds(i[-1] * 1024 + h * 256, 256)], ACT.Copy), [*t_rows, carry_x])
                t_xg += [t1, p.op("pool", lambda *i, h=h, xh=xh, xl=xl: G.tensor_tensor(
                    xl, rows_in[:, bass.ds(i[-1] * 1024 + h * 256, 256)], xh.bitcast(F32), ALU.subtract), [t1])]
                if h == 0:
                    ahead(2)
            gu = {}
            used_h = [[], []]

            def rows_product(b):
                for i in range(KT // 2):
                    w, ready, used = take()
                    m = []
                    for n in range(2):
                        k = 2 * i + n
                        m += three(ps[:, b, :], operand(k * P, P), w[n], k == 0, k == KT - 1)
                    t = mms(m, [*ready, *t_xg[2 * i:2 * i + 2], *(bank_waits(b) if i == 0 else [])])
                    used(t)
                return t

            def gate_up(j):
                u = j % 2
                su, hu = sg[:, u * 512:(u + 1) * 512], hid[:, u * 512:(u + 1) * 512]
                t_g = rows_product(2 * u)
                e1 = act(su, ps[:, 2 * u, :], ACT.Silu, [t_g])
                free[2 * u] = [e1]
                if j:
                    turn_hidden(j - 1)
                t_u = rows_product(2 * u + 1)
                e2 = p.op("dve", lambda *i: V.scalar_tensor_tensor(
                    hu, su, comb_g[:, bass.ds(i[-1] * 20 + j, 1)], ps[:, 2 * u + 1, :], ALU.mult, ALU.mult),
                    [e1, t_u, t_cg, *used_h[u]])
                free[2 * u + 1] = [e2]
                gu[j] = e2
                if j == EPG - 1:
                    carry_x.token = t_u.prev()

            def turn_hidden(j):
                u = j % 2
                hu = hid[:, u * 512:(u + 1) * 512]
                t = transposes([(ps[:, 6, k * P:(k + 1) * P], hu[:, k * P:(k + 1) * P], P) for k in range(4)],
                               [gu[j], *bank_waits(6)])
                used_h[u] = [t]
                gu[j] = free[6] = split(*operand(1024 + u * 512, 512), ps[:, 6, :], [t])

            def back(j):
                for k in range(4):
                    w, ready, used = take()
                    m = []
                    for h in range(2):
                        m += three(ps[:, 4 + h, :], operand(1024 + j % 2 * 512 + k * P, P), w[h], j == 0 and k == 0,
                                   j == 3 and k == 3)
                    t = mms(m, [*gu[j], *ready, *(bank_waits(4, 5) if j == 0 and k == 0 else [])])
                    used(t)
                    if j == EPG - 2 and k == 1:
                        turn_hidden(EPG - 1)
                return t

            gate_up(0)
            for j in range(EPG):
                if j + 1 < EPG:
                    gate_up(j + 1)
                t = back(j)
            for b in range(PIECES):
                carry_w[b].token = piece_free[b][0].prev()
            e4 = p.op("dve", lambda *i: V.tensor_copy(rows_out[:, bass.ds(i[-1] * D, 512)], ps[:, 4, :]),
                      [t, *waits])
            e5 = p.op("dve", lambda *i: V.tensor_copy(rows_out[:, bass.ds(i[-1] * D + 512, 512)], ps[:, 5, :]),
                      [t, *waits])
            free[4], free[5] = [e4], [e5]
            for s in range(RING):
                carry_slot[s].token = slot_free[s][0].prev()
            for b in range(7):
                carry_bank[b].token = free[b][-1].prev()
            free[7] = pre[7]
            p.end_loop()

            t_sr = copy(sel_r, selT, [t, *t_selT], "act")
            outs = []
            parts_of = [operand(0, 2048), (w_hi[:, 0:2048], w_lo[:, 0:2048])]
            t_ros = [[x for g in range(4) for x in split(*(y[:, g * 512:(g + 1) * 512] for y in parts_of[h]),
                                                         rows_out[:, g * D + h * 512:g * D + (h + 1) * 512],
                                                         [t, e4, e5], ("act", ("dve", "pool")[g % 2]))]
                     for h in range(2)]
            for h in range(2):
                parts_h, t_ro = parts_of[h], t_ros[h]
                for a in range(TT):
                    b = 2 * a + h
                    t_s = mms([(ps[:, b, :], sel_r[:, g * S + a * P:g * S + (a + 1) * P], x[:, g * 512:(g + 1) * 512],
                                g == 0 and x is parts_h[0], g == 3 and x is parts_h[1]) for g in range(4) for x in parts_h],
                              [t_sr, *t_ro, *bank_waits(b)])
                    xs = x_tok[:, b * 512:(b + 1) * 512]
                    e = tt(xs, xs, ps[:, b, :], ALU.add, [t_s])
                    free[b] = [e]
                    outs.append(e)
            for b in range(PIECES):
                piece_free[b] = [t_s]
            return outs

        t_x2 = moe(0, t_x1)
        keep = pos[0]
        p.begin_if(flag[0:1, 0:1], [t_flag])
        t_x2 = moe(1, t_x2)
        p.end_if()
        pos[0] = keep

        t_c2 = p.dma("act", lambda *i: A.dma_start(cst[:, 0:C2_W], c2_in), "cst", t_x2)
        cur = stat[:, 800:800 + PL_W]
        post = keys[:, 1024:2048]
        zb3 = zin[:, :].rearrange("p (a n) -> p a n", a=TT)
        ZI, ZZ, ZQA, ZKA, ZVA = 0, 1024, 2048, 3072, 3200
        za3 = tm(scr[:, :])
        level_mask = c2("level").bitcast(U32).rearrange("p (l t) -> p l t", l=LEVELS)

        slots_pre = [list(x) for x in slot_free]
        carry_slot = [Later() for _ in range(RING)]
        carry_w = Later()
        carry_x = [Later() for _ in range(4)]
        splitters[0] = beside_attention
        p.begin_loop(LAYERS)
        pos[0] = 0
        for s in range(RING):
            slot_free[s] = [*slots_pre[s], carry_slot[s]]
        x_old = [*t_x2, *carry_x]
        for b in range(8):
            free[b] = []
        s_users[0], s_users[1], pt_users[0], pt_users[1] = [], [], [], []
        for n in range(L2_PANELS):
            plan_panel(lambda l, n=n: l * L2_PANELS + (PN_L2 + n), halves=1 if n == 2 else 2)
        for b in range(PIECES):
            piece_free[b] = [*t_x2, carry_w]
        t_cur = p.op("dve", lambda l: V.tensor_copy(cur, lay[:, bass.ds(l * PL_W, PL_W)]),
                     [*x_old, *low.values()])
        t_h = norm_transpose([[*t_x2, *carry_x[2 * a:2 * a + 2]] for a in range(TT)], cur[:, 0:8], [t_cur], 3)
        t_post = p.dma("act", lambda l: A.dma_start(post, post_in[l].partition_broadcast(P)), "post", x_old)
        t_A0 = memz(buf_c[:, :], x_old, "dve")

        def token_panel(dst3, col, n, func=None):
            got = []

            def evac(a, src, t):
                dst = dst3[:, a, col:col + n]
                e = act(dst, src, func, [t]) if func is not None else copy(dst, src, [t], "act" if a else "dve")
                got.append(e)
                return [e]
            proj_token(n, t_h, evac)
            return got

        t_qa = token_panel(zb3, ZQA, 512) + token_panel(zb3, ZQA + 512, 512)
        t_kva = token_panel(zb3, ZKA, 256)

        def rope(col, n, dst, t1, t2, waits):
            half = HD // 2
            v = zb3[:, :, col:col + n * HD].rearrange("p a (h d) -> p a h d", h=n)
            u1, u2 = (x.rearrange("p (a h d) -> p a h d", a=TT, h=n) for x in (t1, t2))
            x1, x2 = v[:, :, :, 0:half], v[:, :, :, half:HD]
            co, si = (c2(x).rearrange("p (a d) -> p a d", a=TT).unsqueeze(2).to_broadcast([P, TT, n, half])
                      for x in ("cos", "sin"))
            a1 = tt(u1, x1, co, ALU.mult, waits)
            a2 = tt(u2, x2, si, ALU.mult, waits)
            b1 = tt(dst[:, :, :, 0:half], u1, u2, ALU.subtract, [a1, a2])
            a1 = tt(u1, x2, co, ALU.mult, [b1])
            a2 = tt(u2, x1, si, ALU.mult, [b1])
            b2 = tt(dst[:, :, :, half:HD], u1, u2, ALU.add, [a1, a2])
            return [b1, b2]

        t_rk = rope(ZKA, 2, pt_buf[:, 1024:1280].rearrange("p (a h d) -> p a h d", a=TT, h=2),
                    s_buf[:, 1024:1152], s_buf[:, 1152:1280], [*t_kva, t_c2])
        t_rq = rope(ZQA, 16, scr[:, :].rearrange("p (a h d) -> p a h d", a=TT, h=16),
                    s_buf[:, 0:1024], pt_buf[:, 0:1024], [*t_qa, t_c2])

        swa = {"out": []}

        def swa_evac(r):
            def evac(o, rec, w):
                e = tt(zb3[:, :, ZQA + r * P:ZQA + (r + 1) * P].rearrange("p a (e d) -> p a e d", e=2), o,
                       bc(rec, HD), ALU.mult, w)
                swa["out"].append(e)
                return [e]
            return evac

        def sliding():
            yield
            t_qT = []
            for a in range(TT):
                for i in range(2):
                    b = 4 + 2 * a + i
                    t = transposes([(ps[:, b, r * P:(r + 1) * P], scr[:, a * D + (4 * i + r) * P:a * D + (4 * i + r + 1) * P], P)
                                    for r in range(4)], [*t_rq, *bank_waits(b)])
                    e = ts(zb3[:, a, ZQA + i * 512:ZQA + (i + 1) * 512], ps[:, b, :], HD ** -0.5, None, ALU.mult, None, [t])
                    free[b] = [e]
                    t_qT.append(e)
            t = transposes([(ps[:, 2, a * P:(a + 1) * P], pt_buf[:, 1024 + a * P:1024 + (a + 1) * P], P)
                            for a in range(TT)], [*t_rk, *bank_waits(2)])
            t_kT = [copy(keys[e * HD:(e + 1) * HD, e * S:(e + 1) * S], ps[e * HD:(e + 1) * HD, 2, 0:S], [t])
                    for e in range(2)]
            free[2] = [t_kT[-1]]
            swa["sides"] = [*t_qT, *t_kT]
            yield
            yield from pipeline([
                (lambda r=r: scores(lambda a: zb3[:, a, ZQA + r * P:ZQA + (r + 1) * P], keys[:, 0:512],
                                    swa["sides"], c2("band"), sink=cur[:, 136 + 2 * r:138 + 2 * r]),
                 lambda job, r=r: values(job, lambda kt, e: zb3[:, kt, ZVA + e * HD:ZVA + (e + 1) * HD],
                                         t_kva, swa_evac(r)))
                for r in range(SWA_PAIRS)])

        Q, K, FG = gates[:, 0:2048], gates[:, 2048:4096], buf_d[:, :]
        one_m, floor_, kf = (cur[:, PL_IN + 8 * i:PL_IN + 8 * i + 8] for i in range(3))
        t_q, t_f, t_k = {}, {}, {}
        between.append(sliding())
        for j in range(2):
            def q_evac(b, src, t, j=j):
                c = (4 * j + 2 * b) * S
                e = act(Q[:, c:c + 512], src, ACT.Silu, [t])
                t_q.setdefault(j, []).append(e)
                return [e]

            def f_evac(b, src, t, j=j):
                h = 4 * j + 2 * b
                c = h * S
                e1 = act(FG[:, c:c + 512], src, ACT.Sigmoid, [t])
                e2 = act(K[:, c:c + 512], src, ACT.Sigmoid, [t], scale=-1.0)
                for i in range(2):
                    r = slice(c + i * S, c + (i + 1) * S)
                    t_f.setdefault(j, []).append(ts(FG[:, r], FG[:, r], one_m[:, h + i:h + i + 1],
                                                    floor_[:, h + i:h + i + 1], ALU.mult, ALU.add, [e1]))
                    t_k.setdefault(j, []).append(ts(K[:, r], K[:, r], one_m[:, h + i:h + i + 1],
                                                    kf[:, h + i:h + i + 1], ALU.mult, ALU.add, [e2]))
                return [e2]
            proj_feature(t_h, q_evac)
            proj_feature(t_h, f_evac)

        rec_ = [{"q": t_q[j], "k": t_k[j], "tot": FG[:, j * 1024:(j + 1) * 1024], "t_tot": t_f[j], "am": [t_A0]}
                for j in range(2)]

        def q_of(j):
            return Q[:, j * 1024:(j + 1) * 1024]

        def k_of(j):
            return K[:, j * 1024:(j + 1) * 1024]

        def am_of(j):
            return buf_c[:, j * 1024:(j + 1) * 1024].rearrange("p (n t) -> p n t", n=8)

        def level(j, lv):
            r, q, k, f = rec_[j], q_of(j), k_of(j), FG[:, j * 1024:(j + 1) * 1024]
            b = 2 + 2 * j
            t = mms([(ps[:, b + n // 4, (n % 4) * P:(n % 4 + 1) * P], k[:, n * P:(n + 1) * P],
                      q[:, n * P:(n + 1) * P], True, True) for n in range(8)],
                    [*r["q"], *r["k"], *bank_waits(b, b + 1)])
            if lv == 0:
                r["q"] = [tt(q, q, f, ALU.mult, [t, *t_f[j], *r["am"]])]
            else:
                m = 1 << (lv - 1)
                qv, kv = (x.rearrange("p (b two m) -> p b two m", two=2, m=m) for x in (q, k))
                tv = r["tot"].rearrange("p (b two) -> p b two", two=2)
                r["q"] = [tt(qv[:, :, 1, :], qv[:, :, 1, :], bc(tv[:, :, 0], m), ALU.mult,
                             [t, *r["t_tot"], *r["am"]])]
                r["k"] = [tt(kv[:, :, 0, :], kv[:, :, 0, :], bc(tv[:, :, 1], m), ALU.mult, [t, *r["t_tot"]])]
                n = 1024 >> lv
                tot = buf_b[:, j * 512:j * 512 + n] if lv % 2 else f[:, 0:n]
                r["t_tot"] = [tt(tot, tv[:, :, 0], tv[:, :, 1], ALU.mult, r["t_tot"])]
                r["tot"] = tot
            mask = level_mask[:, lv, :].unsqueeze(1).to_broadcast([P, 8, P])
            data = bank(b, 2).rearrange("p (n t) -> p n t", n=8)
            am = am_of(j)
            e = p.op("dve", lambda *i: V.copy_predicated(am, mask, data), [t, *r["am"]])
            r["am"] = [e]
            free[b] = free[b + 1] = [e]

        def cross(j):
            b = 2 + j
            t = mms([(ps[:, b, h * P:(h + 1) * P], k_of(j)[:, h * S:h * S + P], q_of(j)[:, h * S + P:(h + 1) * S],
                      True, True) for h in range(4)], [*rec_[j]["q"], *rec_[j]["k"], *bank_waits(b)])
            t = act(buf_a[:, j * 512:(j + 1) * 512], ps[:, b, :], ACT.Copy, [t])
            free[b] = [t]
            rec_[j]["cross"] = t

        def hgrn_values(j):
            m0, m1 = [], []
            b = 2
            am = am_of(j)
            for h in range(4):
                hc = slice(ZI + (4 * j + h) * P, ZI + (4 * j + h + 1) * P)
                c = slice(h * P, (h + 1) * P)
                m0 += [(ps[:, b, c], am[:, 2 * h, :], zb3[:, 0, hc], True, True)]
                m1 += [(ps[:, b + 1, c], am[:, 2 * h + 1, :], zb3[:, 1, hc], True, False),
                       (ps[:, b + 1, c], buf_a[:, (j * 4 + h) * P:(j * 4 + h + 1) * P], zb3[:, 0, hc], False, True)]
            t = mms(m0 + m1, [rec_[j]["cross"], *rec_[j]["am"], *t_i, *bank_waits(b, b + 1)])
            for a in range(TT):
                e = act(zb3[:, a, ZI + j * 512:ZI + (j + 1) * 512], ps[:, b + a, :], ACT.Copy, [t])
                free[b + a] = [e]
                hg["out"].append(e)

        hg = {"out": []}

        def turn_half(col, waits):
            outs = []
            for b in range(4):
                t = transposes([(ps[:, b, f * S + a * P:f * S + (a + 1) * P],
                                 zb3[:, a, col + (2 * b + f) * P:col + (2 * b + f + 1) * P], P)
                                for f in range(2) for a in range(TT)], [*waits, *bank_waits(b)])
                e = split(*operand(b * 512, 512), ps[:, b, :], [t])
                free[b] = e
                outs += e
            return outs

        def hgrn():
            for lv in range(LEVELS):
                for j in range(2):
                    level(j, lv)
                    yield
            for j in range(2):
                cross(j)
            hg["levels"] = True
            yield
            for j in range(2):
                hgrn_values(j)
                yield
            oh = zb3[:, :, ZI:ZI + 1024].rearrange("p a (h d) -> p a h d", h=HG)
            zh = zb3[:, :, ZZ:ZZ + 1024].rearrange("p a (h d) -> p a h d", h=HG)
            g_head = cur[:, 8:136].unsqueeze(1).unsqueeze(1).to_broadcast([P, TT, HG, P])
            t_gz = tt(zh, zh, g_head, ALU.mult, [*t_zh, t_cur], "pool")
            sq = buf_d[:, :].rearrange("p (a h d) -> p a h d", a=TT, h=HG)
            ss = stat[:, 992:1008].rearrange("p (a h) -> p a h", a=TT)
            t = tt(sq, oh, oh, ALU.mult, hg["out"])
            t = red(ss, sq, ALU.add, [t])
            t = rstd(ss, ss, P, [t])
            t = tt(oh, oh, bc(ss, P), ALU.mult, [t])
            t = tt(oh, oh, zh, ALU.mult, [t, t_gz])
            hg["normed"] = t
            yield

        t_za = token_panel(za3, 0, 512, ACT.Silu) + token_panel(za3, 512, 512, ACT.Silu)
        while len(swa["out"]) < SWA_PAIRS:
            fill()
        oa = zb3[:, :, ZQA:ZQA + 1024]
        t_oa = tt(oa, oa, za3, ALU.mult, [*swa["out"], *t_za], "pool")
        between.append(hgrn())
        t_i = token_panel(zb3, ZI, 512) + token_panel(zb3, ZI + 512, 512)
        t_zh = token_panel(zb3, ZZ, 512, ACT.Silu) + token_panel(zb3, ZZ + 512, 512, ACT.Silu)

        while "levels" not in hg:
            fill()
        out_product(turn_half(ZQA, [t_oa]), True, False)
        fill_all()
        t = carry_w_now = out_product(turn_half(ZI, [hg["normed"]]), False, True)
        ssb = stat[:, 1008:1012]
        sst, rst = stat[:, 1012:1014], stat[:, 1014:1016]
        t1 = [act(scr[:, b * 512:(b + 1) * 512], ps[:, 4 + b, :], ACT.Square, [t], accum_out=ssb[:, b:b + 1])
              for b in range(4)]
        t2 = red(sst, ssb.rearrange("p (a h) -> p a h", a=TT), ALU.add, t1)
        t2 = rstd(rst, sst, D, [t2])
        t_x3 = []
        for b in range(4):
            a, h = b // 2, b % 2
            tmp = scr[:, b * 512:(b + 1) * 512]
            xs = x_tok[:, b * 512:(b + 1) * 512]
            e = stt(tmp, ps[:, 4 + b, :], rst[:, a:a + 1], post[:, h * 512:(h + 1) * 512], ALU.mult, ALU.mult,
                    [t2, t1[b], t_post])
            t_x3.append(tt(xs, xs, tmp, ALU.add, [e]))
        for s in range(RING):
            carry_slot[s].token = slot_free[s][0].prev()
        carry_w.token = carry_w_now.prev()
        for b in range(4):
            carry_x[b].token = t_x3[b].prev()
        p.end_loop()

        t = p.dma("sp", lambda *i: nc.sync.dma_start(out.rearrange("o (a p) d -> p (o a) d", p=P), x3), "out", t_x3)
        p.fence("sp", [t])

        block = ctx.enter_context(nc.Block())

        @block.sync
        def _(_e):
            p.emit("sp")

        @block.tensor
        def _(_e):
            p.emit("pe")

        @block.vector
        def _(_e):
            p.emit("dve")

        @block.scalar
        def _(_e):
            p.emit("act")

        @block.gpsimd
        def _(_e):
            p.emit("pool")


def slope(g, r):
    return 2.0 ** (-(g * PAIRS + r + 1))


def shape_constants():
    f = np.float32
    s = np.arange(P)[:, None]
    ident = np.eye(P, dtype=f)
    ntri = -(s <= np.arange(S)[None, :]).astype(f)

    def by_query(fn):
        k2, k1 = np.arange(S)[None, :], np.arange(P)[None, :]
        return np.concatenate([fn(s + P, k2, 0), fn(s + P, k2, 1), fn(s, k1, 0), fn(s, k1, 1)], 1)

    causal = by_query(lambda q, k, e: np.where(k <= q, 0.0, NEG))
    band = by_query(lambda q, k, e: np.where((k <= q) & (q - k < 128), 0.0, NEG))
    dist_ = by_query(lambda q, k, e: np.where(k <= q, k - q, NEG))
    n = np.arange(CMP_PAD)[None, :]
    cmp_, any_ = [], []
    for a in range(TT):
        dist = (s + a * P) - (n * 16 + 31)
        ok = (dist >= 0) & (n < N_CMP)
        for r in range(PAIRS):
            for g in range(2):
                cmp_.append(np.where(ok, -slope(g, r) * dist, NEG))
        any_.append(ok.any(1, keepdims=True).astype(f))
    first = np.broadcast_to(np.array([4, 3, 2, 1], f), (P, 4))
    c1 = np.concatenate([ntri, causal, dist_, *cmp_, *any_, first, np.broadcast_to(np.arange(P), (P, P))], 1).astype(f)
    half = HD // 2
    freq = np.float32(10000.0) ** (-np.arange(half, dtype=f) / np.float32(half))
    ang = [((s + a * P).astype(f) * freq[None, :]).astype(f) for a in range(TT)]
    t = np.arange(P)[None, :]
    levels = [(s == t)]
    for lv in range(1, LEVELS):
        m = 1 << (lv - 1)
        levels.append((s // (2 * m) == t // (2 * m)) & (s % (2 * m) < m) & (t % (2 * m) >= m))
    c2 = np.concatenate([band, *[np.cos(x) for x in ang], *[np.sin(x) for x in ang],
                         *[x.astype(f) for x in levels]], 1).astype(f)
    assert c1.shape[1] == C1_W and c2.shape[1] == C2_W
    return ident, c1, c2


def lay_out(x):
    g = {k: np.asarray(v) for k, v in x.items()}
    w = g["w_in"][0]
    cuts = np.cumsum([512, 512, 512, 8, 512, 128, 128, 128, 128, 128, 128, 24, 1024])
    fq, fk, fv, ff, nq, kc, vc, ks, vs, kw, vw, ng, ga, gb = np.split(w, cuts, axis=1)
    nq = nq.reshape(D, 2, 4, HD).transpose(0, 2, 1, 3).reshape(D, 512)
    ng = ng.reshape(D, 2, 4, 3).transpose(0, 3, 2, 1).reshape(D, 24)
    mixed = np.concatenate([kw, vw, ff, ng, np.zeros((D, 512 - Z5), w.dtype)], 1)

    def cols(m):
        n = m.shape[1] // 512
        return list(m.reshape(KT, P, n, 512).transpose(2, 1, 0, 3).reshape(n, P, PANEL))

    def rows(m):
        n = m.shape[0] // 512
        return list(m.reshape(n, 4, P, D).transpose(0, 2, 1, 3).reshape(n, P, PANEL))

    def tiles(m):
        n = m.shape[1] // 512
        return list(m.reshape(KT, P, n, 4, P).transpose(2, 1, 3, 0, 4).reshape(n, P, PANEL))

    def up_tiles(m):
        return [m.reshape(4, P, 8, P).transpose(1, 2, 0, 3).reshape(P, PANEL)]

    pan = cols(fq) + cols(fk) + cols(mixed) + cols(fv) + cols(nq) + cols(np.concatenate([kc, vc, ks, vs], 1))
    pan += tiles(ga) + tiles(gb)
    for nme in ("cmp_k_w1", "cmp_v_w1"):
        pan.append(g[nme][0].reshape(16, P, 256).transpose(1, 0, 2).reshape(P, PANEL))
    pan += up_tiles(g["w_fox_up"][0])
    pan += up_tiles(g["w_nsa_up"][0].reshape(2, 4, HD, D).transpose(1, 0, 2, 3).reshape(512, D))
    pan += rows(g["w_out"][0])
    for e in range(N_EXP):
        pan += cols(g["w_gate"][0, e]) + cols(g["w_up"][0, e]) + rows(g["w_down"][0, e])
    for l in range(LAYERS):
        w2 = g["w_in_2"][l]
        qh, fh, ih, zh, qa, ka, va, za = np.split(w2, np.cumsum([1024, 1024, 1024, 1024, 1024, 128, 128]), axis=1)
        pair = lambda m: m.reshape(-1, 2, 8, HD).transpose(0, 2, 1, 3).reshape(-1, 1024)
        qa, za = pair(qa), pair(za)
        qh, fh = tiles(qh), tiles(fh)
        kv = np.concatenate([ka, va], 1).reshape(KT, P, 256).transpose(1, 0, 2).reshape(P, HALF)
        pan += cols(qa) + [np.concatenate([kv, np.zeros((P, HALF), w2.dtype)], 1)]
        pan += [qh[0], fh[0], qh[1], fh[1]] + cols(za) + cols(ih) + cols(zh)
        wo = g["w_out_2"][l]
        pan += rows(wo[1024:].reshape(2, 8, HD, D).transpose(1, 0, 2, 3).reshape(1024, D))
        pan += rows(wo[:1024])
    panels = np.stack(pan)
    assert panels.shape[0] == N_PANELS
    panels = np.ascontiguousarray(panels.reshape(N_PANELS, P, 2, HALF).transpose(0, 2, 1, 3)).reshape(-1, P, HALF)

    def feat(v):
        return v.reshape(-1, P).T

    def every(v):
        return np.broadcast_to(v.reshape(1, -1), (P, v.size))

    def twice(v):
        return np.concatenate([v, v]).reshape(P, 1)

    def pos_(v):
        return v.reshape(16, P).T

    def w2_(v):
        return v.reshape(2, P, HD).transpose(1, 0, 2).reshape(P, 128)

    route = np.concatenate([g["w_group"][0], g["w_router"][0]], 1).reshape(KT, P, 20).transpose(1, 0, 2).reshape(P, 160)
    prm = np.concatenate([
        feat(g["norm_mix_g"][0]), feat(g["norm_ffn_g"][0]), twice(g["fox_q_g"][0]), twice(g["fox_k_g"][0]),
        twice(g["nsa_q_g"][0]), twice(g["nsa_k_g"][0]), pos_(g["cmp_k_pos"][0]), pos_(g["cmp_v_pos"][0]),
        every(g["b_forget"][0]), every(np.concatenate([g["b_group"][0], g["b_router"][0]])), route,
        w2_(g["cmp_k_w2"][0]), w2_(g["cmp_v_w2"][0]),
        g["lb_param_2"].reshape(LAYERS, HG, P).transpose(2, 0, 1).reshape(P, 16)], 1)
    lay = np.stack([np.concatenate([
        feat(g["g_pre_2"][l]), every(g["g_head_2"][l]),
        every(g["sinks_2"][l].reshape(2, 8).T)], 1) for l in range(LAYERS)])
    return {"panels": panels, "x": g["x"], "prm": prm, "lay": lay, "post": g["g_post_2"]}


def kernel(**inputs):
    import concourse.bacc as bacc
    from concourse.bass_utils import run_bass_kernel_spmd

    arrays = lay_out(inputs)
    arrays["ident"], arrays["c1"], arrays["c2"] = shape_constants()
    arrays = {"in_" + k: np.ascontiguousarray(v) for k, v in arrays.items()}
    nc = bacc.Bacc("TRN2", target_bir_lowering=False, num_devices=1)
    aps = {k: nc.dram_tensor(k, v.shape, mybir.dt.from_np(v.dtype), kind="ExternalInput").ap()
           for k, v in arrays.items()}
    out = nc.dram_tensor("out", (1, S, D), F32, kind="ExternalOutput").ap()
    build(nc, aps["in_panels"], aps["in_x"], aps["in_prm"], aps["in_lay"], aps["in_post"], aps["in_ident"],
          aps["in_c1"], aps["in_c2"], out)
    r = run_bass_kernel_spmd(nc, [arrays], core_ids=[0])
    return r.results[0]["out"]
```
